# Optimizing a Trainium2 kernel written in Bass

```python
import math
import jax
import jax.numpy as jnp
from jax import lax
import numpy as np
import jax, jax.numpy as jnp

D_MODEL = 1024
BATCH = 1
SEQ = 256
DEPTH = 1

MIX_WIDTH = D_MODEL
HYENA_WIDTH = MIX_WIDTH // 2
HYENA_ORDER = 2
HYENA_GROUPS = 8
SHORT_CONV_WIDTH = 3
FILTER_EMB_DIM = 33
FILTER_BANDS = (FILTER_EMB_DIM - 1) // 2
FILTER_HIDDEN = 64
DECAY_TARGET = 1e-2
FAST_DECAY_PCT = 0.3
SLOW_DECAY_PCT = 1.5
ATTN_WIDTH = MIX_WIDTH - HYENA_WIDTH
ATTN_HEADS = 4
ATTN_HEAD_DIM = ATTN_WIDTH // (2 * ATTN_HEADS)
Q_BLOCK = 128
HYENA_COLS = (HYENA_ORDER + 1) * HYENA_WIDTH
IN_COLS = HYENA_COLS + 3 * ATTN_WIDTH
N_EXPERTS = 16
EC_CAPACITY_FACTOR = 2
EXPERT_FF = 2816
NORM_EPS = 1e-6


def _rmsnorm(x, g):
    xf = x.astype(jnp.float32)
    y = xf * lax.rsqrt(jnp.mean(xf * xf, axis=-1, keepdims=True) + NORM_EPS)
    return (y * g.astype(jnp.float32)).astype(x.dtype)

def _alibi_slopes(n):
    return jnp.asarray([2.0 ** (-8.0 * (i + 1) / n) for i in range(n)], dtype=jnp.float32)

def _hyena_filters(L, w1, b1, w2, b2, w3, freq):
    f32 = jnp.float32
    t = jnp.linspace(0.0, 1.0, L, dtype=f32)[:, None]
    w = 2.0 * math.pi * jnp.arange(L, dtype=f32)[:, None] / L
    bands = jnp.linspace(1e-4, FILTER_BANDS - 1, FILTER_BANDS, dtype=f32)[None, :]
    z = jnp.concatenate([t, jnp.cos(bands * w), -jnp.sin(bands * w)], axis=-1)
    fr = freq.astype(f32)
    hid = jnp.sin(fr * (z @ w1.astype(f32) + b1.astype(f32)))
    hid = jnp.sin(fr * (hid @ w2.astype(f32) + b2.astype(f32)))
    h = (hid @ w3.astype(f32)).reshape(L, 2, HYENA_ORDER, HYENA_WIDTH)
    min_decay = math.log(DECAY_TARGET) / SLOW_DECAY_PCT
    max_decay = math.log(DECAY_TARGET) / FAST_DECAY_PCT
    deltas = jnp.abs(jnp.linspace(min_decay, max_decay, HYENA_WIDTH, dtype=f32))
    h = h * jnp.exp(-t[:, :, None, None] * deltas)
    fwd, bwd = h[:, 0], h[:, 1]
    k = jnp.concatenate([fwd, jnp.zeros((1, HYENA_ORDER, HYENA_WIDTH), f32), bwd[:0:-1]], axis=0)
    return k / jnp.sum(jnp.abs(k), axis=0, keepdims=True)

def _fft_conv(u, k_freq, L):
    uf = jnp.fft.rfft(u, n=2 * L, axis=1)
    return jnp.fft.irfft(uf * k_freq[None], n=2 * L, axis=1)[:, :L]

def _hyena_mixer(proj, conv_w, conv_b, w1, b1, w2, b2, w3, freq, skip, norm_g):
    B, L, _ = proj.shape
    pad = SHORT_CONV_WIDTH // 2
    up = jnp.pad(proj, ((0, 0), (pad, pad), (0, 0)))
    u = conv_b
    for j in range(SHORT_CONV_WIDTH):
        u = u + up[:, j:j + L] * conv_w[j]
    x1, x2, v = jnp.split(u, HYENA_ORDER + 1, axis=-1)
    k_freq = jnp.fft.rfft(_hyena_filters(L, w1, b1, w2, b2, w3, freq), axis=0)
    skip = skip.astype(jnp.float32)
    z = v.astype(jnp.float32)
    for n, gate in enumerate((x1, x2)):
        z = gate.astype(jnp.float32) * (_fft_conv(z, k_freq[:, n], L) + skip[n] * z)
    z = z.reshape(B, L, HYENA_GROUPS, HYENA_WIDTH // HYENA_GROUPS)
    z = _rmsnorm(z, norm_g.reshape(HYENA_GROUPS, HYENA_WIDTH // HYENA_GROUPS))
    return z.reshape(B, L, HYENA_WIDTH).astype(proj.dtype)

def _diff_attention(q, k, v, lam, lam_init, subln_g):
    B, L, _ = q.shape
    H, Dh = ATTN_HEADS, ATTN_HEAD_DIM
    q = q.reshape(B, L, H, 2, Dh)
    k = k.reshape(B, L, H, 2, Dh)
    v = v.reshape(B, L, H, 2 * Dh)
    scale = Dh ** -0.5
    slopes = _alibi_slopes(H)
    nb = L // Q_BLOCK
    qb = q.reshape(B, nb, Q_BLOCK, H, 2, Dh).transpose(1, 0, 2, 3, 4, 5)
    starts = jnp.arange(nb, dtype=jnp.int32) * Q_BLOCK
    kpos = jnp.arange(L, dtype=jnp.float32)

    def block(args):
        qblk, s0 = args
        qpos = (s0 + jnp.arange(Q_BLOCK, dtype=jnp.int32)).astype(jnp.float32)
        dist = jnp.abs(qpos[:, None] - kpos[None, :])
        s = jnp.einsum('bqhcd,bkhcd->bhcqk', qblk, k).astype(jnp.float32) * scale
        s = s - slopes[None, :, None, None, None] * dist
        p = jax.nn.softmax(s, axis=-1)
        a = p[:, :, 0] - lam * p[:, :, 1]
        return jnp.einsum('bhqk,bkhe->bqhe', a.astype(v.dtype), v)

    o = lax.map(block, (qb, starts))
    o = o.transpose(1, 0, 2, 3, 4).reshape(B, L, H, 2 * Dh)
    o = _rmsnorm(o, subln_g) * (1.0 - lam_init)
    return o.reshape(B, L, H * 2 * Dh).astype(q.dtype)

def _expert_choice_ffn(h, w_router, w_gate, w_up, w_down):
    B, L, _ = h.shape
    cap = EC_CAPACITY_FACTOR * L // N_EXPERTS
    logits = jnp.einsum('bsd,de->bse', h, w_router).astype(jnp.float32)
    aff = jax.nn.softmax(logits, axis=-1)
    g, idx = lax.top_k(aff.transpose(2, 0, 1), cap)
    bi = jnp.arange(B, dtype=jnp.int32)[None, :, None]
    xin = h[bi, idx]

    def expert(args):
        xe, wg, wu, wd = args
        a = jnp.einsum('bcd,df->bcf', xe, wg)
        u = jnp.einsum('bcd,df->bcf', xe, wu)
        return jnp.einsum('bcf,fd->bcd', jax.nn.silu(a) * u, wd)

    out = lax.map(expert, (xin, w_gate, w_up, w_down))
    out = out * g[..., None].astype(out.dtype)
    return jnp.zeros_like(h).at[bi, idx].add(out)

def first_inputs(seed: int = 0) -> dict:
    key = jax.random.key(seed)
    ks = jax.random.split(key, 25)
    f32 = jnp.float32

    def nrm(k, shape, scale):
        return jax.random.normal(k, shape, f32) * scale

    D, E, F = D_MODEL, N_EXPERTS, EXPERT_FF
    return {
        'x': nrm(ks[0], (BATCH, SEQ, D), 1.0),
        'attn_norm_g': 1.0 + nrm(ks[1], (DEPTH, D), 0.02),
        'w_in': nrm(ks[2], (DEPTH, D, IN_COLS), D ** -0.5),
        'conv_w': nrm(ks[3], (DEPTH, SHORT_CONV_WIDTH, HYENA_COLS), SHORT_CONV_WIDTH ** -0.5),
        'conv_b': nrm(ks[4], (DEPTH, HYENA_COLS), 0.02),
        'filt_w1': nrm(ks[5], (DEPTH, FILTER_EMB_DIM, FILTER_HIDDEN), FILTER_EMB_DIM ** -0.5),
        'filt_b1': nrm(ks[6], (DEPTH, FILTER_HIDDEN), 0.1),
        'filt_w2': nrm(ks[7], (DEPTH, FILTER_HIDDEN, FILTER_HIDDEN), FILTER_HIDDEN ** -0.5),
        'filt_b2': nrm(ks[8], (DEPTH, FILTER_HIDDEN), 0.1),
        'filt_w3': nrm(ks[9], (DEPTH, FILTER_HIDDEN, 2 * HYENA_ORDER * HYENA_WIDTH), FILTER_HIDDEN ** -0.5),
        'filt_freq': 1.0 + nrm(ks[10], (DEPTH, FILTER_HIDDEN), 0.1),
        'hyena_skip': nrm(ks[11], (DEPTH, HYENA_ORDER, HYENA_WIDTH), 1.0),
        'hyena_norm_g': 1.0 + nrm(ks[12], (DEPTH, HYENA_WIDTH), 0.02),
        'lambda_q1': nrm(ks[13], (DEPTH, ATTN_HEAD_DIM), 0.1),
        'lambda_k1': nrm(ks[14], (DEPTH, ATTN_HEAD_DIM), 0.1),
        'lambda_q2': nrm(ks[15], (DEPTH, ATTN_HEAD_DIM), 0.1),
        'lambda_k2': nrm(ks[16], (DEPTH, ATTN_HEAD_DIM), 0.1),
        'subln_g': 1.0 + nrm(ks[17], (DEPTH, 2 * ATTN_HEAD_DIM), 0.02),
        'w_out': nrm(ks[18], (DEPTH, MIX_WIDTH, D), MIX_WIDTH ** -0.5),
        'ffn_norm_g': 1.0 + nrm(ks[19], (DEPTH, D), 0.02),
        'w_router': nrm(ks[20], (DEPTH, D, E), D ** -0.5),
        'w_gate': nrm(ks[21], (DEPTH, E, D, F), D ** -0.5),
        'w_up': nrm(ks[22], (DEPTH, E, D, F), D ** -0.5),
        'w_down': nrm(ks[23], (DEPTH, E, F, D), F ** -0.5),
        'final_norm_g': 1.0 + nrm(ks[24], (D,), 0.02),
    }

def first_block(x, attn_norm_g, w_in, conv_w, conv_b, filt_w1, filt_b1, filt_w2, filt_b2,
              filt_w3, filt_freq, hyena_skip, hyena_norm_g, lambda_q1, lambda_k1,
              lambda_q2, lambda_k2, subln_g, w_out, ffn_norm_g, w_router, w_gate, w_up,
              w_down, final_norm_g):
    f32 = jnp.float32
    for l in range(DEPTH):
        hn = _rmsnorm(x, attn_norm_g[l])
        proj = jnp.einsum('bsd,dn->bsn', hn, w_in[l])
        hy = _hyena_mixer(proj[..., :HYENA_COLS], conv_w[l], conv_b[l], filt_w1[l], filt_b1[l],
                          filt_w2[l], filt_b2[l], filt_w3[l], filt_freq[l], hyena_skip[l],
                          hyena_norm_g[l])
        q, k, v = jnp.split(proj[..., HYENA_COLS:], 3, axis=-1)
        lam_init = 0.8 - 0.6 * math.exp(-0.3 * l)
        lam = (jnp.exp(jnp.sum(lambda_q1[l].astype(f32) * lambda_k1[l].astype(f32)))
               - jnp.exp(jnp.sum(lambda_q2[l].astype(f32) * lambda_k2[l].astype(f32)))
               + lam_init)
        at = _diff_attention(q, k, v, lam, lam_init, subln_g[l])
        mix = jnp.concatenate([hy, at], axis=-1)
        x = x + jnp.einsum('bsm,md->bsd', mix, w_out[l])
        x = x + _expert_choice_ffn(_rmsnorm(x, ffn_norm_g[l]), w_router[l], w_gate[l],
                                   w_up[l], w_down[l])
    return _rmsnorm(x, final_norm_g)


DEPTH_2 = 2

D_FF = 2816
PLE_DIM = 256
CONV_WIDTH = 3
CONV_CH = 512
S5_CH = 512
S5_GROUP = 16
S5_GROUPS = S5_CH // S5_GROUP
S5_STATE = 64
AB_IN = 3 * CONV_CH + S5_CH
N_HEADS = 8
HEAD_DIM = 128
N_KV_HEADS = 2
IDX_HEADS = 8
IDX_DIM = 64
TOPK_MAX = 256
C_SIZES = (N_HEADS * HEAD_DIM, N_KV_HEADS * HEAD_DIM, N_KV_HEADS * HEAD_DIM,
           IDX_HEADS * IDX_DIM, IDX_DIM, IDX_HEADS)
C_SPLITS = tuple(int(v) for v in np.cumsum(C_SIZES)[:-1])
C_IN = int(sum(C_SIZES))
ROPE_THETA = 500000.0
ROT_FRAC = 4
LN_EPS = 1e-5
DN_ALPHA = (2 * DEPTH_2) ** 0.25
DN_BETA = (8 * DEPTH_2) ** -0.25
N_EVEN = (DEPTH_2 + 1) // 2
N_ODD = DEPTH_2 // 2


def layer_norm(x, g, b):
    xf = x.astype(jnp.float32)
    mu = jnp.mean(xf, axis=-1, keepdims=True)
    var = jnp.mean(jnp.square(xf - mu), axis=-1, keepdims=True)
    return ((xf - mu) * lax.rsqrt(var + LN_EPS) * g.astype(jnp.float32) + b.astype(jnp.float32)).astype(x.dtype)

def swiglu(x, w1, w3, w2):
    return (jax.nn.silu(x @ w1) * (x @ w3)) @ w2

def rope_tables(positions, rot_dim):
    inv = ROPE_THETA ** (-jnp.arange(0, rot_dim, 2, dtype=jnp.float32) / rot_dim)
    ang = positions.astype(jnp.float32)[..., None] * inv
    return jnp.cos(ang), jnp.sin(ang)

def partial_rope(t, cos, sin):
    half = cos.shape[-1]
    r = 2 * half
    tr = t[..., :r].astype(jnp.float32)
    t1, t2 = tr[..., :half], tr[..., half:]
    rot = jnp.concatenate([t1 * cos - t2 * sin, t2 * cos + t1 * sin], axis=-1).astype(t.dtype)
    return jnp.concatenate([rot, t[..., r:]], axis=-1)

def short_conv_mixer(h, gb, gc, conv_w):
    u = gc * h
    L = u.shape[1]
    up = jnp.pad(u, ((0, 0), (CONV_WIDTH - 1, 0), (0, 0)))
    v = sum(conv_w[j] * up[:, j:j + L] for j in range(CONV_WIDTH))
    return gb * v

def s5_mixer(u, lam_re, lam_im, log_dt, b_re, b_im, c_re, c_im, d_skip, w_glu, b_glu):
    f32 = jnp.float32
    Bt, L, _ = u.shape
    uf = u.astype(f32)
    ug = uf.reshape(Bt, L, S5_GROUPS, S5_GROUP)
    lr = jnp.minimum(lam_re.astype(f32), -1e-4)
    li = lam_im.astype(f32)
    dt = jnp.exp(log_dt.astype(f32))[:, None]
    mag = jnp.exp(lr * dt)
    ab_re = mag * jnp.cos(li * dt)
    ab_im = mag * jnp.sin(li * dt)
    nr, ni = ab_re - 1.0, ab_im
    den = lr * lr + li * li
    f_re = (nr * lr + ni * li) / den
    f_im = (ni * lr - nr * li) / den
    br, bi = b_re.astype(f32), b_im.astype(f32)
    bb_re = f_re[..., None] * br - f_im[..., None] * bi
    bb_im = f_re[..., None] * bi + f_im[..., None] * br
    bu_re = jnp.einsum('blgc,gpc->blgp', ug, bb_re)
    bu_im = jnp.einsum('blgc,gpc->blgp', ug, bb_im)
    a_re = jnp.broadcast_to(ab_re, bu_re.shape)
    a_im = jnp.broadcast_to(ab_im, bu_im.shape)

    def combine(e1, e2):
        a1r, a1i, b1r, b1i = e1
        a2r, a2i, b2r, b2i = e2
        return (a2r * a1r - a2i * a1i, a2r * a1i + a2i * a1r,
                a2r * b1r - a2i * b1i + b2r, a2r * b1i + a2i * b1r + b2i)

    _, _, s_re, s_im = lax.associative_scan(combine, (a_re, a_im, bu_re, bu_im), axis=1)
    y = (jnp.einsum('blgp,gcp->blgc', s_re, c_re.astype(f32))
         - jnp.einsum('blgp,gcp->blgc', s_im, c_im.astype(f32)))
    y = y.reshape(Bt, L, S5_CH) + d_skip.astype(f32) * uf
    z = jax.nn.gelu(y)
    out = z * jax.nn.sigmoid(z @ w_glu.astype(f32) + b_glu.astype(f32))
    return out.astype(u.dtype)

def dsa_mixer(proj, cos_a, sin_a, cos_i, sin_i):
    f32 = jnp.float32
    Bt, L, _ = proj.shape
    q, k, v, qi, ki, wi = jnp.split(proj, C_SPLITS, axis=-1)
    q = partial_rope(q.reshape(Bt, L, N_HEADS, HEAD_DIM), cos_a[:, :, None], sin_a[:, :, None])
    k = partial_rope(k.reshape(Bt, L, N_KV_HEADS, HEAD_DIM), cos_a[:, :, None], sin_a[:, :, None])
    v = v.reshape(Bt, L, N_KV_HEADS, HEAD_DIM)
    qi = partial_rope(qi.reshape(Bt, L, IDX_HEADS, IDX_DIM), cos_i[:, :, None], sin_i[:, :, None])
    ki = partial_rope(ki, cos_i, sin_i).astype(f32)
    wi = wi.astype(f32) * (IDX_HEADS ** -0.5 * IDX_DIM ** -0.5)
    topk = min(TOPK_MAX, L // 4)
    nb = L // Q_BLOCK

    def to_blocks(t):
        return jnp.moveaxis(t.reshape(Bt, nb, Q_BLOCK, *t.shape[2:]), 1, 0)

    t_pos = jnp.arange(L, dtype=jnp.int32).reshape(nb, Q_BLOCK)
    key_pos = jnp.arange(L, dtype=jnp.int32)
    bidx = jnp.arange(Bt)[:, None, None]
    rep = N_HEADS // N_KV_HEADS

    def block(args):
        qb, qib, wb, tb = args
        logits = jax.nn.relu(jnp.einsum('bthd,bsd->bths', qib.astype(f32), ki))
        score = jnp.einsum('bths,bth->bts', logits, wb)
        causal = key_pos[None, :] <= tb[:, None]
        score = jnp.where(causal[None], score, -jnp.inf)
        _, idx = lax.top_k(score, topk)
        valid = idx <= tb[None, :, None]
        k_sel = k[bidx, idx]
        v_sel = v[bidx, idx]
        qg = qb.reshape(Bt, Q_BLOCK, N_KV_HEADS, rep, HEAD_DIM)
        s = jnp.einsum('btgrd,btjgd->btgrj', qg, k_sel).astype(f32) * (HEAD_DIM ** -0.5)
        s = jnp.where(valid[:, :, None, None, :], s, -jnp.inf)
        pr = jax.nn.softmax(s, axis=-1)
        o = jnp.einsum('btgrj,btjgd->btgrd', pr.astype(v.dtype), v_sel)
        return o.reshape(Bt, Q_BLOCK, N_HEADS * HEAD_DIM)

    out = lax.map(block, (to_blocks(q), to_blocks(qi), to_blocks(wi), t_pos))
    return jnp.moveaxis(out, 0, 1).reshape(Bt, L, N_HEADS * HEAD_DIM)

def second_inputs(seed: int = 0) -> dict:
    key = jax.random.key(seed)
    ks = jax.random.split(key, 32)
    f32 = jnp.float32

    def nrm(i, shape, scale):
        return jax.random.normal(ks[i], shape, f32) * scale

    x = nrm(0, (BATCH, SEQ, D_MODEL), 1.0)
    p = nrm(1, (DEPTH_2, BATCH, SEQ, PLE_DIM), 1.0)
    offs = jax.random.randint(ks[2], (BATCH, 1), 0, 1024, dtype=jnp.int32)
    positions = offs + jnp.arange(SEQ, dtype=jnp.int32)[None, :]
    ln_g = 1.0 + nrm(3, (DEPTH_2, 3, D_MODEL), 0.02)
    ln_b = nrm(4, (DEPTH_2, 3, D_MODEL), 0.02)
    ffn_w1 = nrm(5, (DEPTH_2, 2, D_MODEL, D_FF), D_MODEL ** -0.5)
    ffn_w3 = nrm(6, (DEPTH_2, 2, D_MODEL, D_FF), D_MODEL ** -0.5)
    ffn_w2 = nrm(7, (DEPTH_2, 2, D_FF, D_MODEL), D_FF ** -0.5 * DN_BETA)
    ple_w_proj = nrm(8, (DEPTH_2, PLE_DIM, D_MODEL), PLE_DIM ** -0.5)
    ple_w_gate = nrm(9, (DEPTH_2, D_MODEL, D_MODEL), D_MODEL ** -0.5)
    ab_w_in = nrm(10, (N_EVEN, D_MODEL, AB_IN), D_MODEL ** -0.5)
    ab_w_out = nrm(11, (N_EVEN, CONV_CH + S5_CH, D_MODEL), (CONV_CH + S5_CH) ** -0.5 * DN_BETA)
    conv_w = nrm(12, (N_EVEN, CONV_WIDTH, CONV_CH), CONV_WIDTH ** -0.5)
    s5_lam_re = -0.5 + nrm(13, (N_EVEN, S5_GROUPS, S5_STATE), 0.01)
    s5_lam_im = (math.pi * jnp.arange(S5_STATE, dtype=f32))[None, None, :] + nrm(14, (N_EVEN, S5_GROUPS, S5_STATE), 0.01)
    s5_log_dt = jax.random.uniform(ks[15], (N_EVEN, S5_GROUPS), f32, math.log(1e-3), math.log(1e-1))
    s5_b_re = nrm(16, (N_EVEN, S5_GROUPS, S5_STATE, S5_GROUP), (2 * S5_GROUP) ** -0.5)
    s5_b_im = nrm(17, (N_EVEN, S5_GROUPS, S5_STATE, S5_GROUP), (2 * S5_GROUP) ** -0.5)
    s5_c_re = nrm(18, (N_EVEN, S5_GROUPS, S5_GROUP, S5_STATE), S5_STATE ** -0.5)
    s5_c_im = nrm(19, (N_EVEN, S5_GROUPS, S5_GROUP, S5_STATE), S5_STATE ** -0.5)
    s5_d = nrm(20, (N_EVEN, S5_CH), 1.0)
    s5_w_glu = nrm(21, (N_EVEN, S5_CH, S5_CH), S5_CH ** -0.5)
    s5_b_glu = nrm(22, (N_EVEN, S5_CH), 0.02)
    c_w_in = nrm(23, (N_ODD, D_MODEL, C_IN), D_MODEL ** -0.5)
    c_w_out = nrm(24, (N_ODD, N_HEADS * HEAD_DIM, D_MODEL), (N_HEADS * HEAD_DIM) ** -0.5 * DN_BETA)
    return {'x': x, 'p': p, 'positions': positions, 'ln_g': ln_g, 'ln_b': ln_b,
            'ffn_w1': ffn_w1, 'ffn_w3': ffn_w3, 'ffn_w2': ffn_w2,
            'ple_w_proj': ple_w_proj, 'ple_w_gate': ple_w_gate,
            'ab_w_in': ab_w_in, 'ab_w_out': ab_w_out, 'conv_w': conv_w,
            's5_lam_re': s5_lam_re, 's5_lam_im': s5_lam_im, 's5_log_dt': s5_log_dt,
            's5_b_re': s5_b_re, 's5_b_im': s5_b_im, 's5_c_re': s5_c_re, 's5_c_im': s5_c_im,
            's5_d': s5_d, 's5_w_glu': s5_w_glu, 's5_b_glu': s5_b_glu,
            'c_w_in': c_w_in, 'c_w_out': c_w_out}

def second_block(x, p, positions, ln_g, ln_b, ffn_w1, ffn_w3, ffn_w2, ple_w_proj, ple_w_gate,
              ab_w_in, ab_w_out, conv_w, s5_lam_re, s5_lam_im, s5_log_dt, s5_b_re, s5_b_im,
              s5_c_re, s5_c_im, s5_d, s5_w_glu, s5_b_glu, c_w_in, c_w_out):
    cos_a, sin_a = rope_tables(positions, HEAD_DIM // ROT_FRAC)
    cos_i, sin_i = rope_tables(positions, IDX_DIM // ROT_FRAC)
    h = x
    for i in range(DEPTH_2):
        h = layer_norm(DN_ALPHA * h + 0.5 * swiglu(h, ffn_w1[i, 0], ffn_w3[i, 0], ffn_w2[i, 0]),
                       ln_g[i, 0], ln_b[i, 0])
        j = i // 2
        if i % 2 == 0:
            proj = h @ ab_w_in[j]
            hc, gb, gc, u = jnp.split(proj, [CONV_CH, 2 * CONV_CH, 3 * CONV_CH], axis=-1)
            ya = short_conv_mixer(hc, gb, gc, conv_w[j])
            yb = s5_mixer(u, s5_lam_re[j], s5_lam_im[j], s5_log_dt[j], s5_b_re[j], s5_b_im[j],
                          s5_c_re[j], s5_c_im[j], s5_d[j], s5_w_glu[j], s5_b_glu[j])
            mix = jnp.concatenate([ya, yb], axis=-1) @ ab_w_out[j]
        else:
            proj = h @ c_w_in[j]
            mix = dsa_mixer(proj, cos_a, sin_a, cos_i, sin_i) @ c_w_out[j]
        h = layer_norm(DN_ALPHA * h + mix, ln_g[i, 1], ln_b[i, 1])
        h = layer_norm(DN_ALPHA * h + 0.5 * swiglu(h, ffn_w1[i, 1], ffn_w3[i, 1], ffn_w2[i, 1]),
                       ln_g[i, 2], ln_b[i, 2])
        h = h + (p[i] @ ple_w_proj[i]) * jax.nn.sigmoid(h @ ple_w_gate[i])
    return h


def setup_inputs(seed=0):
    out = dict(first_inputs(seed))
    for name, value in second_inputs(seed + 1).items():
        if name != "x":
            out[name + "_2"] = value
    return out


def reference(
    x, attn_norm_g, w_in, conv_w, conv_b, filt_w1, filt_b1, filt_w2, filt_b2, filt_w3,
    filt_freq, hyena_skip, hyena_norm_g, lambda_q1, lambda_k1, lambda_q2, lambda_k2, subln_g,
    w_out, ffn_norm_g, w_router, w_gate, w_up, w_down, final_norm_g, p_2, positions_2, ln_g_2,
    ln_b_2, ffn_w1_2, ffn_w3_2, ffn_w2_2, ple_w_proj_2, ple_w_gate_2, ab_w_in_2, ab_w_out_2,
    conv_w_2, s5_lam_re_2, s5_lam_im_2, s5_log_dt_2, s5_b_re_2, s5_b_im_2, s5_c_re_2, s5_c_im_2,
    s5_d_2, s5_w_glu_2, s5_b_glu_2, c_w_in_2, c_w_out_2,
):
    x = first_block(
        x, attn_norm_g, w_in, conv_w, conv_b, filt_w1, filt_b1, filt_w2, filt_b2, filt_w3,
        filt_freq, hyena_skip, hyena_norm_g, lambda_q1, lambda_k1, lambda_q2, lambda_k2,
        subln_g, w_out, ffn_norm_g, w_router, w_gate, w_up, w_down, final_norm_g,
    )
    return second_block(
        x, p_2, positions_2, ln_g_2, ln_b_2, ffn_w1_2, ffn_w3_2, ffn_w2_2, ple_w_proj_2,
        ple_w_gate_2, ab_w_in_2, ab_w_out_2, conv_w_2, s5_lam_re_2, s5_lam_im_2, s5_log_dt_2,
        s5_b_re_2, s5_b_im_2, s5_c_re_2, s5_c_im_2, s5_d_2, s5_w_glu_2, s5_b_glu_2, c_w_in_2,
        c_w_out_2,
    )


_drawn_inputs = setup_inputs


def setup_inputs(seed=0):
    import zlib

    import numpy as np

    out = dict(_drawn_inputs(seed))
    spreads = {}
    factors = {'filt_freq': 2.883,
     'hyena_norm_g': 3.883,
     'lambda_k1': 3.225,
     'lambda_k2': 2.883,
     'subln_g': 4.519,
     'ffn_norm_g': 4.702,
     'final_norm_g': 8.278,
     's5_lam_re_2': 64.0,
     's5_lam_im_2': 64.0,
     's5_log_dt_2': 64.0,
     's5_b_re_2': 64.0,
     's5_b_im_2': 64.0,
     's5_c_re_2': 64.0,
     's5_c_im_2': 64.0,
     's5_b_glu_2': 64.0,
     's5_w_glu_2': 2.764}
    for name, (base, spread) in spreads.items():
        noise = np.random.default_rng([zlib.crc32(name.encode()), seed]).standard_normal(out[name].shape)
        drawn = base * np.exp(spread * noise) if base else spread * noise
        out[name] = jnp.asarray(drawn.astype(out[name].dtype))
    for name, factor in factors.items():
        out[name] = (out[name] * factor).astype(out[name].dtype)
    return out
```

```python
import math
from contextlib import ExitStack

import numpy as np
import concourse.bass as bass
from concourse import mybir

F32 = mybir.dt.float32
F32R = mybir.dt.float32r
I32 = mybir.dt.int32
ALU = mybir.AluOpType
ACT = mybir.ActivationFunctionType
AX = mybir.AxisListType.X

P = 128
S = 256
ST = S // P
D = 1024
DK = D // P
EPS = 1e-6
HY = 512
HC = HY // P
NORD = 2
NF = 2 * S
FM = NF // P
EMB, HID = 33, 64
HEADS, DH = 4, 64
LAM_INIT = 0.8 - 0.6 * math.exp(0.0)
NE, CAP, FF = 16, 32, 2816
NG = 4
FG = FF // NG
FH = FG // 2
FT = FG // P
FR = FG - FT * P

ALPHA = 4.0 ** 0.25
LN_EPS = 1e-5
PLE = 256
CC = 512
S5G, S5C, S5N = 32, 16, 64
QH, HD, KVH, IH, ID = 8, 128, 2, 8, 64
TOPK = 64
C_IN = QH * HD + 2 * KVH * HD + IH * ID + ID + IH

SLOT = 3072
SLOTS = 8
ARENA = 16256
WORK = 12288

FIX = {}
_at = 0
for _n, _w in [("ident", P), ("ones", P), ("ones0", P), ("group_mean", P), ("mask_b", 2), ("mask_c", 2), ("seed1", P), ("seed2", P), ("slot_no", CAP),
               ("inv_freq", 24), ("attn_g", DK), ("conv_w", 36), ("conv_b", 12), ("skip", 8), ("hy_g", HC),
               ("subln_g", 1), ("ffn_g", DK), ("filt", 3), ("conv_w2", 12), ("s5_d", 4), ("b_glu", 4), ("misc", 40)]:
    FIX[_n] = (_at, _w)
    _at += _w
FIXED = _at
LOADED = FIX["misc"][0]
X0 = 1024 if FIXED <= 1024 else FIXED
HT0 = X0 + ST * D
R0 = HT0 + DK * S
PARTS = 4096 + 1024


class InOrder:

    def __init__(self, done):
        self.done, self.count = done, 0

    def on(self, engine):
        self.engine = engine
        return self

    def __call__(self, instruction):
        self.count += 1
        instruction.then_inc(self.done, 1)
        self.engine.wait_ge(self.done, self.count)


class Ring:

    def __init__(self):
        self.marks = [0] * SLOTS
        self.mark = {}

    def landing(self, n, dmas=1):
        self.marks[n % SLOTS] += 16 * dmas
        self.mark[n] = self.marks[n % SLOTS]
        return self.mark[n]


class Core:
    pass


ENGINES = ("tensor", "scalar", "vector", "gpsimd")


class Stage:

    def __init__(self, tensor, scalar, vector, gpsimd=None):
        self.tensor, self.scalar, self.vector = tensor, scalar, vector
        self.gpsimd = gpsimd or (lambda pool: None)


def meet(k, name, engine, i):
    engine.drain().then_inc(k.passed[name], 1)
    for other in ENGINES:
        if other != name:
            engine.wait_ge(k.passed[other], i + 1)


def setup(nc, stack):
    k = Core()
    k.nc = nc
    base = -(-nc.sbuf_base // 32) * 32
    place = lambda name, at, shape, dt: nc.alloc_sbuf_tensor_at(name, shape, dt, offset=base + 4 * at)
    at_arena, at_work = SLOTS * SLOT, SLOTS * SLOT + ARENA
    k.ring = place("ring", 0, [P, SLOTS * SLOT], F32)
    k.arena = place("arena", at_arena, [P, ARENA], F32)
    k.work = place("work", at_work, [P, WORK], F32)
    k.w13 = place("w13", at_work, [P, 2, 2, 2, DK, P], F32R)
    k.w2 = place("w2", at_work + 8192, [P, 2, 2, D], F32R)
    k.hsplit = place("hsplit", at_work - PARTS, [P, 2, DK, S], F32R)
    k.hidsplit = place("hidsplit", at_work - PARTS + 4096, [P, 2, 2, S], F32R)
    k.ps = stack.enter_context(nc.psum_tensor("ps", [P, 8, 512], F32))
    made = {}

    def sem(name):
        if name not in made:
            made[name] = stack.enter_context(nc.semaphore(name))
        return made[name]

    k.sem = sem
    k.vector_order, k.pool_order = InOrder(sem("vector_order")), InOrder(sem("pool_order"))
    k.slot_ready = [k.sem(f"slot_ready{i}") for i in range(SLOTS)]
    k.slot_freed = k.sem("slot_freed")
    k.use = Ring()
    k.passed = {name: k.sem(f"{name}_passed") for name in ENGINES}
    k.x = k.arena[:, X0:X0 + ST * D].rearrange("p (t d) -> p t d", t=ST)
    k.hT = k.arena[:, HT0:HT0 + DK * S].rearrange("p (k s) -> p k s", k=DK)
    k.ident = fix(k, "ident")
    return k


def fix(k, name):
    a, w = FIX[name]
    return k.arena[:, a:a + w]


def slot(k, n, width=SLOT):
    s = n % SLOTS
    return k.ring[:, s * SLOT:s * SLOT + width]


def area(core, at, width, /, **shape):
    return view(core.arena[:, R0 + at:R0 + at + width], **shape)


def work(core, at, width, /, **shape):
    return view(core.work[:, at:at + width], **shape)


def view(v, /, **shape):
    if not shape:
        return v
    names = list(shape)
    return v.rearrange(f"p ({' '.join(names)} z) -> p {' '.join(names)} z", **shape)


def load_slots(k, sync, weights):
    for n, pairs in weights:
        if n >= SLOTS:
            sync.wait_ge(k.slot_freed, n - SLOTS + 1)
        for dst, src in pairs:
            sync.dma_start(dst, src).then_inc(k.slot_ready[n % SLOTS], 16)


def range_reduce(step, vector, out, angle, n):
    magic = 12582912.0
    c1 = 6.28125
    c2 = float(np.float32(np.round((2 * math.pi - c1) * 2 ** 21) / 2 ** 21))
    c3 = float(np.float32(2 * math.pi - c1 - c2))
    step(vector.tensor_scalar(n, angle, 1.0 / (2 * math.pi), magic, ALU.mult, ALU.add))
    step(vector.tensor_scalar(n, n, magic, None, ALU.subtract))
    step(vector.scalar_tensor_tensor(out=out, in0=n, scalar=-c1, in1=angle, op0=ALU.mult, op1=ALU.add))
    step(vector.scalar_tensor_tensor(out=out, in0=n, scalar=-c2, in1=out, op0=ALU.mult, op1=ALU.add))
    step(vector.scalar_tensor_tensor(out=out, in0=n, scalar=-c3, in1=out, op0=ALU.mult, op1=ALU.add))
    return vector.tensor_scalar(out, out, 3.1415925, -3.1415925, ALU.min, ALU.max)


def misc(k, a, w):
    b = FIX["misc"][0]
    return k.arena[:, b + a:b + a + w]


def filters(k, x, fixed, dft, filt_tables, filt_w1, filt_w2, filt_w3, zT):
    nc = k.nc
    sem = k.sem
    x_loaded, fixed_loaded, tables_loaded = sem("x_loaded"), sem("fixed_loaded"), sem("tables_loaded")
    ones_set, square_sum, root, normed = sem("ones_set"), sem("ms_ready"), sem("ms_root"), sem("normed")
    turned, sin_arg, sin_done = sem("turned"), sem("sin_arg"), sem("sin_done")
    layer_done, taps_ready, taps_put = sem("layer_done"), sem("taps_ready"), sem("taps_put")
    abs_done, l1_done, l1_inverse = sem("abs_done"), sem("l1_done"), sem("l1_inverse")
    freq_ready, freq_put, hT_put, hT_bank = sem("freq_ready"), sem("freq_put"), sem("hT_put"), sem("hT_bank")

    K = area(k, 0, 4096, o=NORD, m=FM)
    Kn = area(k, 4096, 1024, o=NORD)
    k.K, k.Kn = K, Kn
    dft_sb = area(k, 5120, 2048)
    k.Fwd = view(dft_sb[:, 0:1024], t=ST)
    k.Inv = view(dft_sb[:, 1024:2048], m=FM)
    tab = work(k, 0, 2048)
    Bwd, decay = view(tab[:, 0:1024], t=ST), view(tab[:, 1024:2048], t=ST)
    w3 = work(k, 2048, 2048)
    taps = work(k, 4096, 4096, t=ST, n=4)
    z_sb = work(k, 8192, 256)
    w1, w2 = work(k, 8448, 64), work(k, 8512, 64)
    arg, hid, nrev = work(k, 8576, 256), work(k, 8832, 256), work(k, 9088, 256)
    mag = work(k, 9344, 1024, b=2)
    inv = work(k, 10368, 1024, o=2)
    xn = area(k, 7168, 2048, t=ST)
    ones, ones0 = fix(k, "ones"), fix(k, "ones0")
    stat = misc(k, 0, 8)
    filt = fix(k, "filt")

    def load(sync):
        sync.dma_start(k.x, x.rearrange("b (t p) d -> p (b t) d", p=P)).then_inc(x_loaded, 16)
        sync.dma_start(k.arena[:, 0:LOADED], fixed).then_inc(fixed_loaded, 16)

    def scalar(act):
        for dst, src in ((z_sb[0:EMB, :], zT), (w1[0:EMB, :], filt_w1[0]), (w2[0:HID, :], filt_w2[0]),
                         (w3[0:HID, :], filt_w3[0]), (tab, filt_tables), (dft_sb, dft)):
            act.dma_start(dst, src).then_inc(tables_loaded, 16)
        act.wait_ge(square_sum, 1)
        act.activation(stat[:, 2:4], stat[:, 2:4], ACT.Sqrt).then_inc(root, 1)
        for layer in range(2):
            act.wait_ge(sin_arg, layer + 1)
            act.activation(hid[0:HID, :], arg[0:HID, :], ACT.Sin).then_inc(sin_done, 1)
        for i in range(ST * 4):
            act.wait_ge(taps_put, i + 1)
            if i >= 2:
                act.wait_ge(l1_done, i - 1)
            act.activation(mag[:, i % 2, :], taps[:, i // 4, i % 4, :], ACT.Abs).then_inc(abs_done, 1)

    def tensor(pe):
        pe.wait_ge(fixed_loaded, 16)
        pe.wait_ge(normed, 2)
        for b in range(4):
            for j in range(4):
                kk, t = 2 * b + j // 2, j % 2
                last = pe.transpose(k.ps[:, b, j * P:(j + 1) * P], xn[:, t, kk * P:(kk + 1) * P], k.ident)
            last.then_inc(hT_bank, 1)
        pe.wait_ge(tables_loaded, 16 * 6)
        pe.matmul(k.ps[0:HID, 4, 0:S], w1[0:EMB, :], z_sb[0:EMB, :], start=True, stop=True).then_inc(layer_done, 1)
        pe.wait_ge(sin_done, 1)
        pe.matmul(k.ps[0:HID, 5, 0:S], w2[0:HID, :], hid[0:HID, :], start=True, stop=True).then_inc(layer_done, 1)
        pe.wait_ge(sin_done, 2)
        pe.wait_ge(hT_put, DK)
        for i in range(ST * 4):
            t, n = i // 4, i % 4
            if i >= 4:
                pe.wait_ge(taps_put, i - 3)
            pe.matmul(k.ps[:, i % 4, :], hid[0:HID, t * P:(t + 1) * P], w3[0:HID, n * HY:(n + 1) * HY],
                      start=True, stop=True).then_inc(taps_ready, 1)
        for i in range(ST * 4):
            t, n = i // 4, i % 4
            direction, order = n // 2, n % 2
            pe.wait_ge(abs_done, i + 1)
            pe.matmul(k.ps[:, 6 + order, :], ones0 if direction and t == 0 else ones, mag[:, i % 2, :],
                      start=(t == 0 and direction == 0), stop=(t == ST - 1 and direction == 1)).then_inc(l1_done, 1)
        pe.wait_ge(taps_put, ST * 4)
        for i in range(NORD * FM):
            order, m = i // FM, i % FM
            if i >= 4:
                pe.wait_ge(freq_put, i - 3)
            for a in range(4):
                t, direction = a // 2, a % 2
                table = Bwd if direction else k.Fwd
                last = pe.matmul(k.ps[:, i % 4, :], table[:, t, m * P:(m + 1) * P],
                                 taps[:, t, 2 * direction + order, :], start=(a == 0), stop=(a == 3))
            last.then_inc(freq_ready, 1)

    def vector(dve):
        step = k.vector_order.on(dve)
        dve.wait_ge(x_loaded, 16)
        for t in range(ST):
            step(dve.tensor_tensor_reduce(xn[:, t, :], k.x[:, t, :], k.x[:, t, :], 1.0, 0.0, ALU.mult, ALU.add,
                                          stat[:, t:t + 1]))
        dve.tensor_scalar(stat[:, 2:4], stat[:, 0:2], 1.0 / D, EPS, ALU.mult, ALU.add).then_inc(square_sum, 1)
        dve.wait_ge(root, 1)
        step(dve.reciprocal(stat[:, 4:6], stat[:, 2:4]))
        for t in range(ST):
            dve.tensor_scalar(xn[:, t, :], k.x[:, t, :], stat[:, 4 + t:5 + t], None, ALU.mult).then_inc(normed, 1)
        dve.wait_ge(fixed_loaded, 16)
        for kk in range(DK):
            dve.wait_ge(hT_bank, kk // 2 + 1)
            dve.tensor_scalar(k.hT[:, kk, :], k.ps[:, kk // 2, (kk % 2) * S:(kk % 2 + 1) * S],
                              fix(k, "attn_g")[:, kk:kk + 1], None, ALU.mult).then_inc(hT_put, 1)
        for layer in range(2):
            dve.wait_ge(layer_done, layer + 1)
            step(dve.tensor_scalar(arg[0:HID, :], k.ps[0:HID, 4 + layer, 0:S], filt[0:HID, layer:layer + 1],
                                   filt[0:HID, 2:3], ALU.add, ALU.mult))
            range_reduce(step, dve, arg[0:HID, :], arg[0:HID, :], nrev[0:HID, :]).then_inc(sin_arg, 1)
        for i in range(ST * 4):
            t, n = i // 4, i % 4
            dve.wait_ge(taps_ready, i + 1)
            dve.tensor_tensor(taps[:, t, n, :], k.ps[:, i % 4, :], decay[:, t, :], ALU.mult).then_inc(taps_put, 1)
        dve.wait_ge(l1_done, ST * 4)
        for order in range(NORD):
            step(dve.reciprocal(inv[:, order, :], k.ps[:, 6 + order, :]))
        for i in range(NORD * FM):
            order, m = i // FM, i % FM
            dve.wait_ge(freq_ready, i + 1)
            dve.tensor_tensor(K[:, order, m, :], k.ps[:, i % 4, :], inv[:, order, :], ALU.mult).then_inc(freq_put, 1)
        dve.wait_ge(freq_put, NORD * FM)
        for order in range(NORD):
            step(dve.tensor_copy(Kn[:, order, :], K[:, order, 0, :]))
            step(dve.tensor_copy(Kn[0:1, order, :], K[0:1, order, 2, :]))
            step(dve.memset(K[0:1, order, 2, :], 0.0))

    return load, Stage(tensor, scalar, vector)


def projections(k):
    nc = k.nc
    sem = k.sem
    column_done, convolved, copied = sem("column_done"), sem("convolved"), sem("copied")
    centre_put = sem("centre_put")
    u = work(k, 0, 3072, c=12)
    qk = work(k, 3072, 2048, c=8)
    v = work(k, 5120, 1024, t=ST)
    k.u, k.qk, k.v = u, qk, v
    conv_w, conv_b = fix(k, "conv_w"), fix(k, "conv_b")

    def tensor(pe):
        for n in range(DK):
            pe.wait_ge(k.slot_ready[n], 16)
        for c in range(20):
            if 6 <= c < 18:
                pe.wait_ge(convolved, c - 5)
            elif c >= 18:
                pe.wait_ge(copied, c - 17)
            for kk in range(DK):
                last = pe.matmul(k.ps[:, c % 6, 0:S], slot(k, kk)[:, c * P:(c + 1) * P], k.hT[:, kk, :],
                                 start=(kk == 0), stop=(kk == DK - 1))
            last.then_inc(column_done, 1)
        for t in range(ST):
            for kk in range(DK):
                last = pe.matmul(k.ps[:, 6 + t, :], k.hT[:, kk, t * P:(t + 1) * P], slot(k, kk)[:, 20 * P:24 * P],
                                 start=(kk == 0), stop=(kk == DK - 1))
            last.then_inc(column_done, 1)
        pe.drain().then_inc(k.slot_freed, DK)

    def scalar(act):
        for c in range(20):
            act.wait_ge(column_done, c + 1)
            if c < 12:
                act.activation(u[:, c, :], k.ps[:, c % 6, 0:S], ACT.Identity, scale=conv_w[:, 12 + c:13 + c],
                               bias=conv_b[:, c:c + 1]).then_inc(centre_put, 1)
            else:
                act.activation(qk[:, c - 12, :], k.ps[:, c % 6, 0:S], ACT.Copy).then_inc(copied, 1)
        for t in range(ST):
            act.wait_ge(column_done, 21 + t)
            act.activation(v[:, t, :], k.ps[:, 6 + t, :], ACT.Copy)

    def vector(dve):
        step = k.vector_order.on(dve)
        for c in range(12):
            dve.wait_ge(centre_put, c + 1)
            step(dve.scalar_tensor_tensor(out=u[:, c, 1:S], in0=k.ps[:, c % 6, 0:S - 1], scalar=conv_w[:, c:c + 1],
                                          in1=u[:, c, 1:S], op0=ALU.mult, op1=ALU.add))
            dve.scalar_tensor_tensor(out=u[:, c, 0:S - 1], in0=k.ps[:, c % 6, 1:S],
                                     scalar=conv_w[:, 24 + c:25 + c], in1=u[:, c, 0:S - 1], op0=ALU.mult,
                                     op1=ALU.add).then_inc(convolved, 1)

    return Stage(tensor, scalar, vector)


def hyena(k):
    nc = k.nc
    sem = k.sem
    z_turned, z_put, spectrum_done = sem("z_turned"), sem("z_put"), sem("spectrum_done")
    product_put, mixed, wave_done = sem("product_put"), sem("mixed"), sem("wave_done")
    hy_square, hy_mean, hy_root = sem("hy_square"), sem("hy_mean"), sem("hy_root")
    gated = sem("gated")
    U, K, Kn = k.u, k.K, k.Kn
    prod = area(k, 7168, 2048, n=4)
    Y = work(k, 6144, 2048, m=FM)
    zs = work(k, 8192, 1024, t=ST)
    mixT = k.hT
    tmp = area(k, 9216, 1024, c=HC)
    tmp2 = area(k, 7168, 1024, c=HC)
    z = U[:, 8:12, :]

    def tensor(pe):
        for o in range(NORD):
            if o:
                pe.wait_ge(gated, HC)
            for t in range(ST):
                for c in range(HC):
                    last = pe.transpose(k.ps[:, t, c * P:(c + 1) * P], z[:, c, t * P:(t + 1) * P], k.ident)
            last.then_inc(z_turned, 1)
            pe.wait_ge(z_put, ST * (o + 1))
            for m in (0, 2, 1, 3):
                if m == 0 and o:
                    pe.wait_ge(mixed, 4)
                for t in range(ST):
                    last = pe.matmul(k.ps[:, 2 + m, :], k.Fwd[:, t, m * P:(m + 1) * P], zs[:, t, :],
                                     start=(t == 0), stop=(t == ST - 1))
                last.then_inc(spectrum_done, 1)
            pe.wait_ge(mixed, 4 * (o + 1))
            for c in range(HC):
                if c >= 2:
                    pe.wait_ge(gated, HC * o + c - 1)
                for m in range(FM):
                    last = pe.matmul(k.ps[:, 6 + c % 2, 0:S], Y[:, m, c * P:(c + 1) * P], k.Inv[:, m, :],
                                     start=(m == 0), stop=(m == FM - 1))
                last.then_inc(wave_done, 1)
        for c in range(HC):
            pe.wait_ge(hy_square, c + 1)
            pe.matmul(k.ps[:, c, 0:S], fix(k, "group_mean"), tmp[:, c, :], start=True, stop=True).then_inc(hy_mean, 1)

    def gpsimd(pool):
        for o in range(NORD):
            for h in range(2):
                pool.wait_ge(product_put, 8 * o + 4 * h + 4)
                pool.tensor_tensor(Y[:, h, :], prod[:, 0, :], prod[:, 1, :], ALU.subtract).then_inc(mixed, 1)
                pool.tensor_tensor(Y[:, 2 + h, :], prod[:, 2, :], prod[:, 3, :], ALU.add).then_inc(mixed, 1)

    def scalar(act):
        for o in range(NORD):
            act.wait_ge(z_turned, o + 1)
            for t in range(ST):
                act.activation(zs[:, t, :], k.ps[:, t, :], ACT.Copy).then_inc(z_put, 1)
        for c in range(HC):
            act.wait_ge(gated, HC + c + 1)
            act.activation(tmp[:, c, :], z[:, c, :], ACT.Square).then_inc(hy_square, 1)
        for c in range(HC):
            act.wait_ge(hy_mean, c + 1)
            act.activation(tmp2[:, c, :], k.ps[:, c, 0:S], ACT.Sqrt, bias=misc(k, 8, 1)).then_inc(hy_root, 1)

    def vector(dve):
        step = k.vector_order.on(dve)
        step(dve.memset(misc(k, 8, 1), EPS))
        for o in range(NORD):
            for h in range(2):
                dve.wait_ge(spectrum_done, 4 * o + 2 * h + 2)
                re, im = k.ps[:, 2 + h, :], k.ps[:, 4 + h, :]
                if o or h:
                    dve.wait_ge(mixed, 4 * o + 2 * h)
                for i, (a, b) in enumerate(((re, K[:, o, h, :]), (im, K[:, o, 2 + h, :]),
                                            (im, Kn[:, o, :] if h == 0 else K[:, o, 1, :]),
                                            (re, K[:, o, 2 + h, :]))):
                    dve.tensor_tensor(prod[:, i, :], a, b, ALU.mult).then_inc(product_put, 1)
            dve.wait_ge(gated, HC * o)
            for c in range(HC):
                dve.wait_ge(wave_done, HC * o + c + 1)
                step(dve.scalar_tensor_tensor(out=z[:, c, :], in0=z[:, c, :],
                                              scalar=fix(k, "skip")[:, 4 * o + c:4 * o + c + 1],
                                              in1=k.ps[:, 6 + c % 2, 0:S], op0=ALU.mult, op1=ALU.add))
                dve.tensor_tensor(z[:, c, :], z[:, c, :], U[:, 4 * o + c, :], ALU.mult).then_inc(gated, 1)
        for c in range(HC):
            dve.wait_ge(hy_root, c + 1)
            step(dve.reciprocal(tmp2[:, c, :], tmp2[:, c, :]))
            dve.scalar_tensor_tensor(out=mixT[:, c, :], in0=z[:, c, :], scalar=fix(k, "hy_g")[:, c:c + 1],
                                     in1=tmp2[:, c, :], op0=ALU.mult, op1=ALU.mult)

    return Stage(tensor, scalar, vector, gpsimd)


def attention(k, dist, lam_rows):
    nc = k.nc
    sem = k.sem
    dist_loaded, score_done = sem("dist_loaded"), sem("score_done")
    score_read, score_put = sem("score_read"), sem("score_put")
    exp_done, lam_arg, lam_exp = sem("exp_done"), sem("lam_arg"), sem("lam_exp")
    a_put, a_turned, aT_put, o_done, o_put = sem("p_put"), sem("p_turned"), sem("pT_put"), sem("o_done"), sem("o_put")
    sq_put, ms_done, at_root = sem("sq_put"), sem("ms_done"), sem("at_root")
    mixT = k.hT
    dist_sb = area(k, 0, 512, t=ST)
    lam_sb = area(k, 512, 256)
    s = area(k, 1024, 2048, b=2, n=4)
    a = area(k, 3072, 1024, b=2, t=ST)
    aT = area(k, 4096, 1024, b=2, t=ST)
    oT = area(k, 5120, 1024, h=HEADS)
    sq = area(k, 6144, 1024, n=2)
    rt = area(k, 7168, 1024, h=HEADS)
    m = misc(k, 10, 30)
    lam = m[:, 0:1]
    scale = DH ** -0.5
    slopes = [float(np.float32(2.0 ** (-8.0 * (i + 1) / HEADS))) for i in range(HEADS)]

    def tensor(pe):
        for h in range(HEADS + 1):
            if h < HEADS:
                if h >= 2:
                    pe.wait_ge(score_read, 2 * (h - 1))
                for c in range(2):
                    for t in range(ST):
                        last = pe.matmul(k.ps[:, 2 * (h % 2) + c, t * S:(t + 1) * S],
                                         k.qk[c * DH:(c + 1) * DH, h, t * P:(t + 1) * P],
                                         k.qk[c * DH:(c + 1) * DH, HEADS + h, :], start=True, stop=True)
                    last.then_inc(score_done, 1)
            if h:
                g = h - 1
                pe.wait_ge(a_put, ST * (g + 1))
                if g >= 2:
                    pe.wait_ge(aT_put, g - 1)
                for t in range(ST):
                    for kc in range(ST):
                        last = pe.transpose(k.ps[:, 4 + g % 2, kc * S + t * P:kc * S + (t + 1) * P],
                                            a[:, g % 2, t, kc * P:(kc + 1) * P], k.ident)
                last.then_inc(a_turned, 1)
                pe.wait_ge(aT_put, g + 1)
                if g >= 2:
                    pe.wait_ge(o_put, g - 1)
                for kc in range(ST):
                    last = pe.matmul(k.ps[:, 6 + g % 2, 0:S], k.v[:, kc, g * P:(g + 1) * P], aT[:, g % 2, kc, :],
                                     start=(kc == 0), stop=(kc == ST - 1))
                last.then_inc(o_done, 1)
        for n in range(2):
            pe.wait_ge(sq_put, n + 1)
            pe.matmul(k.ps[:, n, :], fix(k, "ones"), sq[:, n, :], start=True, stop=True).then_inc(ms_done, 1)

    def scalar(act):
        act.dma_start(dist_sb, dist).then_inc(dist_loaded, 16)
        act.dma_start(lam_sb, lam_rows).then_inc(dist_loaded, 16)
        act.wait_ge(lam_arg, 2)
        act.activation(m[:, 1:3], m[:, 1:3], ACT.Exp).then_inc(lam_exp, 1)
        for h in range(HEADS):
            act.wait_ge(score_put, h + 1)
            for n in range(4):
                act.activation(s[:, h % 2, n, :], s[:, h % 2, n, :], ACT.Exp, scale=scale,
                               bias=m[:, 8 + 4 * (h % 2) + n:9 + 4 * (h % 2) + n],
                               accum_out=m[:, 16 + 4 * (h % 2) + n:17 + 4 * (h % 2) + n]).then_inc(exp_done, 1)
            if h:
                act.wait_ge(o_done, h)
                act.activation(oT[:, h - 1, :], k.ps[:, 6 + (h - 1) % 2, 0:S], ACT.Copy).then_inc(o_put, 1)
        act.wait_ge(o_done, HEADS)
        act.activation(oT[:, HEADS - 1, :], k.ps[:, 6 + (HEADS - 1) % 2, 0:S], ACT.Copy).then_inc(o_put, 1)
        for n in range(2):
            act.wait_ge(o_put, HEADS)
            act.activation(sq[:, n, :], oT[:, 2 * n:2 * n + 2, :], ACT.Square).then_inc(sq_put, 1)
        for n in range(2):
            act.wait_ge(ms_done, n + 1)
            act.activation(rt[:, 2 * n:2 * n + 2, :], k.ps[:, n, :], ACT.Sqrt, scale=1.0 / P,
                           bias=misc(k, 8, 1)).then_inc(at_root, 1)

    def vector(dve):
        step = k.vector_order.on(dve)
        dve.wait_ge(dist_loaded, 32)
        for i in range(2):
            dve.tensor_tensor_reduce(lam_sb[:, 2 * i * DH:(2 * i + 1) * DH], lam_sb[:, 2 * i * DH:(2 * i + 1) * DH],
                                     lam_sb[:, (2 * i + 1) * DH:(2 * i + 2) * DH], 1.0, 0.0, ALU.mult, ALU.add,
                                     m[:, 1 + i:2 + i]).then_inc(lam_arg, 1)
        step(dve.tensor_scalar(m[:, 3:4], fix(k, "subln_g"), 1.0 - LAM_INIT, None, ALU.mult))
        dve.wait_ge(lam_exp, 1)
        step(dve.tensor_tensor(m[:, 0:1], m[:, 1:2], m[:, 2:3], ALU.subtract))
        step(dve.tensor_scalar(m[:, 0:1], m[:, 0:1], LAM_INIT, None, ALU.add))

        def score(h):
            b = h % 2
            for c in range(2):
                dve.wait_ge(score_done, 2 * h + c + 1)
                dve.scalar_tensor_tensor(out=s[:, b, 2 * c:2 * c + 2, :], in0=dist_sb, scalar=-slopes[h] / scale,
                                         in1=k.ps[:, 2 * b + c, :].rearrange("p (t s) -> p t s", t=ST),
                                         op0=ALU.mult, op1=ALU.add).then_inc(score_read, 1)
            dve.wait_ge(score_read, 2 * h + 2)
            step(dve.tensor_reduce(m[:, 8 + 4 * b:12 + 4 * b], s[:, b], AX, ALU.max))
            dve.tensor_scalar(m[:, 8 + 4 * b:12 + 4 * b], m[:, 8 + 4 * b:12 + 4 * b], -scale, None,
                              ALU.mult).then_inc(score_put, 1)

        def combine(h):
            b = h % 2
            r = m[:, 16 + 4 * b:20 + 4 * b]
            dve.wait_ge(exp_done, 4 * h + 4)
            step(dve.reciprocal(r, r))
            step(dve.tensor_scalar(r[:, 2:4], r[:, 2:4], lam, None, ALU.mult))
            for t in range(ST):
                step(dve.tensor_scalar(s[:, b, 2 + t, :], s[:, b, 2 + t, :], r[:, 2 + t:3 + t], None, ALU.mult))
            for t in range(ST):
                dve.scalar_tensor_tensor(out=a[:, b, t, :], in0=s[:, b, t, :], scalar=r[:, t:t + 1],
                                         in1=s[:, b, 2 + t, :], op0=ALU.mult, op1=ALU.subtract).then_inc(a_put, 1)
            dve.wait_ge(a_turned, h + 1)
            dve.tensor_copy(aT[:, b], k.ps[:, 4 + b, :].rearrange("p (t s) -> p t s", t=ST)).then_inc(aT_put, 1)

        for h in range(HEADS):
            if h >= 2:
                dve.wait_ge(a_put, ST * (h - 1))
            score(h)
            if h:
                combine(h - 1)
        combine(HEADS - 1)
        for n in range(2):
            dve.wait_ge(at_root, n + 1)
            step(dve.reciprocal(rt[:, 2 * n:2 * n + 2, :], rt[:, 2 * n:2 * n + 2, :]))
            dve.scalar_tensor_tensor(out=mixT[:, HC + 2 * n:HC + 2 * n + 2, :], in0=oT[:, 2 * n:2 * n + 2, :],
                                     scalar=m[:, 3:4], in1=rt[:, 2 * n:2 * n + 2, :], op0=ALU.mult, op1=ALU.mult)

    return Stage(tensor, scalar, vector)


def mixer_out(k, first, mixT, seed=None):
    out_done = k.sem("out_done")

    def tensor(pe):
        for n in range(first, first + 3):
            pe.wait_ge(k.slot_ready[n % SLOTS], k.use.mark[n])
        for t in range(ST):
            for half in range(2):
                if seed is not None:
                    pe.matmul(k.ps[:, 2 * t + half, :], seed, k.x[:, t, half * 512:(half + 1) * 512], start=True, stop=False)
                for kk in range(DK):
                    w = slot(k, first + kk // 3)[:, (kk % 3) * D + half * 512:(kk % 3) * D + (half + 1) * 512]
                    last = pe.matmul(k.ps[:, 2 * t + half, :], mixT[:, kk, t * P:(t + 1) * P], w,
                                     start=(kk == 0 and seed is None), stop=(kk == DK - 1))
                last.then_inc(out_done, 1)
        pe.drain().then_inc(k.slot_freed, 3)

    return out_done, tensor


def routing(k, first_out):
    nc = k.nc
    sem = k.sem
    out_done, out_tensor = mixer_out(k, first_out, k.hT)
    ms_ready, rt_root, h_ready = sem("ms_ready"), sem("ms_root"), sem("rt_h_ready")
    hT_bank, hT_put, logits_done = sem("hT_bank"), sem("hT_put"), sem("logits_done")
    exp_arg, aff_exp, aff_ready, aff_turned = sem("exp_arg"), sem("aff_exp"), sem("aff_ready"), sem("aff_turned")
    slots_ready, slots_turned, pick_ready, weight_ready = sem("slots_ready"), sem("slots_turned"), sem("pick_ready"), sem("weight_ready")
    weight_turned, weight_put, xin_done, xin_put = sem("weight_turned"), sem("weight_put"), sem("xin_done"), sem("xin_put")
    router_loaded = sem("router_loaded")
    h = area(k, 2048, 2048, t=ST)
    pick = area(k, 4096, 1024, t=ST)
    k.weightT = area(k, 5120, 1024, q=NG)
    k.xin = k.arena[:, HT0:HT0 + 4096].rearrange("p (k c) -> p k c", k=DK)
    wr = area(k, 6144, 128, k=DK)
    logit = area(k, 6272, 32, t=ST)
    aff = area(k, 6304, 32, t=ST)
    affT = area(k, 6336, 256)
    left = area(k, 6592, 256)
    count = area(k, 6848, 256)
    top = area(k, 7104, 32)
    slot_of = area(k, 7136, 32, t=ST)
    pickw = area(k, 7168, 1024, t=ST)
    onesr = area(k, 8192, 256)
    m = misc(k, 10, 30)

    def tensor(pe):
        out_tensor(pe)
        pe.wait_ge(h_ready, 2)
        for b in range(4):
            for j in range(4):
                kk, t = 2 * b + j // 2, j % 2
                last = pe.transpose(k.ps[:, 4 + b, j * P:(j + 1) * P], h[:, t, kk * P:(kk + 1) * P], k.ident)
            last.then_inc(hT_bank, 1)
        pe.wait_ge(router_loaded, 16)
        for kk in range(DK):
            pe.wait_ge(hT_put, DK + kk + 1)
            for t in range(ST):
                last = pe.matmul(k.ps[:, t, 0:NE], k.hT[:, kk, t * P:(t + 1) * P], wr[:, kk, :],
                                 start=(kk == 0), stop=(kk == DK - 1))
        last.then_inc(logits_done, 1)
        pe.wait_ge(aff_ready, 1)
        for t in range(ST):
            last = pe.transpose(k.ps[0:NE, 2, t * P:(t + 1) * P], aff[:, t, :], k.ident)
        last.then_inc(aff_turned, 1)
        pe.wait_ge(slots_ready, 1)
        for t in range(ST):
            last = pe.transpose(k.ps[:, 3, t * NE:(t + 1) * NE], count[0:NE, t * P:(t + 1) * P], k.ident[0:NE, 0:NE])
        last.then_inc(slots_turned, 1)
        pe.wait_ge(pick_ready, 2)
        for kk in range(DK):
            if kk >= 4:
                pe.wait_ge(xin_put, kk - 3)
            for t in range(ST):
                last = pe.matmul(k.ps[:, 4 + kk % 4, :], h[:, t, kk * P:(kk + 1) * P], pick[:, t, :],
                                 start=(t == 0), stop=(t == ST - 1))
            last.then_inc(xin_done, 1)
        pe.wait_ge(weight_ready, 2)
        for q in range(NG):
            for t in range(ST):
                last = pe.transpose(k.ps[:, q // 2, (q % 2) * S + t * P:(q % 2) * S + (t + 1) * P],
                                    pickw[:, t, q * P:(q + 1) * P], k.ident)
            if q % 2:
                last.then_inc(weight_turned, 1)

    def scalar(act):
        act.dma_start(wr, k.w_router[0].rearrange("(k p) e -> p k e", p=P)).then_inc(router_loaded, 16)
        act.wait_ge(ms_ready, 2)
        act.activation(m[:, 2:4], m[:, 2:4], ACT.Sqrt).then_inc(rt_root, 1)
        act.wait_ge(exp_arg, 1)
        for t in range(ST):
            act.activation(aff[:, t, :], logit[:, t, :], ACT.Exp, bias=m[:, 6 + t:7 + t],
                           accum_out=m[:, 8 + t:9 + t]).then_inc(aff_exp, 1)
        for kk in range(DK):
            act.wait_ge(xin_done, kk + 1)
            act.activation(k.xin[:, kk, :], k.ps[:, 4 + kk % 4, :], ACT.Copy,
                           scale=fix(k, "ffn_g")[:, kk:kk + 1]).then_inc(xin_put, 1)

    def vector(dve):
        step = k.vector_order.on(dve)
        for t in range(ST):
            for half in range(2):
                dve.wait_ge(out_done, 2 * t + half + 1)
                part = k.x[:, t, half * 512:(half + 1) * 512]
                step(dve.tensor_tensor(part, part, k.ps[:, 2 * t + half, :], ALU.add))
            step(dve.tensor_tensor_reduce(h[:, t, :], k.x[:, t, :], k.x[:, t, :], 1.0, 0.0, ALU.mult, ALU.add,
                                          m[:, t:t + 1]))
        dve.tensor_scalar(m[:, 2:4], m[:, 0:2], 1.0 / D, EPS, ALU.mult, ALU.add).then_inc(ms_ready, 1)
        dve.memset(onesr[0:NE, :], 1.0)
        dve.wait_ge(rt_root, 2)
        step(dve.reciprocal(m[:, 4:6], m[:, 2:4]))
        for t in range(ST):
            dve.tensor_scalar(h[:, t, :], k.x[:, t, :], m[:, 4 + t:5 + t], None, ALU.mult).then_inc(h_ready, 1)
        for kk in range(DK):
            dve.wait_ge(hT_bank, 4 + kk // 2 + 1)
            dve.tensor_scalar(k.hT[:, kk, :], k.ps[:, 4 + kk // 2, (kk % 2) * S:(kk % 2 + 1) * S],
                              fix(k, "ffn_g")[:, kk:kk + 1], None, ALU.mult).then_inc(hT_put, 1)
        dve.wait_ge(logits_done, 1)
        step(dve.tensor_copy(logit, k.ps[:, 0:ST, 0:NE]))
        step(dve.tensor_reduce(m[:, 6:8], logit, AX, ALU.max))
        dve.tensor_scalar(m[:, 6:8], m[:, 6:8], -1.0, None, ALU.mult).then_inc(exp_arg, 1)
        dve.wait_ge(aff_exp, 2)
        step(dve.reciprocal(m[:, 8:10], m[:, 8:10]))
        for t in range(ST):
            last = dve.tensor_scalar(aff[:, t, :], aff[:, t, :], m[:, 8 + t:9 + t], None, ALU.mult)
            if t < ST - 1:
                step(last)
        last.then_inc(aff_ready, 1)
        dve.wait_ge(aff_turned, 1)
        step(dve.tensor_copy(left[0:NE, :], k.ps[0:NE, 2, 0:S]))
        for r in range(CAP // 8):
            step(dve.max(top[0:NE, 8 * r:8 * r + 8], left[0:NE, :]))
            step(dve.match_replace(out=left[0:NE, :], in_to_replace=top[0:NE, 8 * r:8 * r + 8],
                                   in_values=left[0:NE, :], imm_value=-1.0))
        step(dve.tensor_scalar(left[0:NE, :], left[0:NE, :], 0.0, None, ALU.is_lt))
        step(dve.tensor_tensor_scan(count[0:NE, :], onesr[0:NE, :], left[0:NE, :], 0.0, ALU.mult, ALU.add))
        step(dve.tensor_tensor(count[0:NE, :], count[0:NE, :], left[0:NE, :], ALU.mult))
        dve.tensor_scalar(count[0:NE, :], count[0:NE, :], 1.0, None, ALU.subtract).then_inc(slots_ready, 1)
        dve.wait_ge(slots_turned, 1)
        step(dve.tensor_copy(slot_of, k.ps[:, 3, 0:ST * NE].rearrange("p (t e) -> p t e", t=ST)))
        for t in range(ST):
            dve.tensor_tensor(pick[:, t, :].rearrange("p (e c) -> p e c", e=NE),
                              slot_of[:, t, :].unsqueeze(2).to_broadcast([P, NE, CAP]),
                              fix(k, "slot_no").unsqueeze(1).to_broadcast([P, NE, CAP]),
                              ALU.is_equal).then_inc(pick_ready, 1)
        dve.wait_ge(pick_ready, 2)
        for t in range(ST):
            dve.tensor_tensor(pickw[:, t, :].rearrange("p (e c) -> p e c", e=NE),
                              pick[:, t, :].rearrange("p (e c) -> p e c", e=NE),
                              aff[:, t, :].unsqueeze(2).to_broadcast([P, NE, CAP]), ALU.mult).then_inc(weight_ready, 1)
        for q in range(NG):
            dve.wait_ge(weight_turned, q // 2 + 1)
            dve.tensor_copy(k.weightT[:, q, :], k.ps[:, q // 2, (q % 2) * S:(q % 2 + 1) * S])

    return Stage(tensor, scalar, vector)


def experts(k, base, w_gate, w_up, w_down, y_dram):
    nc = k.nc
    sem = k.sem
    x_ready, gate_up_done, silu_put, hidden_put = sem("ex_x_ready"), sem("gate_up_done"), sem("silu_put"), sem("hidden_put")
    turned, hidT_put, hidT_rest_put, down_done, y_put, y_stored = sem("ex_turned"), sem("hidT_put"), sem("hidT_rest_put"), sem("down_done"), sem("y_put"), sem("y_stored")
    xe = area(k, 6144, 256, k=DK)
    silu = area(k, 6400, FG)
    hidden = area(k, 6400 + FG, FG)
    hidT = area(k, 6400 + 2 * FG, (FT + 1) * P, m=FT + 1)
    y = area(k, 6400 + 2 * FG + (FT + 1) * P, 256)
    per = 3 * DK
    dmas = [1] * (2 * DK) + [1, 2] * NG
    mark = [k.use.landing(base + n, dmas[n]) for n in range(per)]
    again = [k.use.landing(base + per + n, dmas[n]) - mark[n] for n in range(per)]
    for e in range(2, NE):
        for n in range(per):
            k.use.landing(base + per * e + n, dmas[n])

    def load(sync):
        with sync.Fori(0, NE) as e:
            for n in range(per):
                s = slot(k, base + n)
                ready = k.slot_ready[(base + n) % SLOTS]
                sync.wait_ge(k.slot_freed, e * per + (base + n - SLOTS + 1))
                if n < 2 * DK:
                    w, kk = (w_gate, w_up)[n % 2], n // 2
                    sync.dma_start(s[:, 0:FF], w[0, bass.ds(e, 1), kk * P:(kk + 1) * P, :].rearrange("e p f -> p (e f)")).then_inc(ready, 16)
                else:
                    g, part = (n - 2 * DK) // 2, n % 2
                    rows = FG * g + 3 * P * part
                    whole = 3 - part
                    sync.dma_start(s[:, 0:whole * D].rearrange("p (m d) -> p m d", m=whole),
                                   w_down[0, bass.ds(e, 1), rows:rows + whole * P, :].rearrange("e (m p) d -> p (e m) d", p=P)).then_inc(ready, 16)
                    if part:
                        sync.dma_start(s[0:FR, 2 * D:3 * D],
                                       w_down[0, bass.ds(e, 1), rows + 2 * P:rows + 2 * P + FR, :].rearrange("e p d -> p (e d)")).then_inc(ready, 16)

    def gpsimd(pool):
        with pool.Fori(0, NE) as e:
            pool.wait_ge(gate_up_done, e + 1)
            pool.tensor_copy(xe, k.xin[:, :, bass.ds(e * CAP, CAP)]).then_inc(x_ready, 1)

    def tensor(pe):
        pe.sem_inc(gate_up_done, 1)
        with pe.Fori(0, NE) as e:
            pe.wait_ge(x_ready, e + 1)
            for kk in range(DK):
                for w in range(2):
                    n = 2 * kk + w
                    pe.wait_ge(k.slot_ready[(base + n) % SLOTS], e * again[n] + mark[n])
                    for half in range(2):
                        for g in range(NG):
                            last = pe.matmul(k.ps[32 * g:32 * g + CAP, 2 * w + half, 0:FH], xe[:, kk, :],
                                             slot(k, base + n)[:, g * FG + half * FH:g * FG + (half + 1) * FH],
                                             start=(kk == 0), stop=(kk == DK - 1))
                    if n < 2 * DK - 1:
                        last.then_inc(k.slot_freed, 1)
            last.then_inc(gate_up_done, 1)
            pe.wait_ge(hidden_put, e + 1)
            for m in range(FT + 1):
                w = P if m < FT else FR
                last = pe.transpose(k.ps[0:w, 4 + m // 4, (m % 4) * P:(m % 4 + 1) * P], hidden[:, m * P:m * P + w], k.ident)
                if m == 0:
                    last.then_inc(k.slot_freed, 1)
            last.then_inc(turned, 1)
            pe.wait_ge(hidT_put, e + 1)
            pe.wait_ge(hidT_rest_put, e + 1)
            pe.wait_ge(y_put, e + 1)
            for g in range(NG):
                for m in range(FT + 1):
                    n = 2 * DK + 2 * g + m // 3
                    if m % 3 == 0:
                        pe.wait_ge(k.slot_ready[(base + n) % SLOTS], e * again[n] + mark[n])
                    w = P if m < FT else FR
                    for j in range(NG):
                        last = pe.matmul(k.ps[32 * j:32 * j + CAP, 6, 0:256], hidT[0:w, m, 32 * g:32 * g + CAP],
                                         slot(k, base + n)[0:w, (m % 3) * D + j * 256:(m % 3) * D + (j + 1) * 256],
                                         start=(g == 0 and m == 0), stop=(g == NG - 1 and m == FT))
                    if m % 3 == 2 and not (g == NG - 1 and m == FT):
                        last.then_inc(k.slot_freed, 1)
            last.then_inc(down_done, 1)
            pe.drain().then_inc(k.slot_freed, 1)

    def scalar(act):
        act.sem_inc(y_put, 1)
        act.sem_inc(y_stored, 16)
        with act.Fori(0, NE) as e:
            act.wait_ge(gate_up_done, e + 2)
            for half in range(2):
                act.activation(silu[:, half * FH:(half + 1) * FH], k.ps[:, half, 0:FH], ACT.Silu).then_inc(silu_put, 1)
            act.wait_ge(turned, e + 1)
            act.activation(hidT[:, 0:4, :], k.ps[:, 4, :], ACT.Copy).then_inc(hidT_put, 1)
            act.wait_ge(down_done, e + 1)
            act.wait_ge(y_stored, e * (16 * NG) + 16)
            act.activation(y, k.ps[:, 6, 0:256], ACT.Copy).then_inc(y_put, 1)
            act.wait_ge(y_put, e + 2)
            for g in range(NG):
                act.dma_start(y_dram[bass.ds(e * CAP, CAP), g * 256:(g + 1) * 256], y[32 * g:32 * g + CAP, :]).then_inc(y_stored, 16)

    def vector(dve):
        with dve.Fori(0, NE) as e:
            for half in range(2):
                dve.wait_ge(silu_put, e * 2 + (half + 1))
                last = dve.tensor_tensor(hidden[:, half * FH:(half + 1) * FH], silu[:, half * FH:(half + 1) * FH],
                                         k.ps[:, 2 + half, 0:FH], ALU.mult)
            last.then_inc(hidden_put, 1)
            dve.wait_ge(turned, e + 1)
            dve.tensor_copy(hidT[:, 4, :], k.ps[:, 5, 0:P])
            dve.tensor_copy(hidT[0:FR, 5, :], k.ps[0:FR, 5, P:2 * P]).then_inc(hidT_rest_put, 1)
    k.y_stored = y_stored

    return load, Stage(tensor, scalar, vector, gpsimd)


def experts_combine(k, y_dram, final_norm_g):
    nc = k.nc
    sem = k.sem
    y_loaded, g_loaded, sum_done = sem("y_loaded"), sem("g_loaded"), sem("sum_done")
    ms_ready, root = sem("ms_ready"), sem("ms_root")
    Y = k.xin.rearrange("p k c -> p (k c)").rearrange("p (q d) -> p q d", q=NG)
    g = area(k, 6144, 1024)
    sq = area(k, 7168, 1024)
    m = misc(k, 10, 30)
    def tensor(pe):
        pe.wait_ge(y_loaded, 16)
        for t in range(ST):
            for half in range(2):
                for q in range(NG):
                    last = pe.matmul(k.ps[:, 2 * t + half, :], k.weightT[:, q, t * P:(t + 1) * P],
                                     Y[:, q, half * 512:(half + 1) * 512], start=(q == 0), stop=(q == NG - 1))
                last.then_inc(sum_done, 1)

    def scalar(act):
        act.dma_start(g, final_norm_g.partition_broadcast(P)).then_inc(g_loaded, 16)
        act.wait_ge(k.y_stored, 16 * NG * NE + 16)
        act.dma_start(Y, y_dram.rearrange("(q p) d -> p q d", p=P)).then_inc(y_loaded, 16)
        act.wait_ge(ms_ready, 3)
        act.activation(m[:, 2:4], m[:, 2:4], ACT.Sqrt).then_inc(root, 1)

    def vector(dve):
        step = k.vector_order.on(dve)
        for t in range(ST):
            for half in range(2):
                dve.wait_ge(sum_done, 2 * t + half + 1)
                part = k.x[:, t, half * 512:(half + 1) * 512]
                step(dve.tensor_tensor(part, part, k.ps[:, 2 * t + half, :], ALU.add))
            step(dve.tensor_tensor_reduce(sq, k.x[:, t, :], k.x[:, t, :], 1.0, 0.0, ALU.mult, ALU.add, m[:, t:t + 1]))
        dve.tensor_scalar(m[:, 2:4], m[:, 0:2], 1.0 / D, EPS, ALU.mult, ALU.add).then_inc(ms_ready, 1)
        dve.wait_ge(root, 3)
        step(dve.reciprocal(m[:, 4:6], m[:, 2:4]))
        dve.wait_ge(g_loaded, 16)
        for t in range(ST):
            step(dve.scalar_tensor_tensor(out=k.x[:, t, :], in0=k.x[:, t, :], scalar=m[:, 4 + t:5 + t], in1=g,
                                          op0=ALU.mult, op1=ALU.mult))

    return Stage(tensor, scalar, vector)


class NormAndTurn:

    GB = 8704

    def __init__(self, k, sums_done, sums_before, factor, gain, bias, rows_at=GB):
        sem = k.sem
        self.k, self.sums_done, self.sums_before, self.factor = k, sums_done, sums_before, factor
        self.u = k.norms
        k.norms += 1
        self.rows = (gain, bias)
        self.loaded, self.var_ready, self.root = sem("ln_rows_loaded"), sem("ln_var_ready"), sem("ln_root")
        self.ab_ready, self.normed, self.gained = sem("ln_ab_ready"), sem("ln_normed"), sem("ln_gained")
        self.turn = Turn(k)
        self.x_put = self.turn.x_put
        self.g, self.b = area(k, rows_at, 1024), area(k, rows_at + 1024, 1024)
        self.m = misc(k, 0, 36)

    def load_rows(self, act):
        for dst, row in zip((self.g, self.b), self.rows):
            act.dma_start(dst, row.partition_broadcast(P)).then_inc(self.loaded, 16)

    def of(self, t, a, w=1):
        return self.m[:, 18 * t + a:18 * t + a + w]

    def scalar(self, act):
        k = self.k
        for t in range(ST):
            act.wait_ge(self.var_ready, ST * self.u + t + 1)
            act.activation(self.of(t, 14), self.of(t, 14), ACT.Sqrt).then_inc(self.root, 1)
            act.wait_ge(self.ab_ready, ST * self.u + t + 1)
            for half in range(2):
                act.activation(k.x[:, t, half * 512:(half + 1) * 512], k.ps[:, 2 * t + half, :], ACT.Identity,
                               scale=self.of(t, 15), bias=self.of(t, 16)).then_inc(self.normed, 1)
        self.turn.scalar(act)

    def vector(self, dve):
        k = self.k
        step = k.vector_order.on(dve)
        dve.wait_ge(self.loaded, 32 * (self.u + 1))

        def statistics(t):
            for half in range(2):
                dve.wait_ge(self.sums_done, self.sums_before + 2 * t + half + 1)
                step(dve.bn_stats(self.of(t, 6 * half, 6), k.ps[:, 2 * t + half, :]))
            step(dve.bn_aggr(self.of(t, 12, 2), self.of(t, 0, 12)))
            dve.tensor_scalar(self.of(t, 14), self.of(t, 13), self.factor ** 2, LN_EPS, ALU.mult,
                              ALU.add).then_inc(self.var_ready, 1)

        def scale(t):
            dve.wait_ge(self.root, ST * self.u + t + 1)
            step(dve.reciprocal(self.of(t, 14), self.of(t, 14)))
            step(dve.tensor_scalar(self.of(t, 15), self.of(t, 14), self.factor, None, ALU.mult))
            dve.tensor_scalar(self.of(t, 16), self.of(t, 12), self.of(t, 15), -1.0, ALU.mult,
                              ALU.mult).then_inc(self.ab_ready, 1)

        def gain(t):
            for half in range(2):
                cols = slice(half * 512, (half + 1) * 512)
                dve.wait_ge(self.normed, 2 * ST * self.u + 2 * t + half + 1)
                dve.tensor_tensor(k.x[:, t, cols], k.x[:, t, cols], self.g[:, cols], ALU.mult).then_inc(self.gained, 1)

        statistics(0)
        scale(0)
        statistics(1)
        scale(1)
        gain(0)
        gain(1)
        self.turn.vector(dve)

    def gpsimd(self, pool):
        k = self.k
        for i in range(2 * ST):
            cols = slice((i % 2) * 512, (i % 2 + 1) * 512)
            pool.wait_ge(self.gained, 2 * ST * self.u + i + 1)
            pool.tensor_tensor(k.x[:, i // 2, cols], k.x[:, i // 2, cols], self.b[:, cols], ALU.add).then_inc(self.x_put, 1)

    def tensor(self, pe):
        self.turn.tensor(pe)


class Turn:

    def __init__(self, k, source="norm"):
        self.k, self.x_put, self.bank = k, k.sem(f"{source}_x_put"), k.sem("x_turned")
        self.u, self.of_source = k.turns, k.turns_of.get(source, 0)
        k.turns += 1
        k.turns_of[source] = self.of_source + 1

    def tensor(self, pe):
        k = self.k
        pe.wait_ge(self.x_put, 2 * ST * (self.of_source + 1))
        for b in range(4):
            for j in range(4):
                kk, t = 2 * b + j // 2, j % 2
                last = pe.transpose(k.ps[:, 4 + b, j * P:(j + 1) * P], k.x[:, t, kk * P:(kk + 1) * P], k.ident)
            last.then_inc(self.bank, 1)

    def copy(self, engine, write, banks):
        k = self.k
        for b in banks:
            engine.wait_ge(self.bank, 4 * self.u + b + 1)
            write(k.hT[:, 2 * b:2 * b + 2, :], k.ps[:, 4 + b, :].rearrange("p (k s) -> p k s", k=2))

    def scalar(self, act):
        self.copy(act, lambda out, src: act.activation(out, src, ACT.Copy), (1, 3))

    def vector(self, dve):
        self.copy(dve, lambda out, src: dve.tensor_copy(out, src), (0, 2))


FC = FF // P


def ffn_weights(k, base, w):
    loads = []
    for c in range(FC):
        k.use.landing(base + c)
        loads.append((base + c, [(slot(k, base + c), w[c])]))
    return loads


def ffn(k, u, base, gain, bias):
    sem = k.sem
    (h_high, h_split, w13_high, w2_high, w13_split, w2_split, pair_done, silu_put, hidden_put,
     hidden_high, hidden_split, sums_done) = (
        sem(f"ffn_{s}") for s in ("h_high", "h_split", "w13_high", "w2_high", "w13_split", "w2_split", "pair_done", "silu_put", "hidden_put", "hidden_high", "hidden_split",
                                  "sums_done"))
    norm = NormAndTurn(k, sums_done, 2 * ST * u, 0.5, gain, bias, rows_at=1024)
    silu = area(k, 0, 2 * S, n=2)
    hidden = area(k, 2 * S, 2 * S, n=2)
    assert R0 + 3072 <= ARENA - PARTS
    before = FC * u
    TURNS = FC // SLOTS

    def landed(c, e):
        return e * 16 + k.use.mark[base + c]

    def raw(c, w):
        return slot(k, base + c)[:, w * D:(w + 1) * D].rearrange("p (k f) -> p k f", k=DK)

    def tensor(pe):
        for t in range(ST):
            for half in range(2):
                pe.matmul(k.ps[:, 2 * t + half, :], fix(k, "seed2"), k.x[:, t, half * 512:(half + 1) * 512],
                          start=True, stop=False, skip_group_check=True)

        def pair(c, e=0):
            b = c % 2
            for w in range(2):
                pe.wait_ge(w13_split, e * (2 * SLOTS) + (2 * (before + c) + w + 1))
                for kk in range(DK):
                    if c == 0 and w == 0:
                        pe.wait_ge(h_split, DK * u + kk + 1)
                    for n, (i, j) in enumerate(((0, 0), (0, 1), (1, 0))):
                        last = pe.matmul(k.ps[:, 4 + c % 4, w * S:(w + 1) * S], k.w13[:, b, w, i, kk, :],
                                         k.hsplit[:, j, kk, :], start=(kk == 0 and n == 0), stop=(kk == DK - 1 and n == 2))
            last.then_inc(pair_done, 1)

        def down(c, e=0):
            b = c % 2
            pe.wait_ge(w2_split, e * SLOTS + (before + c + 1))
            pe.wait_ge(hidden_split, e * SLOTS + (before + c + 1))
            for t in range(ST):
                for i, j in ((0, 0), (0, 1), (1, 0)):
                    for half in range(2):
                        last = pe.matmul(k.ps[:, 2 * t + half, :], k.hidsplit[:, b, i, t * P:(t + 1) * P],
                                         k.w2[:, b, j, half * 512:(half + 1) * 512], start=False, stop=False,
                                         skip_group_check=True)
            last.then_inc(k.slot_freed, 1)

        pair(0)
        with pe.Fori(0, TURNS) as e:
            for c in range(SLOTS):
                pair(c + 1, e)
                down(c, e)
        for c in range(TURNS * SLOTS, FC):
            if c + 1 < FC:
                pair(c + 1)
            down(c)
        pe.drain().then_inc(sums_done, 4)
        norm.tensor(pe)

    def scalar(act):
        def pair_high(c, w, e=0):
            if w == 0:
                act.wait_ge(k.slot_ready[(base + c) % SLOTS], landed(c, e))
            act.activation(k.w13[:, c % 2, w, 0], raw(c, w), ACT.Copy).then_inc(w13_high, 1)

        def down_high(c, e=0):
            if c:
                act.wait_ge(k.slot_freed, e * SLOTS + (base + c - 1))
            act.activation(k.w2[:, c % 2, 0], slot(k, base + c)[:, 2 * D:3 * D], ACT.Copy).then_inc(w2_high, 1)

        def chunk(c, e=0):
            act.wait_ge(pair_done, e * SLOTS + (before + c + 1))
            act.activation(silu[:, c % 2, :], k.ps[:, 4 + c % 4, 0:S], ACT.Silu).then_inc(silu_put, 1)
            if c + 2 < FC:
                pair_high(c + 2, 0, e)
            act.wait_ge(hidden_put, e * SLOTS + (before + c + 1))
            act.activation(k.hidsplit[:, c % 2, 0], hidden[:, c % 2, :], ACT.Copy).then_inc(hidden_high, 1)
            if c + 2 < FC:
                pair_high(c + 2, 1, e)
            if c + 1 < FC:
                down_high(c + 1, e)

        for kk in range(DK):
            act.activation(k.hsplit[:, 0, kk, :], k.hT[:, kk, :], ACT.Copy).then_inc(h_high, 1)
            if kk == 0:
                pair_high(0, 0)
                pair_high(0, 1)
        down_high(0)
        pair_high(1, 0)
        pair_high(1, 1)
        norm.load_rows(act)
        with act.Fori(0, TURNS) as e:
            for c in range(SLOTS):
                chunk(c, e)
        for c in range(TURNS * SLOTS, FC):
            chunk(c)
        norm.scalar(act)

    def vector(dve):
        def pair_low(c, w, e=0):
            dve.wait_ge(w13_high, e * (2 * SLOTS) + (2 * (before + c) + w + 1))
            dve.tensor_tensor(k.w13[:, c % 2, w, 1], raw(c, w), k.w13[:, c % 2, w, 0].bitcast(F32),
                              ALU.subtract).then_inc(w13_split, 1)

        def down_low(c, e=0):
            dve.wait_ge(w2_high, e * SLOTS + (before + c + 1))
            dve.tensor_tensor(k.w2[:, c % 2, 1], slot(k, base + c)[:, 2 * D:3 * D], k.w2[:, c % 2, 0].bitcast(F32),
                              ALU.subtract).then_inc(w2_split, 1)

        def chunk(c, e=0):
            dve.wait_ge(silu_put, e * SLOTS + (before + c + 1))
            dve.tensor_tensor(hidden[:, c % 2, :], silu[:, c % 2, :], k.ps[:, 4 + c % 4, S:2 * S],
                              ALU.mult).then_inc(hidden_put, 1)
            if c + 2 < FC:
                pair_low(c + 2, 0, e)
            dve.wait_ge(hidden_high, e * SLOTS + (before + c + 1))
            dve.tensor_tensor(k.hidsplit[:, c % 2, 1], hidden[:, c % 2, :], k.hidsplit[:, c % 2, 0].bitcast(F32),
                              ALU.subtract).then_inc(hidden_split, 1)
            if c + 2 < FC:
                pair_low(c + 2, 1, e)
            if c + 1 < FC:
                down_low(c + 1, e)

        for kk in range(DK):
            dve.wait_ge(h_high, DK * u + kk + 1)
            dve.tensor_tensor(k.hsplit[:, 1, kk, :], k.hT[:, kk, :], k.hsplit[:, 0, kk, :].bitcast(F32),
                              ALU.subtract).then_inc(h_split, 1)
            if kk == 0:
                pair_low(0, 0)
                pair_low(0, 1)
        down_low(0)
        pair_low(1, 0)
        pair_low(1, 1)
        with dve.Fori(0, TURNS) as e:
            for c in range(SLOTS):
                chunk(c, e)
        for c in range(TURNS * SLOTS, FC):
            chunk(c)
        norm.vector(dve)

    return Stage(tensor, scalar, vector, norm.gpsimd)


def conv_s5(k, base, s5_params, gain, bias):
    sem = k.sem
    n_glu, n_out = base + 8, base + 9
    names = ("gate_put", "param_loaded", "exp1", "exp_arg", "mag_put", "bc_ready", "bc_turned", "bc_put", "input_done", "v_parts", "v_put", "w_put", "s_put", "y_done",
             "gelu_arg", "z_put", "glu_done", "sig_put", "yb_put")
    q = {s: sem(f"s5_{s}") for s in names}
    B = {"column_done": 22, "copied": 8, "sin_arg": 2, "sin_done": 2}
    q.update({s: sem(s) for s in B})
    mixT = area(k, 0, 2048, c=DK)
    u = area(k, 2048, 1024, q=4)
    z = area(k, 3072, 1024, q=4)
    par = area(k, 4096, 1072)
    re_im = par[:, 0:48].rearrange("p (n i) -> p n i", n=3)
    b_in = par[:, 48:560].rearrange("p (n i c) -> p n i c", n=2, i=16)
    c_in = par[:, 560:1072].rearrange("p (n q s) -> p n q s", n=2, q=4)
    bT = area(k, 5168, 1024, n=2, q=4)
    cT = area(k, 6192, 1024, n=2, q=4)
    small = area(k, 7216, 16 * 16, n=16)
    wide = area(k, 7472, 1024)
    cosT, sinT = work(k, 0, 4096, i=16), work(k, 4096, 4096, i=16)
    m1, m2 = work(k, 8192, 1024), work(k, 9216, 1024)
    prod = work(k, 8192, 2048, n=4, i=2)
    w = work(k, 10240, 1024, n=2, i=2)
    s = work(k, 11264, 1024, n=2, i=2)
    conv_w = fix(k, "conv_w2")
    ORDER = [c for j in range(4) for c in (j, 8 + j, 4 + j)] + [12, 13, 14, 15]

    def tensor(pe):
        for n in range(base, base + 8):
            pe.wait_ge(k.slot_ready[n % SLOTS], k.use.mark[n])
        for i, c in enumerate(ORDER):
            if i >= 6:
                pe.wait_ge(q["copied"], B["copied"] + i - 5)
            for kk in range(DK):
                last = pe.matmul(k.ps[:, i % 6, 0:S], slot(k, base + kk)[:, c * P:(c + 1) * P], k.hT[:, kk, :],
                                 start=(kk == 0), stop=(kk == DK - 1))
            last.then_inc(q["column_done"], 1)
        pe.drain().then_inc(k.slot_freed, 8)
        for n in range(4):
            pe.wait_ge(q["bc_ready"], n + 1)
            if n:
                pe.wait_ge(q["bc_put"], n)
            for j in range(4):
                last = pe.transpose(k.ps[:, 6, j * P:(j + 1) * P], wide[:, 0:512][:, j * P:(j + 1) * P] if n % 2 == 0
                                    else wide[:, 512:1024][:, j * P:(j + 1) * P], k.ident)
            last.then_inc(q["bc_turned"], 1)
        pe.wait_ge(q["bc_put"], 4)
        pe.wait_ge(q["copied"], B["copied"] + 16)

        def states(j):
            for i in range(2):
                tile = 2 * j + i
                r = 32 * (tile % 4)
                for n in range(2):
                    last = pe.matmul(k.ps[:, 2 * (j % 2) + i, n * S:(n + 1) * S], bT[r:r + 32, n, tile // 4, :],
                                     u[r:r + 32, tile // 4, :], start=True, stop=True)
            last.then_inc(q["input_done"], 1)

        def outputs(j):
            pe.wait_ge(q["s_put"], 2 * (j + 1))
            for i in range(2):
                tile = 2 * j + i
                r = 32 * (tile % 4)
                for n in range(2):
                    last = pe.matmul(k.ps[r:r + 32, 4 + tile // 4, 0:S], cT[:, n, tile // 4, r:r + 32], s[:, n, i, :],
                                     start=(n == 0), stop=(n == 1))
            last.then_inc(q["y_done"], 1)

        for j in range(8):
            if j >= 2:
                pe.wait_ge(q["v_parts"], 4 * (j - 1))
            states(j)
            if j:
                outputs(j - 1)
        outputs(7)
        pe.wait_ge(k.slot_ready[n_glu % SLOTS], k.use.mark[n_glu])
        pe.wait_ge(q["z_put"], 4)
        for c in range(4):
            for kk in range(4):
                last = pe.matmul(k.ps[:, c, 0:S], slot(k, n_glu)[:, kk * CC + c * P:kk * CC + (c + 1) * P], z[:, kk, :],
                                 start=(kk == 0), stop=(kk == 3))
            last.then_inc(q["glu_done"], 1)
        pe.drain().then_inc(k.slot_freed, 1)
        pe.wait_ge(q["yb_put"], 4)
        out_tensor(pe)
        norm.tensor(pe)

    out_done, out_tensor = mixer_out(k, n_out, mixT, fix(k, "seed1"))
    norm = NormAndTurn(k, out_done, 2 * ST, 1.0, gain, bias)

    def scalar(act):
        act.dma_start(par, s5_params).then_inc(q["param_loaded"], 16)
        norm.load_rows(act)
        act.wait_ge(q["param_loaded"], 16)
        act.activation(re_im[:, 2, :], re_im[:, 2, :], ACT.Exp).then_inc(q["exp1"], 1)
        act.wait_ge(q["exp_arg"], 1)
        act.activation(small[:, 2, :], small[:, 2, :], ACT.Exp).then_inc(q["mag_put"], 1)
        act.wait_ge(q["sin_arg"], B["sin_arg"] + 1)
        act.activation(small[:, 4, :], small[:, 4, :], ACT.Sin).then_inc(q["sin_done"], 1)
        act.activation(small[:, 5, :], small[:, 5, :], ACT.Sin).then_inc(q["sin_done"], 1)
        for i, c in enumerate(ORDER):
            act.wait_ge(q["column_done"], B["column_done"] + i + 1)
            if c >= 12:
                act.activation(u[:, c - 12, :], k.ps[:, i % 6, 0:S], ACT.Copy).then_inc(q["copied"], 1)
            else:
                if i >= 3:
                    act.wait_ge(q["gate_put"], i // 3)
                act.activation(z[:, i % 3, :], k.ps[:, i % 6, 0:S], ACT.Copy).then_inc(q["copied"], 1)
        for n in range(4):
            act.wait_ge(q["bc_turned"], n + 1)
            act.activation((bT if n < 2 else cT)[:, n % 2], k.ps[:, 6, :].rearrange("p (q c) -> p q c", q=4),
                           ACT.Copy).then_inc(q["bc_put"], 1)
        for c in range(4):
            act.wait_ge(q["gelu_arg"], c + 1)
            act.activation(z[:, c, :], z[:, c, :], ACT.Gelu_apprx_tanh).then_inc(q["z_put"], 1)
        for c in range(4):
            act.wait_ge(q["glu_done"], c + 1)
            act.activation(u[:, c, :], k.ps[:, c, 0:S], ACT.Sigmoid, bias=fix(k, "b_glu")[:, c:c + 1]).then_inc(q["sig_put"], 1)
        norm.scalar(act)

    def vector(dve):
        step = k.vector_order.on(dve)

        def sm(i):
            return small[:, i, :]

        lr, li, dt = re_im[:, 0, :], re_im[:, 1, :], re_im[:, 2, :]
        dve.wait_ge(q["param_loaded"], 16)
        step(dve.tensor_scalar(lr, lr, -1e-4, None, ALU.min))
        dve.wait_ge(q["exp1"], 1)
        dve.tensor_tensor(sm(2), lr, dt, ALU.mult).then_inc(q["exp_arg"], 1)
        step(dve.tensor_tensor(sm(3), li, dt, ALU.mult))
        step(range_reduce(step, dve, sm(4), sm(3), sm(5)))
        step(dve.scalar_tensor_tensor(out=sm(5), in0=sm(4), scalar=-1.0, in1=sm(4), op0=ALU.mult, op1=ALU.max))
        dve.tensor_scalar(sm(5), sm(5), -1.0, math.pi / 2, ALU.mult, ALU.add).then_inc(q["sin_arg"], 1)
        step(dve.tensor_tensor(sm(6), lr, lr, ALU.mult))
        step(dve.tensor_tensor(sm(7), li, li, ALU.mult))
        step(dve.tensor_tensor(sm(6), sm(6), sm(7), ALU.add))
        step(dve.reciprocal(sm(6), sm(6)))
        dve.wait_ge(q["mag_put"], 1)
        dve.wait_ge(q["sin_done"], B["sin_done"] + 2)
        step(dve.tensor_tensor(sm(7), sm(2), sm(5), ALU.mult))
        step(dve.tensor_scalar(sm(7), sm(7), 1.0, None, ALU.subtract))
        step(dve.tensor_tensor(sm(8), sm(2), sm(4), ALU.mult))
        step(dve.tensor_tensor(sm(9), sm(7), lr, ALU.mult))
        step(dve.tensor_tensor(sm(10), sm(8), li, ALU.mult))
        step(dve.tensor_tensor(sm(9), sm(9), sm(10), ALU.add))
        step(dve.tensor_tensor(sm(9), sm(9), sm(6), ALU.mult))
        step(dve.tensor_tensor(sm(10), sm(8), lr, ALU.mult))
        step(dve.tensor_tensor(sm(11), sm(7), li, ALU.mult))
        step(dve.tensor_tensor(sm(10), sm(10), sm(11), ALU.subtract))
        step(dve.tensor_tensor(sm(10), sm(10), sm(6), ALU.mult))

        fre, fim = (sm(i).unsqueeze(2).to_broadcast([P, 16, S5C]) for i in (9, 10))
        t1 = wide[:, 0:256].rearrange("p (i c) -> p i c", i=16)
        t2 = wide[:, 256:512].rearrange("p (i c) -> p i c", i=16)
        t3 = z[:, 3, :].rearrange("p (i c) -> p i c", i=16)
        t4 = mixT[:, 7, :].rearrange("p (i c) -> p i c", i=16)
        step(dve.tensor_tensor(t1, b_in[:, 0], fre, ALU.mult))
        step(dve.tensor_tensor(t2, b_in[:, 1], fim, ALU.mult))
        step(dve.tensor_tensor(t3, t1, t2, ALU.subtract))
        step(dve.tensor_tensor(t1, b_in[:, 1], fre, ALU.mult))
        step(dve.tensor_tensor(t2, b_in[:, 0], fim, ALU.mult))
        step(dve.tensor_tensor(t4, t1, t2, ALU.add))
        mb, mc = fix(k, "mask_b"), fix(k, "mask_c")
        for n, src in enumerate((t3, t4)):
            out = wide[:, 512 * n:512 * n + 512].rearrange("p (i g c) -> p i g c", i=16, g=2)
            for g in range(2):
                last = dve.tensor_scalar(out[:, :, g, :], src, mb[:, g:g + 1], None, ALU.mult)
                if g == 0:
                    step(last)
            last.then_inc(q["bc_ready"], 1)

        def c_part(n):
            dve.wait_ge(q["bc_turned"], n + 1)
            out = wide[:, 512 * n:512 * n + 512].rearrange("p (q g s) -> p q g s", q=4, g=2)
            for g in range(2):
                last = dve.tensor_scalar(out[:, :, g, :], c_in[:, n], mc[:, g:g + 1], -1.0 if n else 1.0, ALU.mult, ALU.mult)
                if g == 0:
                    step(last)
            last.then_inc(q["bc_ready"], 1)

        def gate(j):
            dve.wait_ge(q["copied"], B["copied"] + 3 * j + 3)
            h, gc, gb, y = z[:, 0, :], z[:, 1, :], z[:, 2, :], mixT[:, j, :]
            step(dve.tensor_tensor(h, h, gc, ALU.mult))
            step(dve.tensor_scalar(y, h, conv_w[:, 8 + j:9 + j], None, ALU.mult))
            step(dve.scalar_tensor_tensor(out=y[:, 1:S], in0=h[:, 0:S - 1], scalar=conv_w[:, 4 + j:5 + j], in1=y[:, 1:S],
                                          op0=ALU.mult, op1=ALU.add))
            step(dve.scalar_tensor_tensor(out=y[:, 2:S], in0=h[:, 0:S - 2], scalar=conv_w[:, j:j + 1], in1=y[:, 2:S],
                                          op0=ALU.mult, op1=ALU.add))
            dve.tensor_tensor(y, y, gb, ALU.mult).then_inc(q["gate_put"], 1)

        step(dve.memset(cosT[:, :, 0:1], 1.0))
        step(dve.memset(sinT[:, :, 0:1], 0.0))
        step(dve.tensor_copy(sm(12), sm(5)))
        step(dve.tensor_copy(sm(13), sm(4)))
        n = 1
        while n < S:
            pr, pi = (sm(i).unsqueeze(2).to_broadcast([P, 16, n]) for i in (12, 13))
            for h in range(0, 16, 16 if n <= 64 else 8):
                hh = slice(h, h + (16 if n <= 64 else 8))
                size = (16 if n <= 64 else 8) * n
                a1 = m1[:, 0:size].rearrange("p (i t) -> p i t", t=n)
                a2 = m2[:, 0:size].rearrange("p (i t) -> p i t", t=n)
                step(dve.tensor_tensor(a1, cosT[:, hh, 0:n], pr[:, hh], ALU.mult))
                step(dve.tensor_tensor(a2, sinT[:, hh, 0:n], pi[:, hh], ALU.mult))
                step(dve.tensor_tensor(cosT[:, hh, n:2 * n], a1, a2, ALU.subtract))
                step(dve.tensor_tensor(a1, cosT[:, hh, 0:n], pi[:, hh], ALU.mult))
                step(dve.tensor_tensor(a2, sinT[:, hh, 0:n], pr[:, hh], ALU.mult))
                step(dve.tensor_tensor(sinT[:, hh, n:2 * n], a1, a2, ALU.add))
            if n in (16, 64):
                gate((16, 64).index(n))
            n *= 2
            if n < S:
                step(dve.tensor_tensor(sm(14), sm(12), sm(12), ALU.mult))
                step(dve.tensor_tensor(sm(15), sm(13), sm(13), ALU.mult))
                step(dve.scalar_tensor_tensor(out=sm(13), in0=sm(12), scalar=2.0, in1=sm(13), op0=ALU.mult, op1=ALU.mult))
                step(dve.tensor_tensor(sm(12), sm(14), sm(15), ALU.subtract))

        gate(2)
        gate(3)
        c_part(0)
        c_part(1)

        for j in range(8):
            both = slice(2 * j, 2 * j + 2)
            c, sn = cosT[:, both, :], sinT[:, both, :]
            dve.wait_ge(q["input_done"], j + 1)
            if j:
                dve.wait_ge(q["v_put"], 2 * j)
                dve.wait_ge(q["s_put"], 2 * j)
            bre, bim = (k.ps[:, 2 * (j % 2):2 * (j % 2) + 2, n * S:(n + 1) * S] for n in range(2))
            for n, (a, b) in enumerate(((bre, c), (bim, sn), (bim, c), (bre, sn))):
                dve.tensor_tensor(prod[:, n], a, b, ALU.mult).then_inc(q["v_parts"], 1)
            for n in range(2):
                dve.wait_ge(q["v_put"], 2 * j + n + 1)
                for i in range(2):
                    tile = 2 * j + i
                    dve.tensor_tensor_scan(w[:, n, i, :], small[:, 2, tile:tile + 1].to_broadcast([P, S]), s[:, n, i, :],
                                           0.0, ALU.mult, ALU.add).then_inc(q["w_put"], 1)
        for c in range(4):
            dve.wait_ge(q["y_done"], 2 * (c + 1))
            dve.scalar_tensor_tensor(out=z[:, c, :], in0=u[:, c, :], scalar=fix(k, "s5_d")[:, c:c + 1],
                                     in1=k.ps[:, 4 + c, 0:S], op0=ALU.mult, op1=ALU.add).then_inc(q["gelu_arg"], 1)
        for c in range(4):
            dve.wait_ge(q["sig_put"], c + 1)
            dve.tensor_tensor(mixT[:, 4 + c, :], z[:, c, :], u[:, c, :], ALU.mult).then_inc(q["yb_put"], 1)
        norm.vector(dve)

    def gpsimd(pool):
        step = k.pool_order.on(pool)
        for j in range(8):
            both = slice(2 * j, 2 * j + 2)
            c, sn = cosT[:, both, :], sinT[:, both, :]
            pool.wait_ge(q["v_parts"], 4 * j + 4)
            if j:
                pool.wait_ge(q["y_done"], j)
            pool.tensor_tensor(s[:, 0], prod[:, 0], prod[:, 1], ALU.add).then_inc(q["v_put"], 1)
            pool.tensor_tensor(s[:, 1], prod[:, 2], prod[:, 3], ALU.subtract).then_inc(q["v_put"], 1)
            pool.wait_ge(q["w_put"], 4 * j + 4)
            step(pool.tensor_tensor(prod[:, 0], w[:, 0], c, ALU.mult))
            step(pool.tensor_tensor(prod[:, 1], w[:, 1], sn, ALU.mult))
            step(pool.tensor_tensor(prod[:, 2], w[:, 0], sn, ALU.mult))
            step(pool.tensor_tensor(prod[:, 3], w[:, 1], c, ALU.mult))
            pool.tensor_tensor(s[:, 0], prod[:, 0], prod[:, 1], ALU.subtract).then_inc(q["s_put"], 1)
            pool.tensor_tensor(s[:, 1], prod[:, 2], prod[:, 3], ALU.add).then_inc(q["s_put"], 1)
        norm.gpsimd(pool)

    return Stage(tensor, scalar, vector, gpsimd)


def ple(k, u, base, pT, out=None):
    sem = k.sem
    p_loaded, proj_done, gate_done, sig_put, part_put, x_put, stored = (
        sem(f"ple_{s}") for s in ("p_loaded", "proj_done", "gate_done", "sig_put", "part_put", "x_put", "stored"))
    turn = Turn(k, "ple")
    before = 2 * ST * u
    p_sb = area(k, 0, 512, k=2)
    sig = area(k, 1024, 2048, n=4)
    n_proj = base + 3

    def tensor(pe):
        for n in range(base, base + 3):
            pe.wait_ge(k.slot_ready[n % SLOTS], k.use.mark[n])
        for t in range(ST):
            for half in range(2):
                for kk in range(DK):
                    w = slot(k, base + kk // 3)[:, (kk % 3) * D + half * 512:(kk % 3) * D + (half + 1) * 512]
                    last = pe.matmul(k.ps[:, 2 * t + half, :], k.hT[:, kk, t * P:(t + 1) * P], w,
                                     start=(kk == 0), stop=(kk == DK - 1))
                last.then_inc(gate_done, 1)
        pe.drain().then_inc(k.slot_freed, 3)
        pe.wait_ge(k.slot_ready[n_proj % SLOTS], k.use.mark[n_proj])
        pe.wait_ge(p_loaded, 16 * (u + 1))
        for t in range(ST):
            for half in range(2):
                for kk in range(PLE // P):
                    last = pe.matmul(k.ps[:, 4 + 2 * t + half, :], p_sb[:, kk, t * P:(t + 1) * P],
                                     slot(k, n_proj)[:, kk * D + half * 512:kk * D + (half + 1) * 512],
                                     start=(kk == 0), stop=(kk == PLE // P - 1))
                last.then_inc(proj_done, 1)
        pe.drain().then_inc(k.slot_freed, 1)
        if out is None:
            turn.tensor(pe)

    def scalar(act):
        act.dma_start(p_sb, pT).then_inc(p_loaded, 16)
        for i in range(4):
            act.wait_ge(gate_done, before + i + 1)
            act.activation(sig[:, i, :], k.ps[:, i, :], ACT.Sigmoid).then_inc(sig_put, 1)
        if out is None:
            turn.scalar(act)
        else:
            for t in range(ST):
                act.wait_ge(x_put, before + 2 * t + 2)
                act.dma_start(out[0, t * P:(t + 1) * P, :], k.x[:, t, :]).then_inc(stored, 16)
            act.wait_ge(stored, 16 * ST)

    def vector(dve):
        for i in range(4):
            part = k.x[:, i // 2, (i % 2) * 512:(i % 2 + 1) * 512]
            dve.wait_ge(sig_put, before + i + 1)
            dve.wait_ge(proj_done, before + i + 1)
            dve.tensor_tensor(sig[:, i, :], sig[:, i, :], k.ps[:, 4 + i, :], ALU.mult).then_inc(part_put, 1)
            dve.wait_ge(part_put, before + i + 1)
            dve.tensor_tensor(part, part, sig[:, i, :], ALU.add).then_inc(x_put, 1)
        if out is None:
            turn.vector(dve)

    return Stage(tensor, scalar, vector)


def turn_only(k):
    turn = Turn(k, "first_block")

    def vector(dve):
        dve.drain().then_inc(turn.x_put, 2 * ST)
        turn.vector(dve)

    return Stage(turn.tensor, turn.scalar, vector)


def sparse_attention(k, base, causal, positions, gain, bias):
    sem = k.sem
    n_out = base + DK
    names = ("loaded", "rope_done", "turned",
             "turned_act", "turned_dve", "index_done", "relu_put", "relu_used")
    q = {s: sem(f"dsa_{s}") for s in names}
    B = {"column_done": 38, "copied": 24, "sin_arg": 3, "sin_done": 4, "score_done": 2 * HEADS, "score_read": 2 * HEADS, "score_put": HEADS, "exp_done": 4 * HEADS, "p_put": ST * HEADS,
         "p_turned": HEADS, "pT_put": HEADS, "o_done": HEADS, "o_put": HEADS}
    q.update({s: sem(s) for s in B})
    out_done, out_tensor = mixer_out(k, n_out, k.hT, fix(k, "seed1"))
    norm = NormAndTurn(k, out_done, 4 * ST, 1.0, gain, bias)
    HH = QH + KVH
    WIDE, W = HH * HD, IH * ID
    ROW = WIDE + W + ID
    NPR = ST * ROW
    pr = area(k, 0, NPR, t=ST)
    qT = area(k, NPR, QH * S, h=QH)
    kT = area(k, NPR + 2048, KVH * S, h=KVH)
    qiT = area(k, NPR + 2560, 4 * S, h=4)
    kiT = area(k, NPR + 3584, S)
    v = area(k, NPR + 3840, ST * KVH * HD, t=ST)
    wi = area(k, NPR + 4352, ST * IH, t=ST)
    ki2 = area(k, NPR + 4368, ST * 2 * ID, t=ST)
    assert NPR + 4624 <= NormAndTurn.GB
    score = area(k, 0, 512, t=ST)
    left = area(k, 512, 512, t=ST)
    relu = area(k, 1024, 1024, n=4)
    keep = area(k, 2048, 512, t=ST)
    s = area(k, 2560, 1024, b=2, t=ST)
    pT = area(k, 1024, 1024, b=2, c=ST)

    causal_sb = work(k, 0, 512, t=ST)
    pos_i = work(k, 512, ST).bitcast(I32)
    pos = work(k, 514, ST)
    ang, arg, rev = work(k, 520, 48, t=ST), work(k, 568, 96, n=2, t=ST), work(k, 664, 48, t=ST)
    trig = work(k, 712, 96, n=2, t=ST)
    tmp = [work(k, 1024 + 320 * i, 320) for i in range(4)]
    m = misc(k, 0, 40)
    scale = HD ** -0.5
    NOT = -1e30
    TAKEN = -2e30
    CHUNKS = [(0, 512), (512, 1024), (1024, 1536), (1536, 2048), (2048, C_IN)]
    BLOCKS = ([(qT[:, h, :], h * HD) for h in range(QH)] + [(kT[:, h, :], (QH + h) * HD) for h in range(KVH)]
              + [(qiT[:, h, :], WIDE + h * P) for h in range(4)] + [(kiT, None)])

    def tensor(pe):
        for n in range(base, base + DK):
            pe.wait_ge(k.slot_ready[n % SLOTS], k.use.mark[n])
        for i in range(ST * len(CHUNKS)):
            t, (c0, c1) = i // len(CHUNKS), CHUNKS[i % len(CHUNKS)]
            if i >= 8:
                pe.wait_ge(q["copied"], B["copied"] + i - 7)
            for kk in range(DK):
                last = pe.matmul(k.ps[:, i % 8, 0:c1 - c0], k.hT[:, kk, t * P:(t + 1) * P], slot(k, base + kk)[:, c0:c1],
                                 start=(kk == 0), stop=(kk == DK - 1))
            last.then_inc(q["column_done"], 1)
        pe.drain().then_inc(k.slot_freed, DK)
        pe.wait_ge(q["rope_done"], 1)
        pe.wait_ge(q["copied"], B["copied"] + ST * len(CHUNKS))
        for i, (_, at) in enumerate(BLOCKS):
            for t in range(ST):
                src = ki2[:, t, :] if at is None else pr[:, t, at:at + P]
                last = pe.transpose(k.ps[:, i // 2, (i % 2) * S + t * P:(i % 2) * S + (t + 1) * P], src, k.ident)
            if i % 2 or i == len(BLOCKS) - 1:
                last.then_inc(q["turned"], 1)
        pe.wait_ge(q["turned_act"], 4)
        pe.wait_ge(q["turned_dve"], 4)
        for i in range(ST * IH):
            t, h = i // IH, i % IH
            if i >= 8:
                pe.wait_ge(q["relu_put"], i - 7)
            r = ID * (h % 2)
            pe.matmul(k.ps[:, i % 8, 0:P * (t + 1)], qiT[r:r + ID, h // 2, t * P:(t + 1) * P], kiT[r:r + ID, 0:P * (t + 1)],
                      start=True, stop=True).then_inc(q["index_done"], 1)
        pe.wait_ge(q["relu_put"], ST * IH)
        for h in range(QH + 1):
            if h < QH:
                if h >= 2:
                    pe.wait_ge(q["score_read"], B["score_read"] + h - 1)
                for t in range(ST):
                    last = pe.matmul(k.ps[:, h % 2, t * S:(t + 1) * S], qT[:, h, t * P:(t + 1) * P],
                                     kT[:, h // (QH // KVH), :], start=True, stop=True)
                last.then_inc(q["score_done"], 1)
            if h:
                g = h - 1
                pe.wait_ge(q["p_put"], B["p_put"] + ST * (g + 1))
                if g >= 2:
                    pe.wait_ge(q["pT_put"], B["pT_put"] + g - 1)
                for t in range(ST):
                    for kc in range(ST):
                        last = pe.transpose(k.ps[:, 2 + g % 2, kc * S + t * P:kc * S + (t + 1) * P],
                                            s[:, g % 2, t, kc * P:(kc + 1) * P], k.ident)
                last.then_inc(q["p_turned"], 1)
                pe.wait_ge(q["pT_put"], B["pT_put"] + g + 1)
                if g >= 2:
                    pe.wait_ge(q["o_put"], B["o_put"] + g - 1)
                kv = g // (QH // KVH)
                for kc in range(ST):
                    last = pe.matmul(k.ps[:, 4 + g % 2, 0:S], v[:, kc, kv * HD:(kv + 1) * HD], pT[:, g % 2, kc, :],
                                     start=(kc == 0), stop=(kc == ST - 1))
                last.then_inc(q["o_done"], 1)
        pe.wait_ge(q["o_put"], B["o_put"] + QH)
        out_tensor(pe)
        norm.tensor(pe)

    def scalar(act):
        act.dma_start(causal_sb, causal).then_inc(q["loaded"], 16)
        act.dma_start(pos_i, positions).then_inc(q["loaded"], 16)
        norm.load_rows(act)
        for n in range(2):
            act.wait_ge(q["sin_arg"], B["sin_arg"] + n + 1)
            act.activation(trig[:, n], arg[:, n], ACT.Sin).then_inc(q["sin_done"], 1)
        for i in range(ST * len(CHUNKS)):
            t, c = i // len(CHUNKS), i % len(CHUNKS)
            act.wait_ge(q["column_done"], B["column_done"] + i + 1)
            bank = k.ps[:, i % 8, :]
            if c < 2:
                last = act.activation(pr[:, t, c * 512:(c + 1) * 512], bank, ACT.Copy)
            elif c == 2:
                act.activation(pr[:, t, 1024:WIDE], bank[:, 0:256], ACT.Copy)
                last = act.activation(v[:, t, :], bank[:, 256:512], ACT.Copy)
            elif c == 3:
                last = act.activation(pr[:, t, WIDE:WIDE + W], bank, ACT.Copy)
            else:
                act.activation(pr[:, t, WIDE + W:ROW], bank[:, 0:ID], ACT.Copy)
                last = act.activation(wi[:, t, :], bank[:, ID:ID + IH], ACT.Copy, scale=IH ** -0.5 * ID ** -0.5)
            last.then_inc(q["copied"], 1)
        for b in (1, 3, 5, 7):
            act.wait_ge(q["turned"], b + 1)
            for j in range(2):
                if 2 * b + j < len(BLOCKS):
                    last = act.activation(BLOCKS[2 * b + j][0], k.ps[:, b, j * S:(j + 1) * S], ACT.Copy)
            last.then_inc(q["turned_act"], 1)
        for i in range(ST * IH):
            t = i // IH
            act.wait_ge(q["index_done"], i + 1)
            if i >= 4:
                act.wait_ge(q["relu_used"], i - 3)
            act.activation(relu[:, i % 4, 0:P * (t + 1)], k.ps[:, i % 8, 0:P * (t + 1)], ACT.Relu).then_inc(q["relu_put"], 1)
        for h in range(QH):
            act.wait_ge(q["score_put"], B["score_put"] + h + 1)
            for t in range(ST):
                act.activation(s[:, h % 2, t, :], s[:, h % 2, t, :], ACT.Exp, bias=m[:, 2 * (h % 2) + t:2 * (h % 2) + t + 1],
                               accum_out=m[:, 4 + 2 * (h % 2) + t:5 + 2 * (h % 2) + t]).then_inc(q["exp_done"], 1)
            if h:
                act.wait_ge(q["o_done"], B["o_done"] + h)
                act.activation(k.hT[:, h - 1, :], k.ps[:, 4 + (h - 1) % 2, 0:S], ACT.Copy).then_inc(q["o_put"], 1)
        act.wait_ge(q["o_done"], B["o_done"] + QH)
        act.activation(k.hT[:, QH - 1, :], k.ps[:, 4 + (QH - 1) % 2, 0:S], ACT.Copy).then_inc(q["o_put"], 1)
        norm.scalar(act)

    def vector(dve):
        step = k.vector_order.on(dve)
        dve.wait_ge(q["loaded"], 32)
        step(dve.tensor_copy(pos, pos_i))
        for t in range(ST):
            step(dve.tensor_scalar(ang[:, t, :], fix(k, "inv_freq"), pos[:, t:t + 1], None, ALU.mult))
        step(range_reduce(step, dve, arg[:, 0], ang, rev))
        step(dve.scalar_tensor_tensor(out=arg[:, 1], in0=arg[:, 0], scalar=-1.0, in1=arg[:, 0], op0=ALU.mult, op1=ALU.max))
        dve.tensor_scalar(arg[:, 1], arg[:, 1], -1.0, math.pi / 2, ALU.mult, ALU.add).then_inc(q["sin_arg"], 2)
        dve.wait_ge(q["sin_done"], B["sin_done"] + 2)
        dve.wait_ge(q["copied"], B["copied"] + ST * len(CHUNKS))
        for c0, heads, width, a0, half in ((0, HH, HD, 0, 16), (WIDE, IH + 1, ID, 16, 8)):
            part = pr[:, :, c0:c0 + heads * width].rearrange("p t (h d) -> p t h d", d=width)
            t1, t2 = part[:, :, :, 0:half], part[:, :, :, half:2 * half]
            sin, cos = (trig[:, n, :, a0:a0 + half].unsqueeze(2).to_broadcast([P, ST, heads, half]) for n in range(2))
            p = [x[:, 0:ST * heads * half].rearrange("p (t h d) -> p t h d", t=ST, d=half) for x in tmp]
            step(dve.tensor_tensor(p[0], t1, cos, ALU.mult))
            step(dve.tensor_tensor(p[1], t2, sin, ALU.mult))
            step(dve.tensor_tensor(p[2], t2, cos, ALU.mult))
            step(dve.tensor_tensor(p[3], t1, sin, ALU.mult))
            step(dve.tensor_tensor(t1, p[0], p[1], ALU.subtract))
            step(dve.tensor_tensor(t2, p[2], p[3], ALU.add))
        step(dve.tensor_copy(ki2[:, :, 0:ID], pr[:, :, WIDE + W:ROW]))
        dve.tensor_copy(ki2[:, :, ID:2 * ID], pr[:, :, WIDE + W:ROW]).then_inc(q["rope_done"], 1)
        for b in (0, 2, 4, 6):
            dve.wait_ge(q["turned"], b + 1)
            for j in range(2):
                last = dve.tensor_copy(BLOCKS[2 * b + j][0], k.ps[:, b, j * S:(j + 1) * S])
            last.then_inc(q["turned_dve"], 1)
        for i in range(ST * IH):
            t, h = i // IH, i % IH
            w = slice(0, P * (t + 1))
            dve.wait_ge(q["relu_put"], i + 1)
            if h:
                dve.wait_ge(q["relu_used"], i)
            dve.scalar_tensor_tensor(out=score[:, t, w], in0=relu[:, i % 4, w], scalar=wi[:, t, h:h + 1],
                                     in1=causal_sb[:, t, w] if h == 0 else score[:, t, w], op0=ALU.mult,
                                     op1=ALU.add).then_inc(q["relu_used"], 1)
        dve.wait_ge(q["relu_used"], ST * IH)
        for t in range(ST):
            w = slice(0, P * (t + 1))
            for r in range(TOPK // 8):
                src = left[:, t, w] if r else score[:, t, w]
                step(dve.max(m[:, 8:16], src))
                step(dve.match_replace(out=left[:, t, w], in_to_replace=m[:, 8:16], in_values=src, imm_value=TAKEN))
            step(dve.tensor_scalar(left[:, t, w], left[:, t, w], TAKEN, -NOT, ALU.is_equal, ALU.mult))
            step(dve.scalar_tensor_tensor(out=keep[:, t, w], in0=left[:, t, w], scalar=NOT, in1=causal_sb[:, t, w],
                                          op0=ALU.add, op1=ALU.add))
        step(dve.tensor_copy(keep[:, 0, P:S], causal_sb[:, 0, P:S]))

        def weights(h):
            b = h % 2
            neg = m[:, 2 * b:2 * b + 2]
            dve.wait_ge(q["score_done"], B["score_done"] + h + 1)
            dve.scalar_tensor_tensor(out=s[:, b], in0=k.ps[:, b, :].rearrange("p (t s) -> p t s", t=ST), scalar=scale,
                                     in1=keep, op0=ALU.mult, op1=ALU.add).then_inc(q["score_read"], 1)
            dve.wait_ge(q["score_read"], B["score_read"] + h + 1)
            step(dve.tensor_reduce(neg, s[:, b], AX, ALU.max))
            dve.tensor_scalar(neg, neg, -1.0, None, ALU.mult).then_inc(q["score_put"], 1)

        def normalise(h):
            b = h % 2
            total = m[:, 4 + 2 * b:6 + 2 * b]
            dve.wait_ge(q["exp_done"], B["exp_done"] + 2 * h + 2)
            step(dve.reciprocal(total, total))
            for t in range(ST):
                dve.tensor_scalar(s[:, b, t, :], s[:, b, t, :], total[:, t:t + 1], None, ALU.mult).then_inc(q["p_put"], 1)
            dve.wait_ge(q["p_turned"], B["p_turned"] + h + 1)
            dve.tensor_copy(pT[:, b], k.ps[:, 2 + b, :].rearrange("p (c s) -> p c s", c=ST)).then_inc(q["pT_put"], 1)

        for h in range(QH):
            weights(h)
            if h:
                normalise(h - 1)
        normalise(QH - 1)
        norm.vector(dve)

    return Stage(tensor, scalar, vector, norm.gpsimd)


def second(k, t, base, out):
    loads, stages = [], []
    k.norms = k.turns = 0
    k.turns_of = {}

    def rows(i, j):
        return t["ln_g_2"][i, j], t["ln_b_2"][i, j]

    def add(new, stage):
        nonlocal loads
        loads += new
        stages.append(stage)

    def add_ffn(i, j, n):
        add(ffn_weights(k, n, t["ffn_w"][2 * i + j]), ffn(k, 2 * i + j, n, *rows(i, 2 * j)))
        return n + FC

    def add_ple(i, n, out=None):
        new = weights_in_slots(k, n, t["ple_w_gate_2"][i], 3, D)
        new += weights_in_slots(k, n + 3, t["ple_w_proj_2"][i], 3, D)
        add(new, ple(k, i, n, t["pT"][i], out))
        return n + 4

    add([], turn_only(k))
    n = add_ffn(0, 0, base)
    new = weights_in_slots(k, n, t["ab_w_in_2"][0], 1, 3 * CC + S5G * S5C)
    new += weights_in_slots(k, n + 8, t["s5_w_glu_2"][0], 6, CC)
    new += weights_in_slots(k, n + 9, t["ab_w_out_2"][0], 3, D)
    add(new, conv_s5(k, n, t["s5_params"], *rows(0, 1)))
    n = add_ffn(0, 1, n + 12)
    n = add_ple(0, n)
    n = add_ffn(1, 0, n)
    new = weights_in_slots(k, n, t["c_w_in_2"][0], 1, C_IN)
    new += weights_in_slots(k, n + DK, t["c_w_out_2"][0], 3, D)
    add(new, sparse_attention(k, n, t["causal"], t["positions"], *rows(1, 1)))
    n = add_ffn(1, 1, n + DK + 3)
    add_ple(1, n, out)
    return loads, stages


def laid_out_second(a):
    def by_state(v):
        v = np.asarray(v)
        v = v.reshape(S5G // 2, 2 * S5N, -1)
        return v.transpose(1, 0, 2).reshape(P, -1)

    log_dt = np.repeat(np.asarray(a["s5_log_dt_2"][0])[:, None], S5N, 1)
    c_parts = [np.asarray(a[n][0]).reshape(4, P, S5N).transpose(1, 0, 2).reshape(P, -1) for n in ("s5_c_re_2", "s5_c_im_2")]
    params = [by_state(a["s5_lam_re_2"][0]), by_state(a["s5_lam_im_2"][0]), by_state(log_dt),
              by_state(a["s5_b_re_2"][0]), by_state(a["s5_b_im_2"][0])] + c_parts
    w1, w3 = (np.asarray(a[n]).reshape(4, DK, P, FC, P).transpose(0, 3, 2, 1, 4).reshape(4, FC, P, D)
              for n in ("ffn_w1_2", "ffn_w3_2"))
    w2 = np.asarray(a["ffn_w2_2"]).reshape(4, FC, P, D)
    t, s = np.arange(S)[:, None], np.arange(S)[None, :]
    causal = np.where(s <= t, 0.0, -1e30).astype(np.float32)
    return {
        "ffn_w": np.concatenate([w1, w3, w2], 3),
        "s5_params": np.ascontiguousarray(np.concatenate(params, 1)),
        "pT": np.ascontiguousarray(np.asarray(a["p_2"])[:, 0].transpose(0, 2, 1).reshape(2, PLE // P, P, S).transpose(0, 2, 1, 3)),
        "positions": np.ascontiguousarray(np.asarray(a["positions_2"]).reshape(ST, P).T),
        "causal": np.ascontiguousarray(causal.reshape(ST, P, S).transpose(1, 0, 2)),
    }


def weights_in_slots(k, first, w, rows_per_slot, cols, r0=0):
    chunks = w.shape[0] // P
    out = []
    for i in range(-(-chunks // rows_per_slot)):
        c0, c1 = i * rows_per_slot, min((i + 1) * rows_per_slot, chunks)
        n = first + i
        k.use.landing(n)
        dst = slot(k, n, (c1 - c0) * cols).rearrange("p (c f) -> p c f", c=c1 - c0)
        out.append((n, [(dst, w[c0 * P:c1 * P, :].rearrange("(c p) f -> p c f", p=P))]))
    return out


def program(nc, t, out, y_dram):
    with ExitStack() as stack:
        k = setup(nc, stack)
        k.w_router = t["w_router"]
        n_out = DK
        n_experts = n_out + 3
        loads = weights_in_slots(k, 0, t["w_in"][0], 1, 3 * D)
        first_loads, first = filters(k, t["x"], t["fixed"], t["dft"], t["filt_tables"], t["filt_w1"], t["filt_w2"],
                                     t["filt_w3"], t["zT"])
        loads += weights_in_slots(k, n_out, t["w_out"][0], 3, D)
        stages = [first, projections(k), hyena(k), attention(k, t["dist"], t["lam_rows"]), routing(k, n_out)]
        expert_loads, expert_stage = experts(k, n_experts, t["w_gate"], t["w_up"], t["w_down"], y_dram)
        stages += [expert_stage, experts_combine(k, y_dram, t["final_norm_g"])]
        more_loads, more_stages = second(k, t, n_experts + 3 * DK * NE, out["out"])
        stages += more_stages

        with nc.Block() as block:
            @block.sync
            def _(sync):
                first_loads(sync)
                load_slots(k, sync, loads)
                expert_loads(sync)
                load_slots(k, sync, more_loads)

            @block.tensor
            def _(pe):
                for i, stage in enumerate(stages):
                    stage.tensor(pe)
                    meet(k, "tensor", pe, i)

            @block.scalar
            def _(act):
                for i, stage in enumerate(stages):
                    stage.scalar(act)
                    meet(k, "scalar", act, i)

            @block.vector
            def _(dve):
                for i, stage in enumerate(stages):
                    stage.vector(dve)
                    meet(k, "vector", dve, i)

            @block.gpsimd
            def _(pool):
                for i, stage in enumerate(stages):
                    stage.gpsimd(pool)
                    meet(k, "gpsimd", pool, i)


def constants():
    f32 = np.float32
    s = np.arange(S, dtype=np.float64)[:, None]
    f = np.arange(S, dtype=np.float64)[None, :]
    ang = 2 * np.pi * ((s * f) % NF) / NF
    nyq = np.where(np.arange(S) % 2 == 0, 1.0, -1.0)
    fwd = np.concatenate([np.cos(ang), -np.sin(ang)], 1)
    fwd[:, S] = nyq
    bwd = np.concatenate([np.cos(ang), np.sin(ang)], 1)
    bwd[:, S] = nyq
    bwd[0] = 0.0
    inv = np.concatenate([2 * np.cos(ang.T), -2 * np.sin(ang.T)], 0) / NF
    inv[0] = 1.0 / NF
    inv[S] = nyq / NF

    def tiles(a):
        return a.reshape(-1, P, a.shape[1]).transpose(1, 0, 2).reshape(P, -1).astype(f32)

    t = np.linspace(0.0, 1.0, S, dtype=f32)[:, None]
    w = (f32(2.0 * math.pi) * np.arange(S, dtype=f32)[:, None] / f32(S)).astype(f32)
    bands = np.linspace(1e-4, (EMB - 1) // 2 - 1, (EMB - 1) // 2, dtype=f32)[None, :]
    z = np.concatenate([t, np.cos(bands * w), -np.sin(bands * w)], axis=-1).astype(f32)
    deltas = np.abs(np.linspace(math.log(1e-2) / 1.5, math.log(1e-2) / 0.3, HY, dtype=f32))
    decay = np.exp(-t * deltas).astype(f32)
    dist = np.abs(np.arange(S)[:, None] - np.arange(S)[None, :]).astype(f32)
    eye = np.eye(P, dtype=f32)
    ones0 = np.ones((P, P), f32)
    ones0[0] = 0.0
    inv_attn = (500000.0 ** (-np.arange(0, 32, 2, dtype=f32) / f32(32))).astype(f32)
    inv_idx = (500000.0 ** (-np.arange(0, 16, 2, dtype=f32) / f32(16))).astype(f32)
    return {
        "dft": np.concatenate([tiles(fwd), tiles(inv)], 1),
        "filt_tables": np.concatenate([tiles(bwd), tiles(decay)], 1),
        "zT": np.ascontiguousarray(z.T), "dist": tiles(dist).reshape(P, ST, S),
        "ident": eye, "ones": np.ones((P, P), f32), "ones0": ones0,
        "group_mean": np.kron(np.eye(2, dtype=f32), np.full((64, 64), 1 / 64, f32)),
        "mask_b": np.kron(np.eye(2, dtype=f32), np.ones((S5N, 1), f32)),
        "mask_c": np.tile(np.kron(np.eye(2, dtype=f32), np.ones((S5C, 1), f32)), (4, 1)),
        "seed1": eye * f32(ALPHA), "seed2": eye * f32(2 * ALPHA),
        "slot_no": np.tile(np.arange(CAP, dtype=f32), (P, 1)),
        "inv_freq": np.tile(np.concatenate([inv_attn, inv_idx]), (P, 1)),
    }


def laid_out(a):
    c = constants()

    def by_channel(v):
        v = np.asarray(v)
        return np.ascontiguousarray(v.reshape(-1, P).T)

    filt = np.zeros((P, 3), np.float32)
    for i, n in enumerate(("filt_b1", "filt_b2", "filt_freq")):
        filt[:HID, i] = a[n][0]
    parts = dict(c)
    parts.update(attn_g=by_channel(a["attn_norm_g"]), conv_w=by_channel(a["conv_w"]), conv_b=by_channel(a["conv_b"]),
                 skip=by_channel(a["hyena_skip"]), hy_g=by_channel(a["hyena_norm_g"]), subln_g=by_channel(a["subln_g"]),
                 ffn_g=by_channel(a["ffn_norm_g"]), filt=filt, conv_w2=by_channel(a["conv_w_2"]),
                 s5_d=by_channel(a["s5_d_2"]), b_glu=by_channel(a["s5_b_glu_2"]))
    out = {n: np.ascontiguousarray(a[n]) for n in WHOLE}
    out["fixed"] = np.concatenate([parts[n] for n, (at, w) in FIX.items() if n != "misc"], 1)
    for n in ("dft", "filt_tables", "zT", "dist"):
        out[n] = c[n]
    lam = np.concatenate([a[n][0] for n in ("lambda_q1", "lambda_k1", "lambda_q2", "lambda_k2")])
    out["lam_rows"] = np.ascontiguousarray(np.broadcast_to(lam, (P, lam.size)))
    out.update(laid_out_second(a))
    return out


WHOLE = ["x", "w_in", "filt_w1", "filt_w2", "filt_w3", "w_out", "w_router", "w_gate", "w_up", "w_down", "final_norm_g",
         "ln_g_2", "ln_b_2", "ple_w_proj_2", "ple_w_gate_2", "ab_w_in_2",
         "ab_w_out_2", "s5_w_glu_2", "c_w_in_2", "c_w_out_2"]


def kernel(**inputs):
    import concourse.bacc as bacc
    from concourse.bass_utils import run_bass_kernel_spmd

    arrays = laid_out({n: np.asarray(v) for n, v in inputs.items()})
    nc = bacc.Bacc("TRN2", target_bir_lowering=False, num_devices=1)
    tensors = {n: nc.dram_tensor(f"in_{n}", v.shape, mybir.dt.from_np(v.dtype), kind="ExternalInput").ap()
               for n, v in arrays.items()}
    out = nc.dram_tensor("result", (1, S, D), F32, kind="ExternalOutput").ap()
    y_dram = nc.dram_tensor("expert_rows", (NE * CAP, D), F32, kind="Internal").ap()
    program(nc, tensors, {"out": out}, y_dram)
    done = run_bass_kernel_spmd(nc, [{f"in_{n}": v for n, v in arrays.items()}], core_ids=[0])
    return done.results[0]["result"]
```

```python
import math
from contextlib import ExitStack

import numpy as np
import concourse.bass as bass
from concourse import mybir

F32 = mybir.dt.float32
F32R = mybir.dt.float32r
I32 = mybir.dt.int32
ALU = mybir.AluOpType
ACT = mybir.ActivationFunctionType
AX = mybir.AxisListType.X

P = 128
S = 256
ST = S // P
D = 1024
DK = D // P
EPS = 1e-6
HY = 512
HC = HY // P
NORD = 2
NF = 2 * S
FM = NF // P
EMB, HID = 33, 64
HEADS, DH = 4, 64
LAM_INIT = 0.8 - 0.6 * math.exp(0.0)
NE, CAP, FF = 16, 32, 2816
NG = 4
FG = FF // NG
FH = FG // 2
FT = FG // P
FR = FG - FT * P

ALPHA = 4.0 ** 0.25
LN_EPS = 1e-5
PLE = 256
CC = 512
S5G, S5C, S5N = 32, 16, 64
QH, HD, KVH, IH, ID = 8, 128, 2, 8, 64
TOPK = 64
C_IN = QH * HD + 2 * KVH * HD + IH * ID + ID + IH

SLOT = 3072
SLOTS = 8
ARENA = 16256
WORK = 12288

FIX = {}
_at = 0
for _n, _w in [("ident", P), ("ones", P), ("ones0", P), ("group_mean", P), ("mask_b", 2), ("mask_c", 2), ("seed1", P), ("seed2", P), ("slot_no", CAP),
               ("inv_freq", 24), ("attn_g", DK), ("conv_w", 36), ("conv_b", 12), ("skip", 8), ("hy_g", HC),
               ("subln_g", 1), ("ffn_g", DK), ("filt", 3), ("conv_w2", 12), ("s5_d", 4), ("b_glu", 4), ("ln_g", 6 * DK), ("ln_b", 6 * DK), ("misc", 40)]:
    FIX[_n] = (_at, _w)
    _at += _w
FIXED = _at
LOADED = FIX["misc"][0]
X0 = 1024 if FIXED <= 1024 else FIXED
HT0 = X0 + ST * D
R0 = HT0 + DK * S
PARTS = 4096 + 1024


class InOrder:

    def __init__(self, done):
        self.done, self.count = done, 0

    def on(self, engine):
        self.engine = engine
        return self

    def __call__(self, instruction):
        self.count += 1
        instruction.then_inc(self.done, 1)
        self.engine.wait_ge(self.done, self.count)


class Ring:

    def __init__(self):
        self.marks = [0] * SLOTS
        self.mark = {}

    def landing(self, n, dmas=1):
        self.marks[n % SLOTS] += 16 * dmas
        self.mark[n] = self.marks[n % SLOTS]
        return self.mark[n]


class Core:
    pass


ENGINES = ("tensor", "scalar", "vector", "gpsimd")


class Stage:

    def __init__(self, tensor, scalar, vector, gpsimd=None):
        self.tensor, self.scalar, self.vector = tensor, scalar, vector
        self.gpsimd = gpsimd or (lambda pool: None)


def meet(k, name, engine, i):
    engine.drain().then_inc(k.passed[name], 1)
    for other in ENGINES:
        if other != name:
            engine.wait_ge(k.passed[other], i + 1)


def setup(nc, stack):
    k = Core()
    k.nc = nc
    base = -(-nc.sbuf_base // 32) * 32
    place = lambda name, at, shape, dt: nc.alloc_sbuf_tensor_at(name, shape, dt, offset=base + 4 * at)
    at_arena, at_work = SLOTS * SLOT, SLOTS * SLOT + ARENA
    k.ring = place("ring", 0, [P, SLOTS * SLOT], F32)
    k.arena = place("arena", at_arena, [P, ARENA], F32)
    k.work = place("work", at_work, [P, WORK], F32)
    k.w13 = place("w13", at_work, [P, 2, 2, 2, DK, P], F32R)
    k.w2 = place("w2", at_work + 8192, [P, 2, 2, D], F32R)
    k.hsplit = place("hsplit", at_work - PARTS, [P, 2, DK, S], F32R)
    k.hidsplit = place("hidsplit", at_work - PARTS + 4096, [P, 2, 2, S], F32R)
    k.ps = stack.enter_context(nc.psum_tensor("ps", [P, 8, 512], F32))
    k.norms = 0
    made = {}

    def sem(name):
        if name not in made:
            made[name] = stack.enter_context(nc.semaphore(name))
        return made[name]

    k.sem = sem
    k.vector_order, k.pool_order = InOrder(sem("vector_order")), InOrder(sem("pool_order"))
    k.slot_ready = [k.sem(f"slot_ready{i}") for i in range(SLOTS)]
    k.slot_freed = k.sem("slot_freed")
    k.use = Ring()
    k.passed = {name: k.sem(f"{name}_passed") for name in ENGINES}
    k.x = k.arena[:, X0:X0 + ST * D].rearrange("p (t d) -> p t d", t=ST)
    k.hT = k.arena[:, HT0:HT0 + DK * S].rearrange("p (k s) -> p k s", k=DK)
    k.ident = fix(k, "ident")
    return k


def fix(k, name):
    a, w = FIX[name]
    return k.arena[:, a:a + w]


def slot(k, n, width=SLOT):
    s = n % SLOTS
    return k.ring[:, s * SLOT:s * SLOT + width]


def area(core, at, width, /, **shape):
    return view(core.arena[:, R0 + at:R0 + at + width], **shape)


def work(core, at, width, /, **shape):
    return view(core.work[:, at:at + width], **shape)


def view(v, /, **shape):
    if not shape:
        return v
    names = list(shape)
    return v.rearrange(f"p ({' '.join(names)} z) -> p {' '.join(names)} z", **shape)


def load_slots(k, sync, weights):
    for n, pairs in weights:
        if n >= SLOTS:
            sync.wait_ge(k.slot_freed, n - SLOTS + 1)
        for dst, src in pairs:
            sync.dma_start(dst, src).then_inc(k.slot_ready[n % SLOTS], 16)


def range_reduce(step, vector, out, angle, n):
    magic = 12582912.0
    c1 = 6.28125
    c2 = float(np.float32(np.round((2 * math.pi - c1) * 2 ** 21) / 2 ** 21))
    c3 = float(np.float32(2 * math.pi - c1 - c2))
    step(vector.tensor_scalar(n, angle, 1.0 / (2 * math.pi), magic, ALU.mult, ALU.add))
    step(vector.tensor_scalar(n, n, magic, None, ALU.subtract))
    step(vector.scalar_tensor_tensor(out=out, in0=n, scalar=-c1, in1=angle, op0=ALU.mult, op1=ALU.add))
    step(vector.scalar_tensor_tensor(out=out, in0=n, scalar=-c2, in1=out, op0=ALU.mult, op1=ALU.add))
    step(vector.scalar_tensor_tensor(out=out, in0=n, scalar=-c3, in1=out, op0=ALU.mult, op1=ALU.add))
    return vector.tensor_scalar(out, out, 3.1415925, -3.1415925, ALU.min, ALU.max)


def misc(k, a, w):
    b = FIX["misc"][0]
    return k.arena[:, b + a:b + a + w]


def filters(k, x, fixed, dft, filt_tables, filt_w1, filt_w2, filt_w3, zT):
    nc = k.nc
    sem = k.sem
    x_loaded, fixed_loaded, tables_loaded = sem("x_loaded"), sem("fixed_loaded"), sem("tables_loaded")
    ones_set, square_sum, root, normed = sem("ones_set"), sem("ms_ready"), sem("ms_root"), sem("normed")
    turned, sin_arg, sin_done = sem("turned"), sem("sin_arg"), sem("sin_done")
    layer_done, taps_ready, taps_put = sem("layer_done"), sem("taps_ready"), sem("taps_put")
    abs_done, l1_done, l1_inverse = sem("abs_done"), sem("l1_done"), sem("l1_inverse")
    freq_ready, freq_put, hT_put, hT_bank = sem("freq_ready"), sem("freq_put"), sem("hT_put"), sem("hT_bank")

    K = area(k, 0, 4096, o=NORD, m=FM)
    Kn = area(k, 4096, 1024, o=NORD)
    k.K, k.Kn = K, Kn
    dft_sb = area(k, 5120, 2048)
    k.Fwd = view(dft_sb[:, 0:1024], t=ST)
    k.Inv = view(dft_sb[:, 1024:2048], m=FM)
    tab = work(k, 0, 2048)
    Bwd, decay = view(tab[:, 0:1024], t=ST), view(tab[:, 1024:2048], t=ST)
    w3 = work(k, 2048, 2048)
    taps = work(k, 4096, 4096, t=ST, n=4)
    z_sb = work(k, 8192, 256)
    w1, w2 = work(k, 8448, 64), work(k, 8512, 64)
    arg, hid, nrev = work(k, 8576, 256), work(k, 8832, 256), work(k, 9088, 256)
    mag = work(k, 9344, 1024, b=2)
    inv = work(k, 10368, 1024, o=2)
    xn = area(k, 7168, 2048, t=ST)
    ones, ones0 = fix(k, "ones"), fix(k, "ones0")
    stat = misc(k, 0, 8)
    filt = fix(k, "filt")

    def load(sync):
        sync.dma_start(k.x, x.rearrange("b (t p) d -> p (b t) d", p=P)).then_inc(x_loaded, 16)
        sync.dma_start(k.arena[:, 0:LOADED], fixed).then_inc(fixed_loaded, 16)

    def scalar(act):
        for dst, src in ((z_sb[0:EMB, :], zT), (w1[0:EMB, :], filt_w1[0]), (w2[0:HID, :], filt_w2[0]),
                         (w3[0:HID, :], filt_w3[0]), (tab, filt_tables), (dft_sb, dft)):
            act.dma_start(dst, src).then_inc(tables_loaded, 16)
        act.wait_ge(square_sum, 1)
        act.activation(stat[:, 2:4], stat[:, 2:4], ACT.Sqrt).then_inc(root, 1)
        for layer in range(2):
            act.wait_ge(sin_arg, layer + 1)
            act.activation(hid[0:HID, :], arg[0:HID, :], ACT.Sin).then_inc(sin_done, 1)
        for i in range(ST * 4):
            act.wait_ge(taps_put, i + 1)
            if i >= 2:
                act.wait_ge(l1_done, i - 1)
            act.activation(mag[:, i % 2, :], taps[:, i // 4, i % 4, :], ACT.Abs).then_inc(abs_done, 1)

    def tensor(pe):
        pe.wait_ge(fixed_loaded, 16)
        pe.wait_ge(normed, 2)
        for b in range(4):
            for j in range(4):
                kk, t = 2 * b + j // 2, j % 2
                last = pe.transpose(k.ps[:, b, j * P:(j + 1) * P], xn[:, t, kk * P:(kk + 1) * P], k.ident)
            last.then_inc(hT_bank, 1)
        pe.wait_ge(tables_loaded, 16 * 6)
        pe.matmul(k.ps[0:HID, 4, 0:S], w1[0:EMB, :], z_sb[0:EMB, :], start=True, stop=True).then_inc(layer_done, 1)
        pe.wait_ge(sin_done, 1)
        pe.matmul(k.ps[0:HID, 5, 0:S], w2[0:HID, :], hid[0:HID, :], start=True, stop=True).then_inc(layer_done, 1)
        pe.wait_ge(sin_done, 2)
        pe.wait_ge(hT_put, DK)
        for i in range(ST * 4):
            t, n = i // 4, i % 4
            if i >= 4:
                pe.wait_ge(taps_put, i - 3)
            pe.matmul(k.ps[:, i % 4, :], hid[0:HID, t * P:(t + 1) * P], w3[0:HID, n * HY:(n + 1) * HY],
                      start=True, stop=True).then_inc(taps_ready, 1)
        for i in range(ST * 4):
            t, n = i // 4, i % 4
            direction, order = n // 2, n % 2
            pe.wait_ge(abs_done, i + 1)
            pe.matmul(k.ps[:, 6 + order, :], ones0 if direction and t == 0 else ones, mag[:, i % 2, :],
                      start=(t == 0 and direction == 0), stop=(t == ST - 1 and direction == 1)).then_inc(l1_done, 1)
        pe.wait_ge(taps_put, ST * 4)
        for i in range(NORD * FM):
            order, m = i // FM, i % FM
            if i >= 4:
                pe.wait_ge(freq_put, i - 3)
            for a in range(4):
                t, direction = a // 2, a % 2
                table = Bwd if direction else k.Fwd
                last = pe.matmul(k.ps[:, i % 4, :], table[:, t, m * P:(m + 1) * P],
                                 taps[:, t, 2 * direction + order, :], start=(a == 0), stop=(a == 3))
            last.then_inc(freq_ready, 1)

    def vector(dve):
        step = k.vector_order.on(dve)
        dve.wait_ge(x_loaded, 16)
        for t in range(ST):
            step(dve.tensor_tensor_reduce(xn[:, t, :], k.x[:, t, :], k.x[:, t, :], 1.0, 0.0, ALU.mult, ALU.add,
                                          stat[:, t:t + 1]))
        dve.tensor_scalar(stat[:, 2:4], stat[:, 0:2], 1.0 / D, EPS, ALU.mult, ALU.add).then_inc(square_sum, 1)
        dve.wait_ge(root, 1)
        step(dve.reciprocal(stat[:, 4:6], stat[:, 2:4]))
        for t in range(ST):
            dve.tensor_scalar(xn[:, t, :], k.x[:, t, :], stat[:, 4 + t:5 + t], None, ALU.mult).then_inc(normed, 1)
        dve.wait_ge(fixed_loaded, 16)
        for kk in range(DK):
            dve.wait_ge(hT_bank, kk // 2 + 1)
            dve.tensor_scalar(k.hT[:, kk, :], k.ps[:, kk // 2, (kk % 2) * S:(kk % 2 + 1) * S],
                              fix(k, "attn_g")[:, kk:kk + 1], None, ALU.mult).then_inc(hT_put, 1)
        for layer in range(2):
            dve.wait_ge(layer_done, layer + 1)
            step(dve.tensor_scalar(arg[0:HID, :], k.ps[0:HID, 4 + layer, 0:S], filt[0:HID, layer:layer + 1],
                                   filt[0:HID, 2:3], ALU.add, ALU.mult))
            range_reduce(step, dve, arg[0:HID, :], arg[0:HID, :], nrev[0:HID, :]).then_inc(sin_arg, 1)
        for i in range(ST * 4):
            t, n = i // 4, i % 4
            dve.wait_ge(taps_ready, i + 1)
            dve.tensor_tensor(taps[:, t, n, :], k.ps[:, i % 4, :], decay[:, t, :], ALU.mult).then_inc(taps_put, 1)
        dve.wait_ge(l1_done, ST * 4)
        for order in range(NORD):
            step(dve.reciprocal(inv[:, order, :], k.ps[:, 6 + order, :]))
        for i in range(NORD * FM):
            order, m = i // FM, i % FM
            dve.wait_ge(freq_ready, i + 1)
            dve.tensor_tensor(K[:, order, m, :], k.ps[:, i % 4, :], inv[:, order, :], ALU.mult).then_inc(freq_put, 1)
        dve.wait_ge(freq_put, NORD * FM)
        for order in range(NORD):
            step(dve.tensor_copy(Kn[:, order, :], K[:, order, 0, :]))
            step(dve.tensor_copy(Kn[0:1, order, :], K[0:1, order, 2, :]))
            step(dve.memset(K[0:1, order, 2, :], 0.0))

    return load, Stage(tensor, scalar, vector)


def projections(k):
    nc = k.nc
    sem = k.sem
    column_done, convolved, copied = sem("column_done"), sem("convolved"), sem("copied")
    centre_put = sem("centre_put")
    u = work(k, 0, 3072, c=12)
    qk = work(k, 3072, 2048, c=8)
    v = work(k, 5120, 1024, t=ST)
    k.u, k.qk, k.v = u, qk, v
    conv_w, conv_b = fix(k, "conv_w"), fix(k, "conv_b")

    def tensor(pe):
        for n in range(DK):
            pe.wait_ge(k.slot_ready[n], 16)
        for c in range(20):
            if 6 <= c < 18:
                pe.wait_ge(convolved, c - 5)
            elif c >= 18:
                pe.wait_ge(copied, c - 17)
            for kk in range(DK):
                last = pe.matmul(k.ps[:, c % 6, 0:S], slot(k, kk)[:, c * P:(c + 1) * P], k.hT[:, kk, :],
                                 start=(kk == 0), stop=(kk == DK - 1))
            last.then_inc(column_done, 1)
        for t in range(ST):
            for kk in range(DK):
                last = pe.matmul(k.ps[:, 6 + t, :], k.hT[:, kk, t * P:(t + 1) * P], slot(k, kk)[:, 20 * P:24 * P],
                                 start=(kk == 0), stop=(kk == DK - 1))
            last.then_inc(column_done, 1)
        pe.drain().then_inc(k.slot_freed, DK)

    def scalar(act):
        for c in range(20):
            act.wait_ge(column_done, c + 1)
            if c < 12:
                act.activation(u[:, c, :], k.ps[:, c % 6, 0:S], ACT.Identity, scale=conv_w[:, 12 + c:13 + c],
                               bias=conv_b[:, c:c + 1]).then_inc(centre_put, 1)
            else:
                act.activation(qk[:, c - 12, :], k.ps[:, c % 6, 0:S], ACT.Copy).then_inc(copied, 1)
        for t in range(ST):
            act.wait_ge(column_done, 21 + t)
            act.activation(v[:, t, :], k.ps[:, 6 + t, :], ACT.Copy)

    def vector(dve):
        step = k.vector_order.on(dve)
        for c in range(12):
            dve.wait_ge(centre_put, c + 1)
            step(dve.scalar_tensor_tensor(out=u[:, c, 1:S], in0=k.ps[:, c % 6, 0:S - 1], scalar=conv_w[:, c:c + 1],
                                          in1=u[:, c, 1:S], op0=ALU.mult, op1=ALU.add))
            dve.scalar_tensor_tensor(out=u[:, c, 0:S - 1], in0=k.ps[:, c % 6, 1:S],
                                     scalar=conv_w[:, 24 + c:25 + c], in1=u[:, c, 0:S - 1], op0=ALU.mult,
                                     op1=ALU.add).then_inc(convolved, 1)

    return Stage(tensor, scalar, vector)


def hyena(k):
    nc = k.nc
    sem = k.sem
    z_turned, z_put, spectrum_done = sem("z_turned"), sem("z_put"), sem("spectrum_done")
    product_put, mixed, wave_done = sem("product_put"), sem("mixed"), sem("wave_done")
    hy_square, hy_mean, hy_root = sem("hy_square"), sem("hy_mean"), sem("hy_root")
    gated = sem("gated")
    U, K, Kn = k.u, k.K, k.Kn
    prod = area(k, 7168, 2048, n=4)
    Y = work(k, 6144, 2048, m=FM)
    zs = work(k, 8192, 1024, t=ST)
    mixT = k.hT
    tmp = area(k, 9216, 1024, c=HC)
    tmp2 = area(k, 7168, 1024, c=HC)
    z = U[:, 8:12, :]

    def tensor(pe):
        for o in range(NORD):
            if o:
                pe.wait_ge(gated, HC)
            for t in range(ST):
                for c in range(HC):
                    last = pe.transpose(k.ps[:, t, c * P:(c + 1) * P], z[:, c, t * P:(t + 1) * P], k.ident)
            last.then_inc(z_turned, 1)
            pe.wait_ge(z_put, ST * (o + 1))
            for m in (0, 2, 1, 3):
                if m == 0 and o:
                    pe.wait_ge(mixed, 4)
                for t in range(ST):
                    last = pe.matmul(k.ps[:, 2 + m, :], k.Fwd[:, t, m * P:(m + 1) * P], zs[:, t, :],
                                     start=(t == 0), stop=(t == ST - 1))
                last.then_inc(spectrum_done, 1)
            pe.wait_ge(mixed, 4 * (o + 1))
            for c in range(HC):
                if c >= 2:
                    pe.wait_ge(gated, HC * o + c - 1)
                for m in range(FM):
                    last = pe.matmul(k.ps[:, 6 + c % 2, 0:S], Y[:, m, c * P:(c + 1) * P], k.Inv[:, m, :],
                                     start=(m == 0), stop=(m == FM - 1))
                last.then_inc(wave_done, 1)
        for c in range(HC):
            pe.wait_ge(hy_square, c + 1)
            pe.matmul(k.ps[:, c, 0:S], fix(k, "group_mean"), tmp[:, c, :], start=True, stop=True).then_inc(hy_mean, 1)

    def gpsimd(pool):
        for o in range(NORD):
            for h in range(2):
                pool.wait_ge(product_put, 8 * o + 4 * h + 4)
                pool.tensor_tensor(Y[:, h, :], prod[:, 0, :], prod[:, 1, :], ALU.subtract).then_inc(mixed, 1)
                pool.tensor_tensor(Y[:, 2 + h, :], prod[:, 2, :], prod[:, 3, :], ALU.add).then_inc(mixed, 1)

    def scalar(act):
        for o in range(NORD):
            act.wait_ge(z_turned, o + 1)
            for t in range(ST):
                act.activation(zs[:, t, :], k.ps[:, t, :], ACT.Copy).then_inc(z_put, 1)
        for c in range(HC):
            act.wait_ge(gated, HC + c + 1)
            act.activation(tmp[:, c, :], z[:, c, :], ACT.Square).then_inc(hy_square, 1)
        for c in range(HC):
            act.wait_ge(hy_mean, c + 1)
            act.activation(tmp2[:, c, :], k.ps[:, c, 0:S], ACT.Sqrt, bias=misc(k, 8, 1)).then_inc(hy_root, 1)

    def vector(dve):
        step = k.vector_order.on(dve)
        step(dve.memset(misc(k, 8, 1), EPS))
        for o in range(NORD):
            for h in range(2):
                dve.wait_ge(spectrum_done, 4 * o + 2 * h + 2)
                re, im = k.ps[:, 2 + h, :], k.ps[:, 4 + h, :]
                if o or h:
                    dve.wait_ge(mixed, 4 * o + 2 * h)
                for i, (a, b) in enumerate(((re, K[:, o, h, :]), (im, K[:, o, 2 + h, :]),
                                            (im, Kn[:, o, :] if h == 0 else K[:, o, 1, :]),
                                            (re, K[:, o, 2 + h, :]))):
                    dve.tensor_tensor(prod[:, i, :], a, b, ALU.mult).then_inc(product_put, 1)
            dve.wait_ge(gated, HC * o)
            for c in range(HC):
                dve.wait_ge(wave_done, HC * o + c + 1)
                step(dve.scalar_tensor_tensor(out=z[:, c, :], in0=z[:, c, :],
                                              scalar=fix(k, "skip")[:, 4 * o + c:4 * o + c + 1],
                                              in1=k.ps[:, 6 + c % 2, 0:S], op0=ALU.mult, op1=ALU.add))
                dve.tensor_tensor(z[:, c, :], z[:, c, :], U[:, 4 * o + c, :], ALU.mult).then_inc(gated, 1)
        for c in range(HC):
            dve.wait_ge(hy_root, c + 1)
            step(dve.reciprocal(tmp2[:, c, :], tmp2[:, c, :]))
            dve.scalar_tensor_tensor(out=mixT[:, c, :], in0=z[:, c, :], scalar=fix(k, "hy_g")[:, c:c + 1],
                                     in1=tmp2[:, c, :], op0=ALU.mult, op1=ALU.mult)

    return Stage(tensor, scalar, vector, gpsimd)


def skewed(heads, first, second, third):
    for h in range(heads + 2):
        if h < heads:
            first(h)
        if h >= 2 and third:
            third(h - 2)
        if 1 <= h <= heads and second:
            second(h - 1)


def attention(k, dist, lam_rows):
    nc = k.nc
    sem = k.sem
    dist_loaded, score_done = sem("dist_loaded"), sem("score_done")
    score_read, score_put = sem("score_read"), sem("score_put")
    exp_done, lam_arg, lam_exp = sem("exp_done"), sem("lam_arg"), sem("lam_exp")
    a_put, a_turned, aT_put, o_done, o_put = sem("p_put"), sem("p_turned"), sem("pT_put"), sem("o_done"), sem("o_put")
    sq_put, ms_done, at_root = sem("sq_put"), sem("ms_done"), sem("at_root")
    mixT = k.hT
    dist_sb = area(k, 0, 512, t=ST)
    lam_sb = area(k, 512, 256)
    s = area(k, 1024, 2048, b=2, n=4)
    a = area(k, 3072, 1024, b=2, t=ST)
    aT = area(k, 4096, 1024, b=2, t=ST)
    oT = area(k, 5120, 1024, h=HEADS)
    sq = area(k, 6144, 1024, n=2)
    rt = area(k, 7168, 1024, h=HEADS)
    m = misc(k, 10, 30)
    lam = m[:, 0:1]
    scale = DH ** -0.5
    slopes = [float(np.float32(2.0 ** (-8.0 * (i + 1) / HEADS))) for i in range(HEADS)]

    def tensor(pe):
        def scores(h):
            if h >= 2:
                pe.wait_ge(score_read, 2 * (h - 1))
            for c in range(2):
                for t in range(ST):
                    last = pe.matmul(k.ps[:, 2 * (h % 2) + c, t * S:(t + 1) * S],
                                     k.qk[c * DH:(c + 1) * DH, h, t * P:(t + 1) * P],
                                     k.qk[c * DH:(c + 1) * DH, HEADS + h, :], start=True, stop=True)
                last.then_inc(score_done, 1)

        def turn(h):
            pe.wait_ge(a_put, ST * (h + 1))
            if h >= 2:
                pe.wait_ge(aT_put, h - 1)
            for t in range(ST):
                for kc in range(ST):
                    last = pe.transpose(k.ps[:, 4 + h % 2, kc * S + t * P:kc * S + (t + 1) * P],
                                        a[:, h % 2, t, kc * P:(kc + 1) * P], k.ident)
            last.then_inc(a_turned, 1)

        def outputs(h):
            pe.wait_ge(aT_put, h + 1)
            if h >= 2:
                pe.wait_ge(o_put, h - 1)
            for kc in range(ST):
                last = pe.matmul(k.ps[:, 6 + h % 2, 0:S], k.v[:, kc, h * P:(h + 1) * P], aT[:, h % 2, kc, :],
                                 start=(kc == 0), stop=(kc == ST - 1))
            last.then_inc(o_done, 1)

        skewed(HEADS, scores, turn, outputs)
        for n in range(2):
            pe.wait_ge(sq_put, n + 1)
            pe.matmul(k.ps[:, n, :], fix(k, "ones"), sq[:, n, :], start=True, stop=True).then_inc(ms_done, 1)

    def scalar(act):
        act.dma_start(dist_sb, dist).then_inc(dist_loaded, 16)
        act.dma_start(lam_sb, lam_rows).then_inc(dist_loaded, 16)
        act.wait_ge(lam_arg, 2)
        act.activation(m[:, 1:3], m[:, 1:3], ACT.Exp).then_inc(lam_exp, 1)
        def exponentials(h):
            act.wait_ge(score_put, h + 1)
            for n in range(4):
                act.activation(s[:, h % 2, n, :], s[:, h % 2, n, :], ACT.Exp, scale=scale,
                               bias=m[:, 8 + 4 * (h % 2) + n:9 + 4 * (h % 2) + n],
                               accum_out=m[:, 16 + 4 * (h % 2) + n:17 + 4 * (h % 2) + n]).then_inc(exp_done, 1)

        def output(h):
            act.wait_ge(o_done, h + 1)
            act.activation(oT[:, h, :], k.ps[:, 6 + h % 2, 0:S], ACT.Copy).then_inc(o_put, 1)

        skewed(HEADS, exponentials, None, output)
        for n in range(2):
            act.wait_ge(o_put, HEADS)
            act.activation(sq[:, n, :], oT[:, 2 * n:2 * n + 2, :], ACT.Square).then_inc(sq_put, 1)
        for n in range(2):
            act.wait_ge(ms_done, n + 1)
            act.activation(rt[:, 2 * n:2 * n + 2, :], k.ps[:, n, :], ACT.Sqrt, scale=1.0 / P,
                           bias=misc(k, 8, 1)).then_inc(at_root, 1)

    def vector(dve):
        step = k.vector_order.on(dve)
        dve.wait_ge(dist_loaded, 32)
        for i in range(2):
            dve.tensor_tensor_reduce(lam_sb[:, 2 * i * DH:(2 * i + 1) * DH], lam_sb[:, 2 * i * DH:(2 * i + 1) * DH],
                                     lam_sb[:, (2 * i + 1) * DH:(2 * i + 2) * DH], 1.0, 0.0, ALU.mult, ALU.add,
                                     m[:, 1 + i:2 + i]).then_inc(lam_arg, 1)
        step(dve.tensor_scalar(m[:, 3:4], fix(k, "subln_g"), 1.0 - LAM_INIT, None, ALU.mult))
        dve.wait_ge(lam_exp, 1)
        step(dve.tensor_tensor(m[:, 0:1], m[:, 1:2], m[:, 2:3], ALU.subtract))
        step(dve.tensor_scalar(m[:, 0:1], m[:, 0:1], LAM_INIT, None, ALU.add))

        def score(h):
            b = h % 2
            if h >= 2:
                dve.wait_ge(a_put, ST * (h - 1))
            for c in range(2):
                dve.wait_ge(score_done, 2 * h + c + 1)
                dve.scalar_tensor_tensor(out=s[:, b, 2 * c:2 * c + 2, :], in0=dist_sb, scalar=-slopes[h] / scale,
                                         in1=k.ps[:, 2 * b + c, :].rearrange("p (t s) -> p t s", t=ST),
                                         op0=ALU.mult, op1=ALU.add).then_inc(score_read, 1)
            dve.wait_ge(score_read, 2 * h + 2)
            step(dve.tensor_reduce(m[:, 8 + 4 * b:12 + 4 * b], s[:, b], AX, ALU.max))
            dve.tensor_scalar(m[:, 8 + 4 * b:12 + 4 * b], m[:, 8 + 4 * b:12 + 4 * b], -scale, None,
                              ALU.mult).then_inc(score_put, 1)

        def combine(h):
            b = h % 2
            r = m[:, 16 + 4 * b:20 + 4 * b]
            dve.wait_ge(exp_done, 4 * h + 4)
            step(dve.reciprocal(r, r))
            step(dve.tensor_scalar(r[:, 2:4], r[:, 2:4], lam, None, ALU.mult))
            for t in range(ST):
                step(dve.tensor_scalar(s[:, b, 2 + t, :], s[:, b, 2 + t, :], r[:, 2 + t:3 + t], None, ALU.mult))
            for t in range(ST):
                dve.scalar_tensor_tensor(out=a[:, b, t, :], in0=s[:, b, t, :], scalar=r[:, t:t + 1],
                                         in1=s[:, b, 2 + t, :], op0=ALU.mult, op1=ALU.subtract).then_inc(a_put, 1)

        def turned(h):
            dve.wait_ge(a_turned, h + 1)
            dve.tensor_copy(aT[:, h % 2], k.ps[:, 4 + h % 2, :].rearrange("p (t s) -> p t s", t=ST)).then_inc(aT_put, 1)

        skewed(HEADS, score, combine, turned)
        for n in range(2):
            dve.wait_ge(at_root, n + 1)
            step(dve.reciprocal(rt[:, 2 * n:2 * n + 2, :], rt[:, 2 * n:2 * n + 2, :]))
            dve.scalar_tensor_tensor(out=mixT[:, HC + 2 * n:HC + 2 * n + 2, :], in0=oT[:, 2 * n:2 * n + 2, :],
                                     scalar=m[:, 3:4], in1=rt[:, 2 * n:2 * n + 2, :], op0=ALU.mult, op1=ALU.mult)

    return Stage(tensor, scalar, vector)


def mixer_out(k, first, mixT, seed=None):
    out_done = k.sem("out_done")

    def tensor(pe):
        if seed is not None:
            residual(k, pe, seed)
        for n in range(first, first + 3):
            pe.wait_ge(k.slot_ready[n % SLOTS], k.use.mark[n])
        for t in range(ST):
            for half in range(2):
                for kk in range(DK):
                    w = slot(k, first + kk // 3)[:, (kk % 3) * D + half * 512:(kk % 3) * D + (half + 1) * 512]
                    last = pe.matmul(k.ps[:, 2 * t + half, :], mixT[:, kk, t * P:(t + 1) * P], w,
                                     start=(kk == 0 and seed is None), stop=(kk == DK - 1), skip_group_check=True)
                last.then_inc(out_done, 1)
        pe.drain().then_inc(k.slot_freed, 3)

    return out_done, tensor


def routing(k, first_out):
    nc = k.nc
    sem = k.sem
    out_done, out_tensor = mixer_out(k, first_out, k.hT)
    ms_ready, rt_root, h_ready = sem("ms_ready"), sem("ms_root"), sem("rt_h_ready")
    hT_bank, hT_put, logits_done = sem("hT_bank"), sem("hT_put"), sem("logits_done")
    exp_arg, aff_exp, aff_ready, aff_turned = sem("exp_arg"), sem("aff_exp"), sem("aff_ready"), sem("aff_turned")
    slots_ready, slots_turned, pick_ready, weight_ready = sem("slots_ready"), sem("slots_turned"), sem("pick_ready"), sem("weight_ready")
    weight_turned, weight_put, xin_done, xin_put = sem("weight_turned"), sem("weight_put"), sem("xin_done"), sem("xin_put")
    router_loaded = sem("router_loaded")
    h = area(k, 2048, 2048, t=ST)
    pick = area(k, 4096, 1024, t=ST)
    k.weightT = area(k, 8960, 1024, q=NG)
    k.xin = k.arena[:, HT0:HT0 + 4096].rearrange("p (k c) -> p k c", k=DK)
    wr = area(k, 6144, 128, k=DK)
    logit = area(k, 6272, 32, t=ST)
    aff = area(k, 6304, 32, t=ST)
    affT = area(k, 6336, 256)
    left = area(k, 6592, 256)
    count = area(k, 6848, 256)
    top = area(k, 7104, 32)
    slot_of = area(k, 7136, 32, t=ST)
    pickw = area(k, 7168, 1024, t=ST)
    onesr = area(k, 8192, 256)
    m = misc(k, 10, 30)

    def tensor(pe):
        out_tensor(pe)
        pe.wait_ge(h_ready, 2)
        for b in range(4):
            for j in range(4):
                kk, t = 2 * b + j // 2, j % 2
                last = pe.transpose(k.ps[:, 4 + b, j * P:(j + 1) * P], h[:, t, kk * P:(kk + 1) * P], k.ident)
            last.then_inc(hT_bank, 1)
        pe.wait_ge(router_loaded, 16)
        for kk in range(DK):
            pe.wait_ge(hT_put, DK + kk + 1)
            for t in range(ST):
                last = pe.matmul(k.ps[:, t, 0:NE], k.hT[:, kk, t * P:(t + 1) * P], wr[:, kk, :],
                                 start=(kk == 0), stop=(kk == DK - 1))
        last.then_inc(logits_done, 1)
        pe.wait_ge(aff_ready, 1)
        for t in range(ST):
            last = pe.transpose(k.ps[0:NE, 2, t * P:(t + 1) * P], aff[:, t, :], k.ident)
        last.then_inc(aff_turned, 1)
        pe.wait_ge(slots_ready, 1)
        for t in range(ST):
            last = pe.transpose(k.ps[:, 3, t * NE:(t + 1) * NE], count[0:NE, t * P:(t + 1) * P], k.ident[0:NE, 0:NE])
        last.then_inc(slots_turned, 1)
        pe.wait_ge(pick_ready, 2)
        for kk in range(DK):
            if kk >= 4:
                pe.wait_ge(xin_put, kk - 3)
            for t in range(ST):
                last = pe.matmul(k.ps[:, 4 + kk % 4, :], h[:, t, kk * P:(kk + 1) * P], pick[:, t, :],
                                 start=(t == 0), stop=(t == ST - 1))
            last.then_inc(xin_done, 1)
        pe.wait_ge(weight_ready, 2)
        for q in range(NG):
            for t in range(ST):
                last = pe.transpose(k.ps[:, q // 2, (q % 2) * S + t * P:(q % 2) * S + (t + 1) * P],
                                    pickw[:, t, q * P:(q + 1) * P], k.ident)
            if q % 2:
                last.then_inc(weight_turned, 1)

    def scalar(act):
        act.dma_start(wr, k.w_router[0].rearrange("(k p) e -> p k e", p=P)).then_inc(router_loaded, 16)
        act.wait_ge(ms_ready, 2)
        act.activation(m[:, 2:4], m[:, 2:4], ACT.Sqrt).then_inc(rt_root, 1)
        act.wait_ge(exp_arg, 1)
        for t in range(ST):
            act.activation(aff[:, t, :], logit[:, t, :], ACT.Exp, bias=m[:, 6 + t:7 + t],
                           accum_out=m[:, 8 + t:9 + t]).then_inc(aff_exp, 1)
        for kk in range(DK):
            act.wait_ge(xin_done, kk + 1)
            act.activation(k.xin[:, kk, :], k.ps[:, 4 + kk % 4, :], ACT.Copy,
                           scale=fix(k, "ffn_g")[:, kk:kk + 1]).then_inc(xin_put, 1)

    def vector(dve):
        step = k.vector_order.on(dve)
        for t in range(ST):
            for half in range(2):
                dve.wait_ge(out_done, 2 * t + half + 1)
                part = k.x[:, t, half * 512:(half + 1) * 512]
                step(dve.tensor_tensor(part, part, k.ps[:, 2 * t + half, :], ALU.add))
            step(dve.tensor_tensor_reduce(h[:, t, :], k.x[:, t, :], k.x[:, t, :], 1.0, 0.0, ALU.mult, ALU.add,
                                          m[:, t:t + 1]))
        dve.tensor_scalar(m[:, 2:4], m[:, 0:2], 1.0 / D, EPS, ALU.mult, ALU.add).then_inc(ms_ready, 1)
        dve.memset(onesr[0:NE, :], 1.0)
        dve.wait_ge(rt_root, 2)
        step(dve.reciprocal(m[:, 4:6], m[:, 2:4]))
        for t in range(ST):
            dve.tensor_scalar(h[:, t, :], k.x[:, t, :], m[:, 4 + t:5 + t], None, ALU.mult).then_inc(h_ready, 1)
        for kk in range(DK):
            dve.wait_ge(hT_bank, 4 + kk // 2 + 1)
            dve.tensor_scalar(k.hT[:, kk, :], k.ps[:, 4 + kk // 2, (kk % 2) * S:(kk % 2 + 1) * S],
                              fix(k, "ffn_g")[:, kk:kk + 1], None, ALU.mult).then_inc(hT_put, 1)
        dve.wait_ge(logits_done, 1)
        step(dve.tensor_copy(logit, k.ps[:, 0:ST, 0:NE]))
        step(dve.tensor_reduce(m[:, 6:8], logit, AX, ALU.max))
        dve.tensor_scalar(m[:, 6:8], m[:, 6:8], -1.0, None, ALU.mult).then_inc(exp_arg, 1)
        dve.wait_ge(aff_exp, 2)
        step(dve.reciprocal(m[:, 8:10], m[:, 8:10]))
        for t in range(ST):
            last = dve.tensor_scalar(aff[:, t, :], aff[:, t, :], m[:, 8 + t:9 + t], None, ALU.mult)
            if t < ST - 1:
                step(last)
        last.then_inc(aff_ready, 1)
        dve.wait_ge(aff_turned, 1)
        step(dve.tensor_copy(left[0:NE, :], k.ps[0:NE, 2, 0:S]))
        for r in range(CAP // 8):
            step(dve.max(top[0:NE, 8 * r:8 * r + 8], left[0:NE, :]))
            step(dve.match_replace(out=left[0:NE, :], in_to_replace=top[0:NE, 8 * r:8 * r + 8],
                                   in_values=left[0:NE, :], imm_value=-1.0))
        step(dve.tensor_scalar(left[0:NE, :], left[0:NE, :], 0.0, None, ALU.is_lt))
        step(dve.tensor_tensor_scan(count[0:NE, :], onesr[0:NE, :], left[0:NE, :], 0.0, ALU.mult, ALU.add))
        step(dve.tensor_tensor(count[0:NE, :], count[0:NE, :], left[0:NE, :], ALU.mult))
        dve.tensor_scalar(count[0:NE, :], count[0:NE, :], 1.0, None, ALU.subtract).then_inc(slots_ready, 1)
        dve.wait_ge(slots_turned, 1)
        step(dve.tensor_copy(slot_of, k.ps[:, 3, 0:ST * NE].rearrange("p (t e) -> p t e", t=ST)))
        for t in range(ST):
            dve.tensor_tensor(pick[:, t, :].rearrange("p (e c) -> p e c", e=NE),
                              slot_of[:, t, :].unsqueeze(2).to_broadcast([P, NE, CAP]),
                              fix(k, "slot_no").unsqueeze(1).to_broadcast([P, NE, CAP]),
                              ALU.is_equal).then_inc(pick_ready, 1)
        dve.wait_ge(pick_ready, 2)
        for t in range(ST):
            dve.tensor_tensor(pickw[:, t, :].rearrange("p (e c) -> p e c", e=NE),
                              pick[:, t, :].rearrange("p (e c) -> p e c", e=NE),
                              aff[:, t, :].unsqueeze(2).to_broadcast([P, NE, CAP]), ALU.mult).then_inc(weight_ready, 1)
        for q in range(NG):
            dve.wait_ge(weight_turned, q // 2 + 1)
            dve.tensor_copy(k.weightT[:, q, :], k.ps[:, q // 2, (q % 2) * S:(q % 2 + 1) * S])

    return Stage(tensor, scalar, vector)


def experts(k, base, w_gate, w_up, w_down, final_norm_g):
    nc = k.nc
    sem = k.sem
    x_ready, gate_up_done, silu_put, hidden_put = sem("ex_x_ready"), sem("gate_up_done"), sem("silu_put"), sem("hidden_put")
    turned, hidT_put, hidT_rest_put, down_done, y_put = sem("ex_turned"), sem("hidT_put"), sem("hidT_rest_put"), sem("down_done"), sem("y_put")
    xe = area(k, 6144, 256, k=DK)
    silu = area(k, 6400, FG)
    hidden = area(k, 6400 + FG, FG)
    hidT = area(k, 6400 + 2 * FG, (FT + 1) * P, m=FT + 1)
    k.final_g = area(k, 9984, D)
    k.Y = area(k, 2048, NG * D, q=NG)
    per = 3 * DK
    dmas = [1] * (2 * DK) + [1, 2] * NG
    mark = [k.use.landing(base + n, dmas[n]) for n in range(per)]
    again = [k.use.landing(base + per + n, dmas[n]) - mark[n] for n in range(per)]
    for e in range(2, NE):
        for n in range(per):
            k.use.landing(base + per * e + n, dmas[n])

    def load(sync):
        with sync.Fori(0, NE) as e:
            for n in range(per):
                s = slot(k, base + n)
                ready = k.slot_ready[(base + n) % SLOTS]
                sync.wait_ge(k.slot_freed, e * per + (base + n - SLOTS + 1))
                if n < 2 * DK:
                    w, kk = (w_gate, w_up)[n % 2], n // 2
                    sync.dma_start(s[:, 0:FF], w[0, bass.ds(e, 1), kk * P:(kk + 1) * P, :].rearrange("e p f -> p (e f)")).then_inc(ready, 16)
                else:
                    g, part = (n - 2 * DK) // 2, n % 2
                    rows = FG * g + 3 * P * part
                    whole = 3 - part
                    sync.dma_start(s[:, 0:whole * D].rearrange("p (m d) -> p m d", m=whole),
                                   w_down[0, bass.ds(e, 1), rows:rows + whole * P, :].rearrange("e (m p) d -> p (e m) d", p=P)).then_inc(ready, 16)
                    if part:
                        sync.dma_start(s[0:FR, 2 * D:3 * D],
                                       w_down[0, bass.ds(e, 1), rows + 2 * P:rows + 2 * P + FR, :].rearrange("e p d -> p (e d)")).then_inc(ready, 16)

    def gpsimd(pool):
        with pool.Fori(0, NE) as e:
            pool.wait_ge(gate_up_done, e + 1)
            pool.tensor_copy(xe, k.xin[:, :, bass.ds(e * CAP, CAP)]).then_inc(x_ready, 1)

    def tensor(pe):
        pe.sem_inc(gate_up_done, 1)
        def expert(e, last_one=False):
            pe.wait_ge(x_ready, e + 1)
            for kk in range(DK):
                for w in range(2):
                    n = 2 * kk + w
                    pe.wait_ge(k.slot_ready[(base + n) % SLOTS], e * again[n] + mark[n])
                    for half in range(2):
                        for g in range(NG):
                            last = pe.matmul(k.ps[32 * g:32 * g + CAP, 2 * w + half, 0:FH], xe[:, kk, :],
                                             slot(k, base + n)[:, g * FG + half * FH:g * FG + (half + 1) * FH],
                                             start=(kk == 0), stop=(kk == DK - 1))
                    if n < 2 * DK - 1:
                        last.then_inc(k.slot_freed, 1)
            last.then_inc(gate_up_done, 1)
            pe.wait_ge(hidden_put, e + 1)
            for m in range(FT + 1):
                w = P if m < FT else FR
                last = pe.transpose(k.ps[0:w, 4 + m // 4, (m % 4) * P:(m % 4 + 1) * P], hidden[:, m * P:m * P + w], k.ident)
                if m == 0:
                    last.then_inc(k.slot_freed, 1)
            last.then_inc(turned, 1)
            pe.wait_ge(hidT_put, e + 1)
            pe.wait_ge(hidT_rest_put, e + 1)
            pe.wait_ge(y_put, e + 1)
            if last_one:
                weighted_sums(k, pe, range(NG - 1))
            for g in range(NG):
                for m in range(FT + 1):
                    n = 2 * DK + 2 * g + m // 3
                    if m % 3 == 0:
                        pe.wait_ge(k.slot_ready[(base + n) % SLOTS], e * again[n] + mark[n])
                    w = P if m < FT else FR
                    for j in range(NG):
                        last = pe.matmul(k.ps[32 * j:32 * j + CAP, 6, 0:256], hidT[0:w, m, 32 * g:32 * g + CAP],
                                         slot(k, base + n)[0:w, (m % 3) * D + j * 256:(m % 3) * D + (j + 1) * 256],
                                         start=(g == 0 and m == 0), stop=(g == NG - 1 and m == FT))
                    if m % 3 == 2 and not (g == NG - 1 and m == FT):
                        last.then_inc(k.slot_freed, 1)
            last.then_inc(down_done, 1)
            pe.drain().then_inc(k.slot_freed, 1)

        with pe.Fori(0, NE - 1) as e:
            expert(e)
        expert(NE - 1, last_one=True)

    def scalar(act):
        act.dma_start(k.final_g, final_norm_g.partition_broadcast(P)).then_inc(sem("g_loaded"), 16)
        with act.Fori(0, NE) as e:
            act.wait_ge(gate_up_done, e + 2)
            for half in range(2):
                act.activation(silu[:, half * FH:(half + 1) * FH], k.ps[:, half, 0:FH], ACT.Silu).then_inc(silu_put, 1)
            act.wait_ge(turned, e + 1)
            act.activation(hidT[:, 0:4, :], k.ps[:, 4, :], ACT.Copy).then_inc(hidT_put, 1)

    def vector(dve):
        dve.sem_inc(y_put, 1)
        with dve.Fori(0, NE // NG) as four:
            for i in range(NG):
                for half in range(2):
                    dve.wait_ge(silu_put, four * (2 * NG) + (2 * i + half + 1))
                    last = dve.tensor_tensor(hidden[:, half * FH:(half + 1) * FH], silu[:, half * FH:(half + 1) * FH],
                                             k.ps[:, 2 + half, 0:FH], ALU.mult)
                last.then_inc(hidden_put, 1)
                dve.wait_ge(turned, four * NG + (i + 1))
                dve.tensor_copy(hidT[:, 4, :], k.ps[:, 5, 0:P])
                dve.tensor_copy(hidT[0:FR, 5, :], k.ps[0:FR, 5, P:2 * P]).then_inc(hidT_rest_put, 1)
                dve.wait_ge(down_done, four * NG + (i + 1))
                for g in range(NG):
                    last = dve.tensor_copy(k.Y[CAP * i:CAP * (i + 1), bass.ds(four, 1), g * 256:(g + 1) * 256]
                                           .rearrange("p q d -> p (q d)"), k.ps[32 * g:32 * g + CAP, 6, 0:256])
                last.then_inc(y_put, 1)

    return load, Stage(tensor, scalar, vector, gpsimd)


def weighted_sums(k, pe, parts, done=None):
    for t in range(ST):
        for half in range(2):
            for q in parts:
                last = pe.matmul(k.ps[:, 2 * t + half, :], k.weightT[:, q, t * P:(t + 1) * P],
                                 k.Y[:, q, half * 512:(half + 1) * 512], start=(q == 0), stop=(q == NG - 1),
                                 skip_group_check=True)
            if done:
                last.then_inc(done, 1)


class Turn:

    def __init__(self, k):
        self.k, self.x_put, self.bank = k, k.sem("x_put"), k.sem("x_turned")

    def tensor(self, pe):
        k = self.k
        pe.wait_ge(self.x_put, 2 * ST)
        for b in range(4):
            for j in range(4):
                kk, t = 2 * b + j // 2, j % 2
                last = pe.transpose(k.ps[:, 4 + b, j * P:(j + 1) * P], k.x[:, t, kk * P:(kk + 1) * P], k.ident)
            last.then_inc(self.bank, 1)

    def copy(self, engine, write, banks):
        k = self.k
        for b in banks:
            engine.wait_ge(self.bank, b + 1)
            write(k.hT[:, 2 * b:2 * b + 2, :], k.ps[:, 4 + b, :].rearrange("p (k s) -> p k s", k=2))

    def scalar(self, act):
        self.copy(act, lambda out, src: act.activation(out, src, ACT.Copy), (1, 3))

    def vector(self, dve):
        self.copy(dve, lambda out, src: dve.tensor_copy(out, src), (0, 2))


def experts_combine(k):
    sem = k.sem
    g_loaded, sum_done = sem("g_loaded"), sem("sum_done")
    ms_ready, root, y_put = sem("ms_ready"), sem("ms_root"), sem("y_put")
    g = k.final_g
    sq = area(k, 7168, 1024)
    m = misc(k, 10, 30)
    turn = Turn(k)

    def tensor(pe):
        pe.wait_ge(y_put, NE + 1)
        weighted_sums(k, pe, [NG - 1], sum_done)
        turn.tensor(pe)

    def scalar(act):
        act.wait_ge(ms_ready, 3)
        act.activation(m[:, 2:4], m[:, 2:4], ACT.Sqrt).then_inc(root, 1)
        turn.scalar(act)

    def vector(dve):
        step = k.vector_order.on(dve)
        for t in range(ST):
            for half in range(2):
                dve.wait_ge(sum_done, 2 * t + half + 1)
                part = k.x[:, t, half * 512:(half + 1) * 512]
                step(dve.tensor_tensor(part, part, k.ps[:, 2 * t + half, :], ALU.add))
            step(dve.tensor_tensor_reduce(sq, k.x[:, t, :], k.x[:, t, :], 1.0, 0.0, ALU.mult, ALU.add, m[:, t:t + 1]))
        dve.tensor_scalar(m[:, 2:4], m[:, 0:2], 1.0 / D, EPS, ALU.mult, ALU.add).then_inc(ms_ready, 1)
        dve.wait_ge(root, 3)
        step(dve.reciprocal(m[:, 4:6], m[:, 2:4]))
        dve.wait_ge(g_loaded, 16)
        for t in range(ST):
            dve.scalar_tensor_tensor(out=k.x[:, t, :], in0=k.x[:, t, :], scalar=m[:, 4 + t:5 + t], in1=g,
                                     op0=ALU.mult, op1=ALU.mult).then_inc(turn.x_put, 2)
        turn.vector(dve)

    return Stage(tensor, scalar, vector)


class NormAndTurn:

    def __init__(self, k, sums_done, sums_before, factor):
        sem = k.sem
        self.k, self.sums_done, self.sums_before, self.factor = k, sums_done, sums_before, factor
        self.u = k.norms
        k.norms += 1
        self.var_ready, self.root, self.ab_ready = sem("ln_var_ready"), sem("ln_root"), sem("ln_ab_ready")
        self.normed = (sem("ln_normed_0"), sem("ln_normed_1"))
        self.turned = sem("ln_turned")
        self.m = misc(k, 0, 36)

    def of(self, t, a, w=1):
        return self.m[:, 18 * t + a:18 * t + a + w]

    def tensor(self, pe):
        k = self.k
        for t in range(ST):
            for half in range(2):
                pe.wait_ge(self.normed[t], 2 * self.u + half + 1)
                for j in range(4):
                    kk = 4 * half + j
                    last = pe.transpose(k.ps[:, 4 + 2 * t + half, j * P:(j + 1) * P], k.x[:, t, kk * P:(kk + 1) * P], k.ident)
                last.then_inc(self.turned, 1)

    def copy(self, engine, write, banks):
        k = self.k
        for t, half in banks:
            engine.wait_ge(self.turned, 2 * ST * self.u + 2 * t + half + 1)
            for j in range(4):
                kk = 4 * half + j
                g, b = (fix(k, n)[:, DK * self.u + kk:DK * self.u + kk + 1] for n in ("ln_g", "ln_b"))
                write(k.hT[:, kk, t * P:(t + 1) * P], k.ps[:, 4 + 2 * t + half, j * P:(j + 1) * P], g, b)

    def scalar(self, act):
        k = self.k
        for t in range(ST):
            act.wait_ge(self.var_ready, ST * self.u + t + 1)
            act.activation(self.of(t, 14), self.of(t, 14), ACT.Sqrt).then_inc(self.root, 1)
            if t == 0:
                act.wait_ge(self.ab_ready, self.u + 1)
                for half in range(2):
                    act.activation(k.x[:, 0, half * 512:(half + 1) * 512], k.ps[:, half, :], ACT.Identity,
                                   scale=self.of(0, 15), bias=self.of(0, 16)).then_inc(self.normed[0], 1)
        self.copy(act, lambda out, src, g, b: act.activation(out, src, ACT.Identity, scale=g, bias=b),
                  [(0, 0), (0, 1), (1, 0)])

    def vector(self, dve):
        k = self.k
        step = k.vector_order.on(dve)

        def statistics(t):
            for half in range(2):
                dve.wait_ge(self.sums_done, self.sums_before + 2 * t + half + 1)
                step(dve.bn_stats(self.of(t, 6 * half, 6), k.ps[:, 2 * t + half, :]))
            step(dve.bn_aggr(self.of(t, 12, 2), self.of(t, 0, 12)))
            dve.tensor_scalar(self.of(t, 14), self.of(t, 13), self.factor ** 2, LN_EPS, ALU.mult,
                              ALU.add).then_inc(self.var_ready, 1)

        def scale(t):
            dve.wait_ge(self.root, ST * self.u + t + 1)
            step(dve.reciprocal(self.of(t, 14), self.of(t, 14)))
            step(dve.tensor_scalar(self.of(t, 15), self.of(t, 14), self.factor, None, ALU.mult))
            return dve.tensor_scalar(self.of(t, 16), self.of(t, 12), self.of(t, 15), -1.0, ALU.mult, ALU.mult)

        statistics(0)
        scale(0).then_inc(self.ab_ready, 1)
        statistics(1)
        step(scale(1))
        for half in range(2):
            dve.tensor_scalar(k.x[:, 1, half * 512:(half + 1) * 512], k.ps[:, 2 + half, :], self.of(1, 15), self.of(1, 16),
                              ALU.mult, ALU.add).then_inc(self.normed[1], 1)
        self.copy(dve, lambda out, src, g, b: dve.tensor_scalar(out, src, g, b, ALU.mult, ALU.add), [(1, 1)])


def residual(k, pe, seed):
    for t in range(ST):
        for kk in range(DK):
            pe.matmul(k.ps[:, 2 * t + kk // 4, (kk % 4) * P:(kk % 4 + 1) * P], k.hT[:, kk, t * P:(t + 1) * P], seed,
                      start=(kk % 4 == 0), stop=False, skip_group_check=True)


FC = FF // P


def ffn_weights(k, base, w):
    loads = []
    for c in range(FC):
        k.use.landing(base + c)
        loads.append((base + c, [(slot(k, base + c), w[c])]))
    return loads


def ffn(k, u, base):
    sem = k.sem
    (h_high, h_split, w13_high, w2_high, w13_split, w2_split, pair_done, silu_put, hidden_put,
     hidden_high, hidden_split, sums_done) = (
        sem(f"ffn_{s}") for s in ("h_high", "h_split", "w13_high", "w2_high", "w13_split", "w2_split", "pair_done", "silu_put", "hidden_put", "hidden_high", "hidden_split",
                                  "sums_done"))
    norm = NormAndTurn(k, sums_done, 2 * ST * u, 0.5)
    silu = area(k, 0, 2 * S, n=2)
    hidden = area(k, 2 * S, 2 * S, n=2)
    assert R0 + 3072 <= ARENA - PARTS
    before = FC * u
    TURNS = FC // SLOTS

    def landed(c, e):
        return e * 16 + k.use.mark[base + c]

    def raw(c, w):
        return slot(k, base + c)[:, w * D:(w + 1) * D].rearrange("p (k f) -> p k f", k=DK)

    def tensor(pe):
        residual(k, pe, fix(k, "seed2"))

        def pair(c, e=0):
            b = c % 2
            for w in range(2):
                pe.wait_ge(w13_split, e * (2 * SLOTS) + (2 * (before + c) + w + 1))
                for kk in range(DK):
                    if c == 0 and w == 0:
                        pe.wait_ge(h_split, DK * u + kk + 1)
                    for n, (i, j) in enumerate(((0, 0), (0, 1), (1, 0))):
                        last = pe.matmul(k.ps[:, 4 + c % 4, w * S:(w + 1) * S], k.w13[:, b, w, i, kk, :],
                                         k.hsplit[:, j, kk, :], start=(kk == 0 and n == 0), stop=(kk == DK - 1 and n == 2))
            last.then_inc(pair_done, 1)

        def down(c, e=0):
            b = c % 2
            pe.wait_ge(w2_split, e * SLOTS + (before + c + 1))
            pe.wait_ge(hidden_split, e * SLOTS + (before + c + 1))
            for t in range(ST):
                for i, j in ((0, 0), (0, 1), (1, 0)):
                    for half in range(2):
                        last = pe.matmul(k.ps[:, 2 * t + half, :], k.hidsplit[:, b, i, t * P:(t + 1) * P],
                                         k.w2[:, b, j, half * 512:(half + 1) * 512], start=False, stop=False,
                                         skip_group_check=True)
                if c == FC - 1 and t == 0:
                    last.then_inc(sums_done, 2)
            last.then_inc(k.slot_freed, 1)

        pair(0)
        with pe.Fori(0, TURNS) as e:
            for c in range(SLOTS):
                pair(c + 1, e)
                down(c, e)
        for c in range(TURNS * SLOTS, FC):
            if c + 1 < FC:
                pair(c + 1)
            down(c)
        pe.drain().then_inc(sums_done, 2)
        norm.tensor(pe)

    def scalar(act):
        def pair_high(c, w, e=0):
            if w == 0:
                act.wait_ge(k.slot_ready[(base + c) % SLOTS], landed(c, e))
            act.activation(k.w13[:, c % 2, w, 0], raw(c, w), ACT.Copy).then_inc(w13_high, 1)

        def down_high(c, e=0):
            if c:
                act.wait_ge(k.slot_freed, e * SLOTS + (base + c - 1))
            act.activation(k.w2[:, c % 2, 0], slot(k, base + c)[:, 2 * D:3 * D], ACT.Copy).then_inc(w2_high, 1)

        def chunk(c, e=0):
            act.wait_ge(pair_done, e * SLOTS + (before + c + 1))
            act.activation(silu[:, c % 2, :], k.ps[:, 4 + c % 4, 0:S], ACT.Silu).then_inc(silu_put, 1)
            if c + 2 < FC:
                pair_high(c + 2, 0, e)
            act.wait_ge(hidden_put, e * SLOTS + (before + c + 1))
            act.activation(k.hidsplit[:, c % 2, 0], hidden[:, c % 2, :], ACT.Copy).then_inc(hidden_high, 1)
            if c + 2 < FC:
                pair_high(c + 2, 1, e)
            if c + 1 < FC:
                down_high(c + 1, e)

        for kk in range(DK):
            act.activation(k.hsplit[:, 0, kk, :], k.hT[:, kk, :], ACT.Copy).then_inc(h_high, 1)
            if kk == 0:
                pair_high(0, 0)
                pair_high(0, 1)
        down_high(0)
        pair_high(1, 0)
        pair_high(1, 1)
        with act.Fori(0, TURNS) as e:
            for c in range(SLOTS):
                chunk(c, e)
        for c in range(TURNS * SLOTS, FC):
            chunk(c)
        norm.scalar(act)

    def vector(dve):
        def pair_low(c, w, e=0):
            dve.wait_ge(w13_high, e * (2 * SLOTS) + (2 * (before + c) + w + 1))
            dve.tensor_tensor(k.w13[:, c % 2, w, 1], raw(c, w), k.w13[:, c % 2, w, 0].bitcast(F32),
                              ALU.subtract).then_inc(w13_split, 1)

        def down_low(c, e=0):
            dve.wait_ge(w2_high, e * SLOTS + (before + c + 1))
            dve.tensor_tensor(k.w2[:, c % 2, 1], slot(k, base + c)[:, 2 * D:3 * D], k.w2[:, c % 2, 0].bitcast(F32),
                              ALU.subtract).then_inc(w2_split, 1)

        def chunk(c, e=0):
            dve.wait_ge(silu_put, e * SLOTS + (before + c + 1))
            dve.tensor_tensor(hidden[:, c % 2, :], silu[:, c % 2, :], k.ps[:, 4 + c % 4, S:2 * S],
                              ALU.mult).then_inc(hidden_put, 1)
            if c + 2 < FC:
                pair_low(c + 2, 0, e)
            dve.wait_ge(hidden_high, e * SLOTS + (before + c + 1))
            dve.tensor_tensor(k.hidsplit[:, c % 2, 1], hidden[:, c % 2, :], k.hidsplit[:, c % 2, 0].bitcast(F32),
                              ALU.subtract).then_inc(hidden_split, 1)
            if c + 2 < FC:
                pair_low(c + 2, 1, e)
            if c + 1 < FC:
                down_low(c + 1, e)

        for kk in range(DK):
            dve.wait_ge(h_high, DK * u + kk + 1)
            dve.tensor_tensor(k.hsplit[:, 1, kk, :], k.hT[:, kk, :], k.hsplit[:, 0, kk, :].bitcast(F32),
                              ALU.subtract).then_inc(h_split, 1)
            if kk == 0:
                pair_low(0, 0)
                pair_low(0, 1)
        down_low(0)
        pair_low(1, 0)
        pair_low(1, 1)
        with dve.Fori(0, TURNS) as e:
            for c in range(SLOTS):
                chunk(c, e)
        for c in range(TURNS * SLOTS, FC):
            chunk(c)
        norm.vector(dve)

    return Stage(tensor, scalar, vector)


def conv_s5(k, base, s5_params):
    sem = k.sem
    n_glu, n_out = base + 8, base + 9
    names = ("gate_put", "param_loaded", "exp1", "exp_arg", "mag_put", "bc_ready", "bc_turned", "bc_put", "input_done", "v_parts", "v_put", "w_put", "s_put", "s_put_dve", "y_done",
             "gelu_arg", "z_put", "glu_done", "sig_put", "yb_put")
    q = {s: sem(f"s5_{s}") for s in names}
    B = {"column_done": 22, "copied": 8, "sin_arg": 2, "sin_done": 2}
    q.update({s: sem(s) for s in B})
    mixT = area(k, 0, 2048, c=DK)
    u = area(k, 2048, 1024, q=4)
    z = area(k, 3072, 1024, q=4)
    par = area(k, 4096, 1072)
    re_im = par[:, 0:48].rearrange("p (n i) -> p n i", n=3)
    b_in = par[:, 48:560].rearrange("p (n i c) -> p n i c", n=2, i=16)
    c_in = par[:, 560:1072].rearrange("p (n q s) -> p n q s", n=2, q=4)
    bT = area(k, 5168, 1024, n=2, q=4)
    cT = area(k, 6192, 1024, n=2, q=4)
    small = area(k, 7216, 16 * 16, n=16)
    wide = area(k, 7472, 1024)
    cosT, sinT = work(k, 0, 4096, i=16), work(k, 4096, 4096, i=16)
    m1, m2 = work(k, 8192, 1024), work(k, 9216, 1024)
    prods = [work(k, 8192, 2048, n=4, i=2), work(k, 10240, 2048, n=4, i=2), area(k, 8704, 2048, n=4, i=2)]
    conv_w = fix(k, "conv_w2")

    def phases(j):
        return cosT[:, 2 * j:2 * j + 2, :], sinT[:, 2 * j:2 * j + 2, :]

    ORDER = [c for j in range(4) for c in (j, 8 + j, 4 + j)] + [12, 13, 14, 15]

    def tensor(pe):
        for n in range(base, base + 8):
            pe.wait_ge(k.slot_ready[n % SLOTS], k.use.mark[n])
        for i, c in enumerate(ORDER):
            if i >= 6:
                pe.wait_ge(q["copied"], B["copied"] + i - 5)
            for kk in range(DK):
                last = pe.matmul(k.ps[:, i % 6, 0:S], slot(k, base + kk)[:, c * P:(c + 1) * P], k.hT[:, kk, :],
                                 start=(kk == 0), stop=(kk == DK - 1))
            last.then_inc(q["column_done"], 1)
        pe.drain().then_inc(k.slot_freed, 8)
        for n in range(4):
            pe.wait_ge(q["bc_ready"], n + 1)
            if n:
                pe.wait_ge(q["bc_put"], n)
            for j in range(4):
                last = pe.transpose(k.ps[:, 6, j * P:(j + 1) * P], wide[:, 0:512][:, j * P:(j + 1) * P] if n % 2 == 0
                                    else wide[:, 512:1024][:, j * P:(j + 1) * P], k.ident)
            last.then_inc(q["bc_turned"], 1)
        pe.wait_ge(q["bc_put"], 4)
        pe.wait_ge(q["copied"], B["copied"] + 16)

        def states(j):
            for i in range(2):
                tile = 2 * j + i
                r = 32 * (tile % 4)
                for n in range(2):
                    last = pe.matmul(k.ps[:, 2 * (j % 2) + i, n * S:(n + 1) * S], bT[r:r + 32, n, tile // 4, :],
                                     u[r:r + 32, tile // 4, :], start=True, stop=True)
            last.then_inc(q["input_done"], 1)

        def outputs(j):
            pe.wait_ge(q["s_put"], 2 * (j + 1))
            pe.wait_ge(q["s_put_dve"], 2 * (j + 1))
            for i in range(2):
                tile = 2 * j + i
                r = 32 * (tile % 4)
                for at, (n, part) in enumerate(((0, 1), (0, 3), (1, 0), (1, 2))):
                    last = pe.matmul(k.ps[r:r + 32, 4 + tile // 4, 0:S], cT[:, n, tile // 4, r:r + 32],
                                     prods[j % 3][:, part, i, :], start=(at == 0), stop=(at == 3))
            last.then_inc(q["y_done"], 1)

        states(0)
        states(1)
        for j in range(8):
            if j < 6:
                pe.wait_ge(q["v_parts"], 4 * (j + 1))
                states(j + 2)
            outputs(j)
        pe.wait_ge(k.slot_ready[n_glu % SLOTS], k.use.mark[n_glu])
        pe.wait_ge(q["z_put"], 4)
        for c in range(4):
            for kk in range(4):
                last = pe.matmul(k.ps[:, c, 0:S], slot(k, n_glu)[:, kk * CC + c * P:kk * CC + (c + 1) * P], z[:, kk, :],
                                 start=(kk == 0), stop=(kk == 3))
            last.then_inc(q["glu_done"], 1)
        pe.drain().then_inc(k.slot_freed, 1)
        pe.wait_ge(q["yb_put"], 4)
        out_tensor(pe)
        norm.tensor(pe)

    out_done, out_tensor = mixer_out(k, n_out, mixT, fix(k, "seed1"))
    norm = NormAndTurn(k, out_done, 2 * ST, 1.0)

    def scalar(act):
        act.dma_start(par, s5_params).then_inc(q["param_loaded"], 16)
        act.wait_ge(q["param_loaded"], 16)
        act.activation(re_im[:, 2, :], re_im[:, 2, :], ACT.Exp).then_inc(q["exp1"], 1)
        act.wait_ge(q["exp_arg"], 1)
        act.activation(small[:, 2, :], small[:, 2, :], ACT.Exp).then_inc(q["mag_put"], 1)
        act.wait_ge(q["sin_arg"], B["sin_arg"] + 1)
        act.activation(small[:, 4, :], small[:, 4, :], ACT.Sin).then_inc(q["sin_done"], 1)
        act.activation(small[:, 5, :], small[:, 5, :], ACT.Sin).then_inc(q["sin_done"], 1)
        for i, c in enumerate(ORDER):
            act.wait_ge(q["column_done"], B["column_done"] + i + 1)
            if c >= 12:
                act.activation(u[:, c - 12, :], k.ps[:, i % 6, 0:S], ACT.Copy).then_inc(q["copied"], 1)
            else:
                if i >= 3:
                    act.wait_ge(q["gate_put"], i // 3)
                act.activation(z[:, i % 3, :], k.ps[:, i % 6, 0:S], ACT.Copy).then_inc(q["copied"], 1)
        for n in range(4):
            act.wait_ge(q["bc_turned"], n + 1)
            act.activation((bT if n < 2 else cT)[:, n % 2], k.ps[:, 6, :].rearrange("p (q c) -> p q c", q=4),
                           ACT.Copy).then_inc(q["bc_put"], 1)
        for c in range(4):
            act.wait_ge(q["gelu_arg"], c + 1)
            act.activation(z[:, c, :], z[:, c, :], ACT.Gelu_apprx_tanh).then_inc(q["z_put"], 1)
        for c in range(4):
            act.wait_ge(q["glu_done"], c + 1)
            act.activation(u[:, c, :], k.ps[:, c, 0:S], ACT.Sigmoid, bias=fix(k, "b_glu")[:, c:c + 1]).then_inc(q["sig_put"], 1)
        norm.scalar(act)

    def vector(dve):
        step = k.vector_order.on(dve)

        def sm(i):
            return small[:, i, :]

        lr, li, dt = re_im[:, 0, :], re_im[:, 1, :], re_im[:, 2, :]
        dve.wait_ge(q["param_loaded"], 16)
        step(dve.tensor_scalar(lr, lr, -1e-4, None, ALU.min))
        dve.wait_ge(q["exp1"], 1)
        dve.tensor_tensor(sm(2), lr, dt, ALU.mult).then_inc(q["exp_arg"], 1)
        step(dve.tensor_tensor(sm(3), li, dt, ALU.mult))
        step(range_reduce(step, dve, sm(4), sm(3), sm(5)))
        step(dve.scalar_tensor_tensor(out=sm(5), in0=sm(4), scalar=-1.0, in1=sm(4), op0=ALU.mult, op1=ALU.max))
        dve.tensor_scalar(sm(5), sm(5), -1.0, math.pi / 2, ALU.mult, ALU.add).then_inc(q["sin_arg"], 1)
        step(dve.tensor_tensor(sm(6), lr, lr, ALU.mult))
        step(dve.tensor_tensor(sm(7), li, li, ALU.mult))
        step(dve.tensor_tensor(sm(6), sm(6), sm(7), ALU.add))
        step(dve.reciprocal(sm(6), sm(6)))
        dve.wait_ge(q["mag_put"], 1)
        dve.wait_ge(q["sin_done"], B["sin_done"] + 2)
        step(dve.tensor_tensor(sm(7), sm(2), sm(5), ALU.mult))
        step(dve.tensor_scalar(sm(7), sm(7), 1.0, None, ALU.subtract))
        step(dve.tensor_tensor(sm(8), sm(2), sm(4), ALU.mult))
        step(dve.tensor_tensor(sm(9), sm(7), lr, ALU.mult))
        step(dve.tensor_tensor(sm(10), sm(8), li, ALU.mult))
        step(dve.tensor_tensor(sm(9), sm(9), sm(10), ALU.add))
        step(dve.tensor_tensor(sm(9), sm(9), sm(6), ALU.mult))
        step(dve.tensor_tensor(sm(10), sm(8), lr, ALU.mult))
        step(dve.tensor_tensor(sm(11), sm(7), li, ALU.mult))
        step(dve.tensor_tensor(sm(10), sm(10), sm(11), ALU.subtract))
        step(dve.tensor_tensor(sm(10), sm(10), sm(6), ALU.mult))

        fre, fim = (sm(i).unsqueeze(2).to_broadcast([P, 16, S5C]) for i in (9, 10))
        t1 = wide[:, 0:256].rearrange("p (i c) -> p i c", i=16)
        t2 = wide[:, 256:512].rearrange("p (i c) -> p i c", i=16)
        t3 = z[:, 3, :].rearrange("p (i c) -> p i c", i=16)
        t4 = mixT[:, 7, :].rearrange("p (i c) -> p i c", i=16)
        step(dve.tensor_tensor(t1, b_in[:, 0], fre, ALU.mult))
        step(dve.tensor_tensor(t2, b_in[:, 1], fim, ALU.mult))
        step(dve.tensor_tensor(t3, t1, t2, ALU.subtract))
        step(dve.tensor_tensor(t1, b_in[:, 1], fre, ALU.mult))
        step(dve.tensor_tensor(t2, b_in[:, 0], fim, ALU.mult))
        step(dve.tensor_tensor(t4, t1, t2, ALU.add))
        mb, mc = fix(k, "mask_b"), fix(k, "mask_c")
        for n, src in enumerate((t3, t4)):
            out = wide[:, 512 * n:512 * n + 512].rearrange("p (i g c) -> p i g c", i=16, g=2)
            for g in range(2):
                last = dve.tensor_scalar(out[:, :, g, :], src, mb[:, g:g + 1], None, ALU.mult)
                if g == 0:
                    step(last)
            last.then_inc(q["bc_ready"], 1)

        def c_part(n):
            dve.wait_ge(q["bc_turned"], n + 1)
            out = wide[:, 512 * n:512 * n + 512].rearrange("p (q g s) -> p q g s", q=4, g=2)
            for g in range(2):
                last = dve.tensor_scalar(out[:, :, g, :], c_in[:, n], mc[:, g:g + 1], -1.0 if n else 1.0, ALU.mult, ALU.mult)
                if g == 0:
                    step(last)
            last.then_inc(q["bc_ready"], 1)

        def gate(j):
            dve.wait_ge(q["copied"], B["copied"] + 3 * j + 3)
            h, gc, gb, y = z[:, 0, :], z[:, 1, :], z[:, 2, :], mixT[:, j, :]
            step(dve.tensor_tensor(h, h, gc, ALU.mult))
            step(dve.tensor_scalar(y, h, conv_w[:, 8 + j:9 + j], None, ALU.mult))
            step(dve.scalar_tensor_tensor(out=y[:, 1:S], in0=h[:, 0:S - 1], scalar=conv_w[:, 4 + j:5 + j], in1=y[:, 1:S],
                                          op0=ALU.mult, op1=ALU.add))
            step(dve.scalar_tensor_tensor(out=y[:, 2:S], in0=h[:, 0:S - 2], scalar=conv_w[:, j:j + 1], in1=y[:, 2:S],
                                          op0=ALU.mult, op1=ALU.add))
            dve.tensor_tensor(y, y, gb, ALU.mult).then_inc(q["gate_put"], 1)

        step(dve.memset(cosT[:, :, 0:1], 1.0))
        step(dve.memset(sinT[:, :, 0:1], 0.0))
        step(dve.tensor_copy(sm(12), sm(5)))
        step(dve.tensor_copy(sm(13), sm(4)))
        n = 1
        while n < S:
            pr, pi = (sm(i).unsqueeze(2).to_broadcast([P, 16, n]) for i in (12, 13))
            for h in range(0, 16, 16 if n <= 64 else 8):
                hh = slice(h, h + (16 if n <= 64 else 8))
                size = (16 if n <= 64 else 8) * n
                a1 = m1[:, 0:size].rearrange("p (i t) -> p i t", t=n)
                a2 = m2[:, 0:size].rearrange("p (i t) -> p i t", t=n)
                step(dve.tensor_tensor(a1, cosT[:, hh, 0:n], pr[:, hh], ALU.mult))
                step(dve.tensor_tensor(a2, sinT[:, hh, 0:n], pi[:, hh], ALU.mult))
                step(dve.tensor_tensor(cosT[:, hh, n:2 * n], a1, a2, ALU.subtract))
                step(dve.tensor_tensor(a1, cosT[:, hh, 0:n], pi[:, hh], ALU.mult))
                step(dve.tensor_tensor(a2, sinT[:, hh, 0:n], pr[:, hh], ALU.mult))
                step(dve.tensor_tensor(sinT[:, hh, n:2 * n], a1, a2, ALU.add))
            if n in (16, 64):
                gate((16, 64).index(n))
            n *= 2
            if n < S:
                step(dve.tensor_tensor(sm(14), sm(12), sm(12), ALU.mult))
                step(dve.tensor_tensor(sm(15), sm(13), sm(13), ALU.mult))
                step(dve.scalar_tensor_tensor(out=sm(13), in0=sm(12), scalar=2.0, in1=sm(13), op0=ALU.mult, op1=ALU.mult))
                step(dve.tensor_tensor(sm(12), sm(14), sm(15), ALU.subtract))

        gate(2)
        gate(3)
        c_part(0)
        c_part(1)

        def turn_back(j):
            c, sn = phases(j)
            dve.wait_ge(q["input_done"], j + 1)
            if j >= 3:
                dve.wait_ge(q["y_done"], j - 2)
            bre, bim = (k.ps[:, 2 * (j % 2):2 * (j % 2) + 2, n * S:(n + 1) * S] for n in range(2))
            for n, (x, y) in enumerate(((bre, c), (bim, sn), (bim, c), (bre, sn))):
                dve.tensor_tensor(prods[j % 3][:, n], x, y, ALU.mult).then_inc(q["v_parts"], 1)

        def scan(j):
            c, sn = phases(j)
            part = prods[j % 3]
            for n in range(2):
                dve.wait_ge(q["v_put"], 2 * j + n + 1)
                for i in range(2):
                    tile = 2 * j + i
                    dve.tensor_tensor_scan(part[:, 2 * n, i, :], small[:, 2, tile:tile + 1].to_broadcast([P, S]),
                                           part[:, 2 * n, i, :], 0.0, ALU.mult, ALU.add).then_inc(q["w_put"], 1)
            dve.wait_ge(q["w_put"], 4 * j + 4)
            dve.tensor_tensor(part[:, 1], part[:, 0], c, ALU.mult).then_inc(q["s_put_dve"], 1)
            dve.scalar_tensor_tensor(out=part[:, 3], in0=part[:, 2], scalar=-1.0, in1=sn, op0=ALU.mult,
                                     op1=ALU.mult).then_inc(q["s_put_dve"], 1)

        turn_back(0)
        for j in range(8):
            if j < 7:
                turn_back(j + 1)
            scan(j)
        for c in range(4):
            dve.wait_ge(q["y_done"], 2 * (c + 1))
            dve.scalar_tensor_tensor(out=z[:, c, :], in0=u[:, c, :], scalar=fix(k, "s5_d")[:, c:c + 1],
                                     in1=k.ps[:, 4 + c, 0:S], op0=ALU.mult, op1=ALU.add).then_inc(q["gelu_arg"], 1)
        for c in range(4):
            dve.wait_ge(q["sig_put"], c + 1)
            dve.tensor_tensor(mixT[:, 4 + c, :], z[:, c, :], u[:, c, :], ALU.mult).then_inc(q["yb_put"], 1)
        norm.vector(dve)

    def gpsimd(pool):
        def add(j):
            part = prods[j % 3]
            pool.wait_ge(q["v_parts"], 4 * j + 4)
            pool.tensor_tensor(part[:, 0], part[:, 0], part[:, 1], ALU.add).then_inc(q["v_put"], 1)
            pool.tensor_tensor(part[:, 2], part[:, 2], part[:, 3], ALU.subtract).then_inc(q["v_put"], 1)

        add(0)
        for j in range(8):
            if j < 7:
                add(j + 1)
            c, sn = phases(j)
            part = prods[j % 3]
            for n, phase in enumerate((sn, c)):
                pool.wait_ge(q["s_put_dve"], 2 * j + n + 1)
                pool.tensor_tensor(part[:, 2 * n], part[:, 2 * n], phase, ALU.mult).then_inc(q["s_put"], 1)

    return Stage(tensor, scalar, vector, gpsimd)


def ple(k, u, base, pT, out=None):
    sem = k.sem
    p_loaded, proj_done, gate_done, sig_put, part_put, turned, x_put, stored = (
        sem(f"ple_{s}") for s in ("p_loaded", "proj_done", "gate_done", "sig_put", "part_put", "turned", "x_put", "stored"))
    before = 2 * ST * u
    p_sb = area(k, 0, 512, k=2)
    sig = area(k, 1024, 2048, n=4)
    n_proj = base + 3

    def tensor(pe):
        for n in range(base, base + 3):
            pe.wait_ge(k.slot_ready[n % SLOTS], k.use.mark[n])
        for t in range(ST):
            for half in range(2):
                for kk in range(DK):
                    w = slot(k, base + kk // 3)[:, (kk % 3) * D + half * 512:(kk % 3) * D + (half + 1) * 512]
                    last = pe.matmul(k.ps[:, 2 * t + half, :], k.hT[:, kk, t * P:(t + 1) * P], w,
                                     start=(kk == 0), stop=(kk == DK - 1))
                last.then_inc(gate_done, 1)
        pe.drain().then_inc(k.slot_freed, 3)
        pe.wait_ge(k.slot_ready[n_proj % SLOTS], k.use.mark[n_proj])
        pe.wait_ge(p_loaded, 16 * (u + 1))
        for t in range(ST):
            for half in range(2):
                for kk in range(PLE // P):
                    last = pe.matmul(k.ps[:, 4 + 2 * t + half, :], p_sb[:, kk, t * P:(t + 1) * P],
                                     slot(k, n_proj)[:, kk * D + half * 512:kk * D + (half + 1) * 512],
                                     start=(kk == 0), stop=(kk == PLE // P - 1))
                last.then_inc(proj_done, 1)
        for i in range(4):
            t, half = i // 2, i % 2
            pe.wait_ge(sig_put, before + i + 1)
            if out is None:
                pe.wait_ge(part_put, before + i + 1)
            for j in range(4):
                kk = 4 * half + j
                src = sig[:, i, j * P:(j + 1) * P] if out is None else k.hT[:, kk, t * P:(t + 1) * P]
                last = pe.transpose(k.ps[:, i, j * P:(j + 1) * P], src, k.ident)
            last.then_inc(turned, 1)
        pe.drain().then_inc(k.slot_freed, 1)

    def scalar(act):
        act.dma_start(p_sb, pT).then_inc(p_loaded, 16)
        for i in range(4):
            act.wait_ge(gate_done, before + i + 1)
            act.activation(sig[:, i, :], k.ps[:, i, :], ACT.Sigmoid).then_inc(sig_put, 1)
        if out is not None:
            for i in range(4):
                t, cols = i // 2, slice((i % 2) * 512, (i % 2 + 1) * 512)
                act.wait_ge(x_put, before + i + 1)
                act.dma_start(out[0, t * P:(t + 1) * P, cols], k.x[:, t, cols]).then_inc(stored, 16)
            act.wait_ge(stored, 16 * 4)

    def vector(dve):
        for i in range(4):
            dve.wait_ge(sig_put, before + i + 1)
            dve.wait_ge(proj_done, before + i + 1)
            dve.tensor_tensor(sig[:, i, :], sig[:, i, :], k.ps[:, 4 + i, :], ALU.mult).then_inc(part_put, 1)
        for i in range(4):
            t, half = i // 2, i % 2
            dve.wait_ge(turned, before + i + 1)
            if out is None:
                x = k.hT[:, 4 * half:4 * half + 4, t * P:(t + 1) * P]
                dve.tensor_tensor(x, x, k.ps[:, i, :].rearrange("p (k s) -> p k s", k=4), ALU.add).then_inc(x_put, 1)
            else:
                dve.wait_ge(part_put, before + i + 1)
                dve.tensor_tensor(k.x[:, t, half * 512:(half + 1) * 512], sig[:, i, :], k.ps[:, i, :],
                                  ALU.add).then_inc(x_put, 1)

    return Stage(tensor, scalar, vector)


def sparse_attention(k, base, causal, positions):
    sem = k.sem
    n_out = base + DK
    names = ("loaded", "rope_done", "turned",
             "turned_act", "turned_dve", "index_done", "relu_put", "relu_used")
    q = {s: sem(f"dsa_{s}") for s in names}
    B = {"column_done": 38, "copied": 24, "sin_arg": 3, "sin_done": 4, "score_done": 2 * HEADS, "score_read": 2 * HEADS, "score_put": HEADS, "exp_done": 4 * HEADS, "p_put": ST * HEADS,
         "p_turned": HEADS, "pT_put": HEADS, "o_done": HEADS, "o_put": HEADS}
    q.update({s: sem(s) for s in B})
    HH = QH + KVH
    WIDE, W = HH * HD, IH * ID
    ROW = WIDE + W + ID
    NPR = ST * ROW
    pr = area(k, 0, NPR, t=ST)
    qT = area(k, NPR, QH * S, h=QH)
    kT = area(k, NPR + 2048, KVH * S, h=KVH)
    qiT = area(k, NPR + 2560, 4 * S, h=4)
    kiT = area(k, NPR + 3584, S)
    v = area(k, NPR + 3840, ST * KVH * HD, t=ST)
    wi = area(k, NPR + 4352, ST * IH, t=ST)
    ki2 = area(k, NPR + 4368, ST * 2 * ID, t=ST)
    mixT = area(k, NPR + 4624, DK * S, k=DK)
    assert R0 + NPR + 4624 + DK * S <= ARENA
    out_done, out_tensor = mixer_out(k, n_out, mixT, fix(k, "seed1"))
    norm = NormAndTurn(k, out_done, 4 * ST, 1.0)
    score = area(k, 0, 512, t=ST)
    left = area(k, 512, 512, t=ST)
    relu = area(k, 1024, 1024, n=4)
    keep = area(k, 2048, 512, t=ST)
    s = k.arena[:, X0:X0 + 4 * ST * S].rearrange("p (b t s) -> p b t s", b=4, t=ST)
    pT = area(k, 1024, 1024, b=2, c=ST)

    causal_sb = work(k, 0, 512, t=ST)
    pos_i = work(k, 512, ST).bitcast(I32)
    pos = work(k, 514, ST)
    ang, arg, rev = work(k, 520, 48, t=ST), work(k, 568, 96, n=2, t=ST), work(k, 664, 48, t=ST)
    trig = work(k, 712, 96, n=2, t=ST)
    tmp = [work(k, 1024 + 320 * i, 320) for i in range(4)]
    m = misc(k, 0, 40)
    scale = HD ** -0.5
    NOT = -1e30
    TAKEN = -2e30
    CHUNKS = [(0, 512), (512, 1024), (1024, 1536), (1536, 2048), (2048, C_IN)]
    BLOCKS = ([(qT[:, h, :], h * HD) for h in range(QH)] + [(kT[:, h, :], (QH + h) * HD) for h in range(KVH)]
              + [(qiT[:, h, :], WIDE + h * P) for h in range(4)] + [(kiT, None)])

    def tensor(pe):
        for n in range(base, base + DK):
            pe.wait_ge(k.slot_ready[n % SLOTS], k.use.mark[n])
        for i in range(ST * len(CHUNKS)):
            t, (c0, c1) = i // len(CHUNKS), CHUNKS[i % len(CHUNKS)]
            if i >= 8:
                pe.wait_ge(q["copied"], B["copied"] + i - 7)
            for kk in range(DK):
                last = pe.matmul(k.ps[:, i % 8, 0:c1 - c0], k.hT[:, kk, t * P:(t + 1) * P], slot(k, base + kk)[:, c0:c1],
                                 start=(kk == 0), stop=(kk == DK - 1))
            last.then_inc(q["column_done"], 1)
        pe.drain().then_inc(k.slot_freed, DK)
        pe.wait_ge(q["rope_done"], 1)
        pe.wait_ge(q["copied"], B["copied"] + ST * len(CHUNKS))
        for i, (_, at) in enumerate(BLOCKS):
            for t in range(ST):
                src = ki2[:, t, :] if at is None else pr[:, t, at:at + P]
                last = pe.transpose(k.ps[:, i // 2, (i % 2) * S + t * P:(i % 2) * S + (t + 1) * P], src, k.ident)
            if i % 2 or i == len(BLOCKS) - 1:
                last.then_inc(q["turned"], 1)
        pe.wait_ge(q["turned_act"], 4)
        pe.wait_ge(q["turned_dve"], 4)
        for i in range(ST * IH):
            t, h = i // IH, i % IH
            if i >= 8:
                pe.wait_ge(q["relu_put"], i - 7)
            r = ID * (h % 2)
            pe.matmul(k.ps[:, i % 8, 0:P * (t + 1)], qiT[r:r + ID, h // 2, t * P:(t + 1) * P], kiT[r:r + ID, 0:P * (t + 1)],
                      start=True, stop=True).then_inc(q["index_done"], 1)
        pe.wait_ge(q["relu_put"], ST * IH)
        def scores(h):
            if h >= 2:
                pe.wait_ge(q["score_read"], B["score_read"] + h - 1)
            for t in range(ST):
                last = pe.matmul(k.ps[:, h % 2, t * S:(t + 1) * S], qT[:, h, t * P:(t + 1) * P],
                                 kT[:, h // (QH // KVH), :], start=True, stop=True)
            last.then_inc(q["score_done"], 1)

        def turn(h):
            pe.wait_ge(q["p_put"], B["p_put"] + ST * (h + 1))
            if h >= 2:
                pe.wait_ge(q["pT_put"], B["pT_put"] + h - 1)
            for t in range(ST):
                for kc in range(ST):
                    last = pe.transpose(k.ps[:, 2 + h % 2, kc * S + t * P:kc * S + (t + 1) * P],
                                        s[:, h % 4, t, kc * P:(kc + 1) * P], k.ident)
            last.then_inc(q["p_turned"], 1)

        def outputs(h):
            pe.wait_ge(q["pT_put"], B["pT_put"] + h + 1)
            if h >= 2:
                pe.wait_ge(q["o_put"], B["o_put"] + h - 1)
            kv = h // (QH // KVH)
            for kc in range(ST):
                last = pe.matmul(k.ps[:, 4 + h % 2, 0:S], v[:, kc, kv * HD:(kv + 1) * HD], pT[:, h % 2, kc, :],
                                 start=(kc == 0), stop=(kc == ST - 1))
            last.then_inc(q["o_done"], 1)

        skewed(QH, scores, turn, outputs)
        pe.wait_ge(q["o_put"], B["o_put"] + QH)
        out_tensor(pe)
        norm.tensor(pe)

    def scalar(act):
        act.dma_start(causal_sb, causal).then_inc(q["loaded"], 16)
        act.dma_start(pos_i, positions).then_inc(q["loaded"], 16)
        for n in range(2):
            act.wait_ge(q["sin_arg"], B["sin_arg"] + n + 1)
            act.activation(trig[:, n], arg[:, n], ACT.Sin).then_inc(q["sin_done"], 1)
        for i in range(ST * len(CHUNKS)):
            t, c = i // len(CHUNKS), i % len(CHUNKS)
            act.wait_ge(q["column_done"], B["column_done"] + i + 1)
            bank = k.ps[:, i % 8, :]
            if c < 2:
                last = act.activation(pr[:, t, c * 512:(c + 1) * 512], bank, ACT.Copy)
            elif c == 2:
                act.activation(pr[:, t, 1024:WIDE], bank[:, 0:256], ACT.Copy)
                last = act.activation(v[:, t, :], bank[:, 256:512], ACT.Copy)
            elif c == 3:
                last = act.activation(pr[:, t, WIDE:WIDE + W], bank, ACT.Copy)
            else:
                act.activation(pr[:, t, WIDE + W:ROW], bank[:, 0:ID], ACT.Copy)
                last = act.activation(wi[:, t, :], bank[:, ID:ID + IH], ACT.Copy, scale=IH ** -0.5 * ID ** -0.5)
            last.then_inc(q["copied"], 1)
        for b in (1, 3, 5, 7):
            act.wait_ge(q["turned"], b + 1)
            for j in range(2):
                if 2 * b + j < len(BLOCKS):
                    last = act.activation(BLOCKS[2 * b + j][0], k.ps[:, b, j * S:(j + 1) * S], ACT.Copy)
            last.then_inc(q["turned_act"], 1)
        for i in range(ST * IH):
            t = i // IH
            act.wait_ge(q["index_done"], i + 1)
            if i >= 4:
                act.wait_ge(q["relu_used"], i - 3)
            act.activation(relu[:, i % 4, 0:P * (t + 1)], k.ps[:, i % 8, 0:P * (t + 1)], ACT.Relu).then_inc(q["relu_put"], 1)
        def exponentials(h):
            act.wait_ge(q["score_put"], B["score_put"] + h + 1)
            for t in range(ST):
                act.activation(s[:, h % 4, t, :], s[:, h % 4, t, :], ACT.Exp, bias=m[:, 2 * (h % 2) + t:2 * (h % 2) + t + 1],
                               accum_out=m[:, 4 + 2 * (h % 2) + t:5 + 2 * (h % 2) + t]).then_inc(q["exp_done"], 1)

        def output(h):
            act.wait_ge(q["o_done"], B["o_done"] + h + 1)
            act.activation(mixT[:, h, :], k.ps[:, 4 + h % 2, 0:S], ACT.Copy).then_inc(q["o_put"], 1)

        skewed(QH, exponentials, None, output)
        norm.scalar(act)

    def vector(dve):
        step = k.vector_order.on(dve)
        dve.wait_ge(q["loaded"], 32)
        step(dve.tensor_copy(pos, pos_i))
        for t in range(ST):
            step(dve.tensor_scalar(ang[:, t, :], fix(k, "inv_freq"), pos[:, t:t + 1], None, ALU.mult))
        step(range_reduce(step, dve, arg[:, 0], ang, rev))
        step(dve.scalar_tensor_tensor(out=arg[:, 1], in0=arg[:, 0], scalar=-1.0, in1=arg[:, 0], op0=ALU.mult, op1=ALU.max))
        dve.tensor_scalar(arg[:, 1], arg[:, 1], -1.0, math.pi / 2, ALU.mult, ALU.add).then_inc(q["sin_arg"], 2)
        dve.wait_ge(q["sin_done"], B["sin_done"] + 2)
        dve.wait_ge(q["copied"], B["copied"] + ST * len(CHUNKS))
        for c0, heads, width, a0, half in ((0, HH, HD, 0, 16), (WIDE, IH + 1, ID, 16, 8)):
            part = pr[:, :, c0:c0 + heads * width].rearrange("p t (h d) -> p t h d", d=width)
            t1, t2 = part[:, :, :, 0:half], part[:, :, :, half:2 * half]
            sin, cos = (trig[:, n, :, a0:a0 + half].unsqueeze(2).to_broadcast([P, ST, heads, half]) for n in range(2))
            p = [x[:, 0:ST * heads * half].rearrange("p (t h d) -> p t h d", t=ST, d=half) for x in tmp]
            step(dve.tensor_tensor(p[0], t1, cos, ALU.mult))
            step(dve.tensor_tensor(p[1], t2, sin, ALU.mult))
            step(dve.tensor_tensor(p[2], t2, cos, ALU.mult))
            step(dve.tensor_tensor(p[3], t1, sin, ALU.mult))
            step(dve.tensor_tensor(t1, p[0], p[1], ALU.subtract))
            step(dve.tensor_tensor(t2, p[2], p[3], ALU.add))
        step(dve.tensor_copy(ki2[:, :, 0:ID], pr[:, :, WIDE + W:ROW]))
        dve.tensor_copy(ki2[:, :, ID:2 * ID], pr[:, :, WIDE + W:ROW]).then_inc(q["rope_done"], 1)
        for b in (0, 2, 4, 6):
            dve.wait_ge(q["turned"], b + 1)
            for j in range(2):
                last = dve.tensor_copy(BLOCKS[2 * b + j][0], k.ps[:, b, j * S:(j + 1) * S])
            last.then_inc(q["turned_dve"], 1)
        for i in range(ST * IH):
            t, h = i // IH, i % IH
            w = slice(0, P * (t + 1))
            dve.wait_ge(q["relu_put"], i + 1)
            if h:
                dve.wait_ge(q["relu_used"], i)
            dve.scalar_tensor_tensor(out=score[:, t, w], in0=relu[:, i % 4, w], scalar=wi[:, t, h:h + 1],
                                     in1=causal_sb[:, t, w] if h == 0 else score[:, t, w], op0=ALU.mult,
                                     op1=ALU.add).then_inc(q["relu_used"], 1)
        dve.wait_ge(q["relu_used"], ST * IH)
        for t in range(ST):
            w = slice(0, P * (t + 1))
            for r in range(TOPK // 8):
                src = left[:, t, w] if r else score[:, t, w]
                step(dve.max(m[:, 8:16], src))
                step(dve.match_replace(out=left[:, t, w], in_to_replace=m[:, 8:16], in_values=src, imm_value=TAKEN))
            step(dve.tensor_scalar(left[:, t, w], left[:, t, w], TAKEN, -NOT, ALU.is_equal, ALU.mult))
            step(dve.scalar_tensor_tensor(out=keep[:, t, w], in0=left[:, t, w], scalar=NOT, in1=causal_sb[:, t, w],
                                          op0=ALU.add, op1=ALU.add))
        step(dve.tensor_copy(keep[:, 0, P:S], causal_sb[:, 0, P:S]))

        def weights(h):
            b = h % 2
            neg = m[:, 2 * b:2 * b + 2]
            dve.wait_ge(q["score_done"], B["score_done"] + h + 1)
            dve.scalar_tensor_tensor(out=s[:, h % 4], in0=k.ps[:, b, :].rearrange("p (t s) -> p t s", t=ST), scalar=scale,
                                     in1=keep, op0=ALU.mult, op1=ALU.add).then_inc(q["score_read"], 1)
            dve.wait_ge(q["score_read"], B["score_read"] + h + 1)
            step(dve.tensor_reduce(neg, s[:, h % 4], AX, ALU.max))
            dve.tensor_scalar(neg, neg, -1.0, None, ALU.mult).then_inc(q["score_put"], 1)

        def normalise(h):
            b = h % 2
            total = m[:, 4 + 2 * b:6 + 2 * b]
            dve.wait_ge(q["exp_done"], B["exp_done"] + 2 * h + 2)
            step(dve.reciprocal(total, total))
            for t in range(ST):
                dve.tensor_scalar(s[:, h % 4, t, :], s[:, h % 4, t, :], total[:, t:t + 1], None, ALU.mult).then_inc(q["p_put"], 1)

        def turned(h):
            b = h % 2
            dve.wait_ge(q["p_turned"], B["p_turned"] + h + 1)
            dve.tensor_copy(pT[:, b], k.ps[:, 2 + b, :].rearrange("p (c s) -> p c s", c=ST)).then_inc(q["pT_put"], 1)

        skewed(QH, weights, normalise, turned)
        norm.vector(dve)

    return Stage(tensor, scalar, vector)


def second(k, t, base, out):
    loads, stages = [], []

    def add(new, stage):
        nonlocal loads
        loads += new
        stages.append(stage)

    def add_ffn(i, j, n):
        add(ffn_weights(k, n, t["ffn_w"][2 * i + j]), ffn(k, 2 * i + j, n))
        return n + FC

    def add_ple(i, n, out=None):
        new = weights_in_slots(k, n, t["ple_w_gate_2"][i], 3, D)
        new += weights_in_slots(k, n + 3, t["ple_w_proj_2"][i], 3, D)
        add(new, ple(k, i, n, t["pT"][i], out))
        return n + 4

    n = add_ffn(0, 0, base)
    new = weights_in_slots(k, n, t["ab_w_in_2"][0], 1, 3 * CC + S5G * S5C)
    new += weights_in_slots(k, n + 8, t["s5_w_glu_2"][0], 6, CC)
    new += weights_in_slots(k, n + 9, t["ab_w_out_2"][0], 3, D)
    add(new, conv_s5(k, n, t["s5_params"]))
    n = add_ffn(0, 1, n + 12)
    n = add_ple(0, n)
    n = add_ffn(1, 0, n)
    new = weights_in_slots(k, n, t["c_w_in_2"][0], 1, C_IN)
    new += weights_in_slots(k, n + DK, t["c_w_out_2"][0], 3, D)
    add(new, sparse_attention(k, n, t["causal"], t["positions"]))
    n = add_ffn(1, 1, n + DK + 3)
    add_ple(1, n, out)
    return loads, stages


def laid_out_second(a):
    def by_state(v):
        v = np.asarray(v)
        v = v.reshape(S5G // 2, 2 * S5N, -1)
        return v.transpose(1, 0, 2).reshape(P, -1)

    log_dt = np.repeat(np.asarray(a["s5_log_dt_2"][0])[:, None], S5N, 1)
    c_parts = [np.asarray(a[n][0]).reshape(4, P, S5N).transpose(1, 0, 2).reshape(P, -1) for n in ("s5_c_re_2", "s5_c_im_2")]
    params = [by_state(a["s5_lam_re_2"][0]), by_state(a["s5_lam_im_2"][0]), by_state(log_dt),
              by_state(a["s5_b_re_2"][0]), by_state(a["s5_b_im_2"][0])] + c_parts
    w1, w3 = (np.asarray(a[n]).reshape(4, DK, P, FC, P).transpose(0, 3, 2, 1, 4).reshape(4, FC, P, D)
              for n in ("ffn_w1_2", "ffn_w3_2"))
    w2 = np.asarray(a["ffn_w2_2"]).reshape(4, FC, P, D)
    t, s = np.arange(S)[:, None], np.arange(S)[None, :]
    causal = np.where(s <= t, 0.0, -1e30).astype(np.float32)
    return {
        "ffn_w": np.concatenate([w1, w3, w2], 3),
        "s5_params": np.ascontiguousarray(np.concatenate(params, 1)),
        "pT": np.ascontiguousarray(np.asarray(a["p_2"])[:, 0].transpose(0, 2, 1).reshape(2, PLE // P, P, S).transpose(0, 2, 1, 3)),
        "positions": np.ascontiguousarray(np.asarray(a["positions_2"]).reshape(ST, P).T),
        "causal": np.ascontiguousarray(causal.reshape(ST, P, S).transpose(1, 0, 2)),
    }


def weights_in_slots(k, first, w, rows_per_slot, cols, r0=0):
    chunks = w.shape[0] // P
    out = []
    for i in range(-(-chunks // rows_per_slot)):
        c0, c1 = i * rows_per_slot, min((i + 1) * rows_per_slot, chunks)
        n = first + i
        k.use.landing(n)
        dst = slot(k, n, (c1 - c0) * cols).rearrange("p (c f) -> p c f", c=c1 - c0)
        out.append((n, [(dst, w[c0 * P:c1 * P, :].rearrange("(c p) f -> p c f", p=P))]))
    return out


def program(nc, t, out):
    with ExitStack() as stack:
        k = setup(nc, stack)
        k.w_router = t["w_router"]
        n_out = DK
        n_experts = n_out + 3
        loads = weights_in_slots(k, 0, t["w_in"][0], 1, 3 * D)
        first_loads, first = filters(k, t["x"], t["fixed"], t["dft"], t["filt_tables"], t["filt_w1"], t["filt_w2"],
                                     t["filt_w3"], t["zT"])
        loads += weights_in_slots(k, n_out, t["w_out"][0], 3, D)
        stages = [first, projections(k), hyena(k), attention(k, t["dist"], t["lam_rows"]), routing(k, n_out)]
        expert_loads, expert_stage = experts(k, n_experts, t["w_gate"], t["w_up"], t["w_down"],
                                             t["final_norm_g"])
        stages += [expert_stage, experts_combine(k)]
        more_loads, more_stages = second(k, t, n_experts + 3 * DK * NE, out["out"])
        stages += more_stages

        with nc.Block() as block:
            @block.sync
            def _(sync):
                first_loads(sync)
                sync.wait_ge(k.sem("tables_loaded"), 16 * 6)
                load_slots(k, sync, loads)
                expert_loads(sync)
                load_slots(k, sync, more_loads)

            @block.tensor
            def _(pe):
                for i, stage in enumerate(stages):
                    stage.tensor(pe)
                    meet(k, "tensor", pe, i)

            @block.scalar
            def _(act):
                for i, stage in enumerate(stages):
                    stage.scalar(act)
                    meet(k, "scalar", act, i)

            @block.vector
            def _(dve):
                for i, stage in enumerate(stages):
                    stage.vector(dve)
                    meet(k, "vector", dve, i)

            @block.gpsimd
            def _(pool):
                for i, stage in enumerate(stages):
                    stage.gpsimd(pool)
                    meet(k, "gpsimd", pool, i)


def constants():
    f32 = np.float32
    s = np.arange(S, dtype=np.float64)[:, None]
    f = np.arange(S, dtype=np.float64)[None, :]
    ang = 2 * np.pi * ((s * f) % NF) / NF
    nyq = np.where(np.arange(S) % 2 == 0, 1.0, -1.0)
    fwd = np.concatenate([np.cos(ang), -np.sin(ang)], 1)
    fwd[:, S] = nyq
    bwd = np.concatenate([np.cos(ang), np.sin(ang)], 1)
    bwd[:, S] = nyq
    bwd[0] = 0.0
    inv = np.concatenate([2 * np.cos(ang.T), -2 * np.sin(ang.T)], 0) / NF
    inv[0] = 1.0 / NF
    inv[S] = nyq / NF

    def tiles(a):
        return a.reshape(-1, P, a.shape[1]).transpose(1, 0, 2).reshape(P, -1).astype(f32)

    t = np.linspace(0.0, 1.0, S, dtype=f32)[:, None]
    w = (f32(2.0 * math.pi) * np.arange(S, dtype=f32)[:, None] / f32(S)).astype(f32)
    bands = np.linspace(1e-4, (EMB - 1) // 2 - 1, (EMB - 1) // 2, dtype=f32)[None, :]
    z = np.concatenate([t, np.cos(bands * w), -np.sin(bands * w)], axis=-1).astype(f32)
    deltas = np.abs(np.linspace(math.log(1e-2) / 1.5, math.log(1e-2) / 0.3, HY, dtype=f32))
    decay = np.exp(-t * deltas).astype(f32)
    dist = np.abs(np.arange(S)[:, None] - np.arange(S)[None, :]).astype(f32)
    eye = np.eye(P, dtype=f32)
    ones0 = np.ones((P, P), f32)
    ones0[0] = 0.0
    inv_attn = (500000.0 ** (-np.arange(0, 32, 2, dtype=f32) / f32(32))).astype(f32)
    inv_idx = (500000.0 ** (-np.arange(0, 16, 2, dtype=f32) / f32(16))).astype(f32)
    return {
        "dft": np.concatenate([tiles(fwd), tiles(inv)], 1),
        "filt_tables": np.concatenate([tiles(bwd), tiles(decay)], 1),
        "zT": np.ascontiguousarray(z.T), "dist": tiles(dist).reshape(P, ST, S),
        "ident": eye, "ones": np.ones((P, P), f32), "ones0": ones0,
        "group_mean": np.kron(np.eye(2, dtype=f32), np.full((64, 64), 1 / 64, f32)),
        "mask_b": np.kron(np.eye(2, dtype=f32), np.ones((S5N, 1), f32)),
        "mask_c": np.tile(np.kron(np.eye(2, dtype=f32), np.ones((S5C, 1), f32)), (4, 1)),
        "seed1": eye * f32(ALPHA), "seed2": eye * f32(2 * ALPHA),
        "slot_no": np.tile(np.arange(CAP, dtype=f32), (P, 1)),
        "inv_freq": np.tile(np.concatenate([inv_attn, inv_idx]), (P, 1)),
    }


def laid_out(a):
    c = constants()

    def by_channel(v):
        v = np.asarray(v)
        return np.ascontiguousarray(v.reshape(-1, P).T)

    filt = np.zeros((P, 3), np.float32)
    for i, n in enumerate(("filt_b1", "filt_b2", "filt_freq")):
        filt[:HID, i] = a[n][0]
    parts = dict(c)
    parts.update(attn_g=by_channel(a["attn_norm_g"]), conv_w=by_channel(a["conv_w"]), conv_b=by_channel(a["conv_b"]),
                 skip=by_channel(a["hyena_skip"]), hy_g=by_channel(a["hyena_norm_g"]), subln_g=by_channel(a["subln_g"]),
                 ffn_g=by_channel(a["ffn_norm_g"]), filt=filt, conv_w2=by_channel(a["conv_w_2"]),
                 s5_d=by_channel(a["s5_d_2"]), b_glu=by_channel(a["s5_b_glu_2"]),
                 ln_g=by_channel(a["ln_g_2"]), ln_b=by_channel(a["ln_b_2"]))
    out = {n: np.ascontiguousarray(a[n]) for n in WHOLE}
    out["fixed"] = np.concatenate([parts[n] for n, (at, w) in FIX.items() if n != "misc"], 1)
    for n in ("dft", "filt_tables", "zT", "dist"):
        out[n] = c[n]
    lam = np.concatenate([a[n][0] for n in ("lambda_q1", "lambda_k1", "lambda_q2", "lambda_k2")])
    out["lam_rows"] = np.ascontiguousarray(np.broadcast_to(lam, (P, lam.size)))
    out.update(laid_out_second(a))
    return out


WHOLE = ["x", "w_in", "filt_w1", "filt_w2", "filt_w3", "w_out", "w_router", "w_gate", "w_up", "w_down", "final_norm_g",
         "ple_w_proj_2", "ple_w_gate_2", "ab_w_in_2",
         "ab_w_out_2", "s5_w_glu_2", "c_w_in_2", "c_w_out_2"]


def kernel(**inputs):
    import concourse.bacc as bacc
    from concourse.bass_utils import run_bass_kernel_spmd

    arrays = laid_out({n: np.asarray(v) for n, v in inputs.items()})
    nc = bacc.Bacc("TRN2", target_bir_lowering=False, num_devices=1)
    tensors = {n: nc.dram_tensor(f"in_{n}", v.shape, mybir.dt.from_np(v.dtype), kind="ExternalInput").ap()
               for n, v in arrays.items()}
    out = nc.dram_tensor("result", (1, S, D), F32, kind="ExternalOutput").ap()
    program(nc, tensors, {"out": out})
    done = run_bass_kernel_spmd(nc, [{f"in_{n}": v for n, v in arrays.items()}], core_ids=[0])
    return done.results[0]["result"]
```

```python
import math
from contextlib import ExitStack

import numpy as np
import concourse.bass as bass
from concourse import mybir

F32 = mybir.dt.float32
F32R = mybir.dt.float32r
I32 = mybir.dt.int32
ALU = mybir.AluOpType
ACT = mybir.ActivationFunctionType
AX = mybir.AxisListType.X

P = 128
S = 256
ST = S // P
D = 1024
DK = D // P
EPS = 1e-6
HY = 512
HC = HY // P
NORD = 2
NF = 2 * S
FM = NF // P
EMB, HID = 33, 64
HEADS, DH = 4, 64
LAM_INIT = 0.8 - 0.6 * math.exp(0.0)
NE, CAP, FF = 16, 32, 2816
NG = 4
FG = FF // NG
FH = FG // 2
FT = FG // P
FR = FG - FT * P

ALPHA = 4.0 ** 0.25
LN_EPS = 1e-5
PLE = 256
CC = 512
S5G, S5C, S5N = 32, 16, 64
QH, HD, KVH, IH, ID = 8, 128, 2, 8, 64
TOPK = 64
C_IN = QH * HD + 2 * KVH * HD + IH * ID + ID + IH

SLOT = 3072
SLOTS = 8
WIDE = 12
FIRST_WIDE = DK + 3
WIDE_USES = 3 * DK * NE
ARENA = 16256
WORK = 12288

FIX = {}
_at = 0
for _n, _w in [("ident", P), ("ones", P), ("ones0", P), ("group_mean", P), ("mask_b", 2), ("mask_c", 2), ("seed1", P), ("seed2", P), ("slot_no", CAP),
               ("inv_freq", 24), ("attn_g", DK), ("conv_w", 36), ("conv_b", 12), ("skip", 8), ("hy_g", HC),
               ("subln_g", 1), ("ffn_g", DK), ("filt", 3), ("conv_w2", 12), ("s5_d", 4), ("b_glu", 4), ("ln_g", 6 * DK), ("ln_b", 6 * DK), ("misc", 40)]:
    FIX[_n] = (_at, _w)
    _at += _w
FIXED = _at
LOADED = FIX["misc"][0]
X0 = 1024 if FIXED <= 1024 else FIXED
HT0 = X0 + ST * D
R0 = HT0 + DK * S
PARTS = 4096 + 1024


W_IN_TILES = 24
C_TILE = 384
C_SLOTS = 6
C_HT_LOW = 8336
HIGHS = 6


class InOrder:

    def __init__(self, done):
        self.done, self.count = done, 0

    def on(self, engine):
        self.engine = engine
        return self

    def __call__(self, instruction):
        self.count += 1
        instruction.then_inc(self.done, 1)
        self.engine.wait_ge(self.done, self.count)


class Ring:

    def __init__(self):
        self.marks = [0] * WIDE
        self.last = [-1] * WIDE
        self.mark = {}
        self.freed = {}

    @staticmethod
    def slot_of(n):
        if FIRST_WIDE <= n < FIRST_WIDE + WIDE_USES:
            return (n - FIRST_WIDE + FIRST_WIDE % SLOTS) % WIDE
        return n % SLOTS

    def landing(self, n, dmas=1):
        s = self.slot_of(n)
        self.marks[s] += 16 * dmas
        self.mark[n] = self.marks[s]
        self.freed[n] = self.last[s] + 1
        self.last[s] = n
        return self.mark[n]


class Core:
    pass


ENGINES = ("tensor", "scalar", "vector", "gpsimd")


class Stage:

    def __init__(self, tensor, scalar, vector, gpsimd=None):
        self.tensor, self.scalar, self.vector = tensor, scalar, vector
        self.gpsimd = gpsimd or (lambda pool: None)


def meet(k, name, engine, i):
    engine.drain().then_inc(k.passed[name], 1)
    for other in ENGINES:
        if other != name:
            engine.wait_ge(k.passed[other], i + 1)


def setup(nc, stack):
    k = Core()
    k.nc = nc
    base = -(-nc.sbuf_base // 32) * 32
    place = lambda name, at, shape, dt: nc.alloc_sbuf_tensor_at(name, shape, dt, offset=base + 4 * at)
    at_arena, at_work = SLOTS * SLOT, SLOTS * SLOT + ARENA
    k.ring = place("ring", 0, [P, SLOTS * SLOT], F32)
    k.arena = place("arena", at_arena, [P, ARENA], F32)
    k.work = place("work", at_work, [P, WORK], F32)
    k.w13 = place("w13", at_work, [P, 2, 2, 2, DK, P], F32R)
    k.w2 = place("w2", at_work + 8192, [P, 2, 2, D], F32R)
    k.hsplit = place("hsplit", at_work - PARTS, [P, 2, DK, S], F32R)
    k.hidsplit = place("hidsplit", at_work - PARTS + 4096, [P, 2, 2, S], F32R)
    k.w_low = place("w_low", 0, [P, SLOTS * SLOT // D, DK, P], F32R)
    k.w_high = place("w_high", at_work + 6144, [P, HIGHS, DK, P], F32R)
    k.hT_low = place("hT_low", at_arena + HT0, [P, DK, S], F32R)
    k.hT_high = place("hT_high", at_arena + R0 + 7168, [P, DK, S], F32R)
    k.gate_high = [place(f"gate_high{i}", at_work + 4096 * i, [P, DK // 2, D], F32R) for i in range(2)]
    k.c_high = place("c_high", at_work + 4096, [P, 2, SLOT], F32R)
    k.c_hT_high = place("c_hT_high", at_work + 10240, [P, DK, S], F32R)
    k.c_hT_low = place("c_hT_low", at_arena + R0 + C_HT_LOW, [P, DK, S], F32R)
    k.ps = stack.enter_context(nc.psum_tensor("ps", [P, 8, 512], F32))
    k.norms = 0
    k.h_splits = k.w_splits = 0
    made = {}

    def sem(name):
        if name not in made:
            made[name] = stack.enter_context(nc.semaphore(name))
        return made[name]

    k.sem = sem
    k.vector_order, k.pool_order = InOrder(sem("vector_order")), InOrder(sem("pool_order"))
    k.slot_ready = [k.sem(f"slot_ready{i}") for i in range(WIDE)]
    k.ready = lambda n: k.slot_ready[Ring.slot_of(n)]
    k.slot_freed = k.sem("slot_freed")
    k.use = Ring()
    k.passed = {name: k.sem(f"{name}_passed") for name in ENGINES}
    k.x = k.arena[:, X0:X0 + ST * D].rearrange("p (t d) -> p t d", t=ST)
    k.hT = k.arena[:, HT0:HT0 + DK * S].rearrange("p (k s) -> p k s", k=DK)
    k.ident = fix(k, "ident")
    return k


def fix(k, name):
    a, w = FIX[name]
    return k.arena[:, a:a + w]


def slot(k, n, width=SLOT):
    s = Ring.slot_of(n)
    if s >= SLOTS:
        return k.work[:, (s - SLOTS) * SLOT:(s - SLOTS) * SLOT + width]
    return k.ring[:, s * SLOT:s * SLOT + width]


def area(core, at, width, /, **shape):
    return view(core.arena[:, R0 + at:R0 + at + width], **shape)


def work(core, at, width, /, **shape):
    return view(core.work[:, at:at + width], **shape)


def view(v, /, **shape):
    if not shape:
        return v
    names = list(shape)
    return v.rearrange(f"p ({' '.join(names)} z) -> p {' '.join(names)} z", **shape)


def load_slots(k, sync, weights):
    for n, pairs in weights:
        if k.use.freed[n]:
            sync.wait_ge(k.slot_freed, k.use.freed[n])
        for dst, src in pairs:
            sync.dma_start(dst, src).then_inc(k.ready(n), 16)


def range_reduce(step, vector, out, angle, n):
    magic = 12582912.0
    c1 = 6.28125
    c2 = float(np.float32(np.round((2 * math.pi - c1) * 2 ** 21) / 2 ** 21))
    c3 = float(np.float32(2 * math.pi - c1 - c2))
    step(vector.tensor_scalar(n, angle, 1.0 / (2 * math.pi), magic, ALU.mult, ALU.add))
    step(vector.tensor_scalar(n, n, magic, None, ALU.subtract))
    step(vector.scalar_tensor_tensor(out=out, in0=n, scalar=-c1, in1=angle, op0=ALU.mult, op1=ALU.add))
    step(vector.scalar_tensor_tensor(out=out, in0=n, scalar=-c2, in1=out, op0=ALU.mult, op1=ALU.add))
    step(vector.scalar_tensor_tensor(out=out, in0=n, scalar=-c3, in1=out, op0=ALU.mult, op1=ALU.add))
    return vector.tensor_scalar(out, out, 3.1415925, -3.1415925, ALU.min, ALU.max)


def misc(k, a, w):
    b = FIX["misc"][0]
    return k.arena[:, b + a:b + a + w]


def filters(k, x, fixed, dft, filt_tables, filt_w1, filt_w2, filt_w3, zT):
    sem = k.sem
    x_loaded, fixed_loaded, tables_loaded = sem("x_loaded"), sem("fixed_loaded"), sem("tables_loaded")
    ones_set, square_sum, root, normed = sem("ones_set"), sem("ms_ready"), sem("ms_root"), sem("normed")
    turned, sin_arg, sin_done = sem("turned"), sem("sin_arg"), sem("sin_done")
    layer_done, taps_ready, taps_put = sem("layer_done"), sem("taps_ready"), sem("taps_put")
    abs_done, l1_done, l1_inverse = sem("abs_done"), sem("l1_done"), sem("l1_inverse")
    freq_ready, freq_put, hT_put, hT_bank = sem("freq_ready"), sem("freq_put"), sem("hT_put"), sem("hT_bank")

    K = area(k, 0, 4096, o=NORD, m=FM)
    Kn = area(k, 4096, 1024, o=NORD)
    k.K, k.Kn = K, Kn
    dft_sb = area(k, 5120, 2048)
    k.Fwd = view(dft_sb[:, 0:1024], t=ST)
    k.Inv = view(dft_sb[:, 1024:2048], m=FM)
    tab = work(k, 1024, 1024)
    decay = view(tab, t=ST)
    w3 = work(k, 2048, 2048)
    taps = work(k, 4096, 4096, t=ST, n=4)
    z_sb = work(k, 8192, 256)
    w1, w2 = work(k, 8448, 64), work(k, 8512, 64)
    arg, hid, nrev = work(k, 8576, 256), work(k, 8832, 256), work(k, 9088, 256)
    mag = work(k, 9344, 1024, b=2)
    inv = work(k, 10368, 1024, o=2)
    xn = area(k, 7168, 2048, t=ST)
    plus = [area(k, 7168 + 1024 * o, 1024, t=ST) for o in range(NORD)]
    minus = [work(k, 0, 1024, t=ST), area(k, 9216, 1024, t=ST)]
    pairs_put = sem("pairs_put")
    ones, ones0 = fix(k, "ones"), fix(k, "ones0")
    stat = misc(k, 0, 8)
    filt = fix(k, "filt")

    def load(sync):
        sync.dma_start(k.x, x.rearrange("b (t p) d -> p (b t) d", p=P)).then_inc(x_loaded, 16)
        sync.dma_start(k.arena[:, 0:LOADED], fixed).then_inc(fixed_loaded, 16)

    def scalar(act):
        for dst, src in ((z_sb[0:EMB, :], zT), (w1[0:EMB, :], filt_w1[0]), (w2[0:HID, :], filt_w2[0]),
                         (w3[0:HID, :], filt_w3[0]), (tab, filt_tables), (dft_sb, dft)):
            act.dma_start(dst, src).then_inc(tables_loaded, 16)
        act.wait_ge(square_sum, 1)
        act.activation(stat[:, 2:4], stat[:, 2:4], ACT.Sqrt).then_inc(root, 1)
        for layer in range(2):
            act.wait_ge(sin_arg, layer + 1)
            act.activation(hid[0:HID, :], arg[0:HID, :], ACT.Sin).then_inc(sin_done, 1)
        for i in range(ST * 4):
            act.wait_ge(taps_put, i + 1)
            if i >= 2:
                act.wait_ge(l1_done, i - 1)
            act.activation(mag[:, i % 2, :], taps[:, i // 4, i % 4, :], ACT.Abs).then_inc(abs_done, 1)

    def tensor(pe):
        pe.wait_ge(fixed_loaded, 16)
        pe.wait_ge(normed, 2)
        for b in range(4):
            for j in range(4):
                kk, t = 2 * b + j // 2, j % 2
                last = pe.transpose(k.ps[:, b, j * P:(j + 1) * P], xn[:, t, kk * P:(kk + 1) * P], k.ident)
            last.then_inc(hT_bank, 1)
        pe.wait_ge(tables_loaded, 16 * 6)
        pe.matmul(k.ps[0:HID, 4, 0:S], w1[0:EMB, :], z_sb[0:EMB, :], start=True, stop=True).then_inc(layer_done, 1)
        pe.wait_ge(sin_done, 1)
        pe.matmul(k.ps[0:HID, 5, 0:S], w2[0:HID, :], hid[0:HID, :], start=True, stop=True).then_inc(layer_done, 1)
        pe.wait_ge(sin_done, 2)
        pe.wait_ge(hT_put, DK)
        for i in range(ST * 4):
            t, n = i // 4, i % 4
            if i >= 4:
                pe.wait_ge(taps_put, i - 3)
            pe.matmul(k.ps[:, i % 4, :], hid[0:HID, t * P:(t + 1) * P], w3[0:HID, n * HY:(n + 1) * HY],
                      start=True, stop=True).then_inc(taps_ready, 1)
        for i in range(ST * 4):
            t, n = i // 4, i % 4
            direction, order = n // 2, n % 2
            pe.wait_ge(abs_done, i + 1)
            pe.matmul(k.ps[:, 6 + order, :], ones0 if direction and t == 0 else ones, mag[:, i % 2, :],
                      start=(t == 0 and direction == 0), stop=(t == ST - 1 and direction == 1)).then_inc(l1_done, 1)
        pe.wait_ge(pairs_put, 4 * ST)
        for i in range(NORD * (FM + 1)):
            order, m = i // (FM + 1), i % (FM + 1)
            if i >= 4:
                pe.wait_ge(freq_put, i - 3)
            cols, src = (slice(m * P, (m + 1) * P), (plus if m < 2 else minus)) if m < FM else (slice(S, S + 1), plus)
            for t in range(ST):
                last = pe.matmul(k.ps[0:cols.stop - cols.start, i % 4, :], k.Fwd[:, t, cols], src[order][:, t, :],
                                 start=(t == 0), stop=(t == ST - 1))
            last.then_inc(freq_ready, 1)

    def vector(dve):
        step = k.vector_order.on(dve)
        dve.wait_ge(x_loaded, 16)
        for t in range(ST):
            step(dve.tensor_tensor_reduce(xn[:, t, :], k.x[:, t, :], k.x[:, t, :], 1.0, 0.0, ALU.mult, ALU.add,
                                          stat[:, t:t + 1]))
        dve.tensor_scalar(stat[:, 2:4], stat[:, 0:2], 1.0 / D, EPS, ALU.mult, ALU.add).then_inc(square_sum, 1)
        dve.wait_ge(root, 1)
        step(dve.reciprocal(stat[:, 4:6], stat[:, 2:4]))
        for t in range(ST):
            dve.tensor_scalar(xn[:, t, :], k.x[:, t, :], stat[:, 4 + t:5 + t], None, ALU.mult).then_inc(normed, 1)
        dve.wait_ge(fixed_loaded, 16)
        for kk in range(DK):
            dve.wait_ge(hT_bank, kk // 2 + 1)
            dve.tensor_scalar(k.hT[:, kk, :], k.ps[:, kk // 2, (kk % 2) * S:(kk % 2 + 1) * S],
                              fix(k, "attn_g")[:, kk:kk + 1], None, ALU.mult).then_inc(hT_put, 1)
        for layer in range(2):
            dve.wait_ge(layer_done, layer + 1)
            step(dve.tensor_scalar(arg[0:HID, :], k.ps[0:HID, 4 + layer, 0:S], filt[0:HID, layer:layer + 1],
                                   filt[0:HID, 2:3], ALU.add, ALU.mult))
            range_reduce(step, dve, arg[0:HID, :], arg[0:HID, :], nrev[0:HID, :]).then_inc(sin_arg, 1)
        for i in range(ST * 4):
            t, n = i // 4, i % 4
            dve.wait_ge(taps_ready, i + 1)
            last = dve.tensor_tensor(taps[:, t, n, :], k.ps[:, i % 4, :], decay[:, t, :], ALU.mult)
            if t == 0 and n >= 2:
                step(last)
                last = dve.memset(taps[0:1, 0, n, :], 0.0)
            last.then_inc(taps_put, 1)
        dve.wait_ge(taps_put, ST * 4)
        for t in range(ST):
            for order in range(NORD):
                dve.tensor_tensor(plus[order][:, t, :], taps[:, t, order, :], taps[:, t, 2 + order, :],
                                  ALU.add).then_inc(pairs_put, 1)
                dve.tensor_tensor(minus[order][:, t, :], taps[:, t, order, :], taps[:, t, 2 + order, :],
                                  ALU.subtract).then_inc(pairs_put, 1)
        dve.wait_ge(l1_done, ST * 4)
        for order in range(NORD):
            step(dve.reciprocal(inv[:, order, :], k.ps[:, 6 + order, :]))
        for i in range(NORD * (FM + 1)):
            order, m = i // (FM + 1), i % (FM + 1)
            dve.wait_ge(freq_ready, i + 1)
            if m < FM:
                dve.tensor_tensor(K[:, order, m, :], k.ps[:, i % 4, :], inv[:, order, :], ALU.mult).then_inc(freq_put, 1)
                continue
            dve.wait_ge(freq_put, i)
            step(dve.tensor_copy(Kn[:, order, :], K[:, order, 0, :]))
            dve.tensor_tensor(Kn[0:1, order, :], k.ps[0:1, i % 4, :], inv[0:1, order, :], ALU.mult).then_inc(freq_put, 1)
            step(dve.memset(K[0:1, order, 2, :], 0.0))

    return load, Stage(tensor, scalar, vector)


def projections(k):
    sem = k.sem
    column_done, convolved, copied = sem("column_done"), sem("convolved"), sem("copied")
    centre_put = sem("centre_put")
    k.h_splits, k.w_splits = DK, W_IN_TILES
    win_high, win_split, hT_high, hT_split = (sem(f"ffn_{s}") for s in ("w13_high", "w13_split", "h_high", "h_split"))
    u = work(k, 0, 3072, c=12)
    qk = work(k, 3072, 2048, c=8)
    v = work(k, 5120, 1024, t=ST)
    k.u, k.qk, k.v = u, qk, v
    conv_w, conv_b = fix(k, "conv_w"), fix(k, "conv_b")

    AHEAD = HIGHS - 2
    PASSES = ((0, 0), (0, 1), (1, 0))
    w_parts = lambda c: (k.w_high[:, c % HIGHS], k.w_low[:, c])
    v_parts = (k.w_high[:, 20 % HIGHS:], k.w_low[:, 20:])
    h_parts = (k.hT_high, k.hT_low)

    def tensor(pe):
        for c in range(20):
            if 6 <= c < 18:
                pe.wait_ge(convolved, c - 5)
            elif c >= 18:
                pe.wait_ge(copied, c - 17)
            pe.wait_ge(win_split, c + 1)
            for kk in range(DK):
                if c == 0:
                    pe.wait_ge(hT_split, kk + 1)
                for n, (i, j) in enumerate(PASSES):
                    last = pe.matmul(k.ps[:, c % 6, 0:S], w_parts(c)[i][:, kk, :], h_parts[j][:, kk, :],
                                     start=(kk == 0 and n == 0), stop=(kk == DK - 1 and n == 2))
            last.then_inc(column_done, 1)
        pe.wait_ge(win_split, W_IN_TILES)
        for t in range(ST):
            for kk in range(DK):
                for n, (i, j) in enumerate(PASSES):
                    last = pe.matmul(k.ps[:, 6 + t, :], h_parts[i][:, kk, t * P:(t + 1) * P], v_parts[j][:, :, kk, :],
                                     start=(kk == 0 and n == 0), stop=(kk == DK - 1 and n == 2))
            last.then_inc(column_done, 1)
        pe.drain().then_inc(k.slot_freed, DK)

    def raw(c):
        return slot(k, c // 3)[:, (c % 3) * D:(c % 3 + 1) * D].rearrange("p (k f) -> p k f", k=DK)

    def scalar(act):
        def high(c):
            if c % 3 == 0:
                act.wait_ge(k.ready(c // 3), 16)
            act.activation(k.w_high[:, c % HIGHS], raw(c), ACT.Copy).then_inc(win_high, 1)

        for kk in range(DK):
            act.activation(k.hT_high[:, kk, :], k.hT[:, kk, :], ACT.Copy).then_inc(hT_high, 1)
            if kk == 0:
                high(0)
        for c in range(1, AHEAD):
            high(c)
        for c in range(20):
            act.wait_ge(column_done, c + 1)
            if c < 12:
                act.activation(u[:, c, :], k.ps[:, c % 6, 0:S], ACT.Identity, scale=conv_w[:, 12 + c:13 + c],
                               bias=conv_b[:, c:c + 1]).then_inc(centre_put, 1)
            else:
                act.activation(qk[:, c - 12, :], k.ps[:, c % 6, 0:S], ACT.Copy).then_inc(copied, 1)
            high(c + AHEAD)
        for t in range(ST):
            act.wait_ge(column_done, 21 + t)
            act.activation(v[:, t, :], k.ps[:, 6 + t, :], ACT.Copy)

    def vector(dve):
        step = k.vector_order.on(dve)

        def low(c):
            dve.wait_ge(win_high, c + 1)
            dve.tensor_tensor(k.w_low[:, c], raw(c), k.w_high[:, c % HIGHS].bitcast(F32), ALU.subtract).then_inc(win_split, 1)

        for kk in range(DK):
            dve.wait_ge(hT_high, kk + 1)
            dve.tensor_tensor(k.hT_low[:, kk, :], k.hT[:, kk, :], k.hT_high[:, kk, :].bitcast(F32),
                              ALU.subtract).then_inc(hT_split, 1)
            if kk == 0:
                low(0)
        for c in range(1, AHEAD):
            low(c)
        for c in range(20):
            if c < 12:
                dve.wait_ge(centre_put, c + 1)
                step(dve.scalar_tensor_tensor(out=u[:, c, 1:S], in0=k.ps[:, c % 6, 0:S - 1], scalar=conv_w[:, c:c + 1],
                                              in1=u[:, c, 1:S], op0=ALU.mult, op1=ALU.add))
                dve.scalar_tensor_tensor(out=u[:, c, 0:S - 1], in0=k.ps[:, c % 6, 1:S],
                                         scalar=conv_w[:, 24 + c:25 + c], in1=u[:, c, 0:S - 1], op0=ALU.mult,
                                         op1=ALU.add).then_inc(convolved, 1)
            low(c + AHEAD)

    return Stage(tensor, scalar, vector)


def hyena(k):
    sem = k.sem
    z_turned, z_put, spectrum_done = sem("z_turned"), sem("z_put"), sem("spectrum_done")
    product_put, mixed, wave_done = sem("product_put"), sem("mixed"), sem("wave_done")
    hy_square, hy_mean, hy_root = sem("hy_square"), sem("hy_mean"), sem("hy_root")
    gated, hy_inverse, inverse_turned = sem("gated"), sem("hy_inverse"), sem("inverse_turned")
    U, K, Kn = k.u, k.K, k.Kn
    prods = area(k, 7168, 2048, n=4), work(k, 9216, 2048, n=4)
    mixed_dve = sem("mixed_dve")
    Y = work(k, 6144, 2048, m=FM)
    zs = work(k, 8192, 1024, t=ST)
    mixT = k.hT
    tmp = area(k, 9216, 1024, c=HC)
    inverse = area(k, 7168, 1024, c=2 * HC)
    m = misc(k, 9, 16)
    z = U[:, 8:12, :]

    def tensor(pe):
        for o in range(NORD):
            if o:
                pe.wait_ge(gated, HC)
            for t in range(ST):
                for c in range(HC):
                    last = pe.transpose(k.ps[:, t, c * P:(c + 1) * P], z[:, c, t * P:(t + 1) * P], k.ident)
            last.then_inc(z_turned, 1)
            pe.wait_ge(z_put, ST * (o + 1))
            for m in (0, 2, 1, 3):
                if m == 0 and o:
                    pe.wait_ge(mixed, 3)
                    pe.wait_ge(mixed_dve, 1)
                for t in range(ST):
                    last = pe.matmul(k.ps[:, 2 + m, :], k.Fwd[:, t, m * P:(m + 1) * P], zs[:, t, :],
                                     start=(t == 0), stop=(t == ST - 1))
                last.then_inc(spectrum_done, 1)
            pe.wait_ge(mixed, 3 * (o + 1))
            pe.wait_ge(mixed_dve, o + 1)
            for c in range(HC):
                if c >= 2:
                    pe.wait_ge(gated, HC * o + c - 1)
                for m in range(FM):
                    last = pe.matmul(k.ps[:, 6 + c % 2, 0:S], Y[:, m, c * P:(c + 1) * P], k.Inv[:, m, :],
                                     start=(m == 0), stop=(m == FM - 1))
                last.then_inc(wave_done, 1)
        for c in range(HC):
            pe.wait_ge(hy_square, c + 1)
            for t in range(ST):
                at = 2 * (ST * c + t)
                last = pe.matmul(k.ps[:, 0, at:at + 2], tmp[:, c, t * P:(t + 1) * P], fix(k, "group_mean")[:, 0:P:P // 2],
                                 start=True, stop=True)
        last.then_inc(hy_mean, 1)
        pe.wait_ge(hy_inverse, 1)
        for b in range(2):
            for j in range(4):
                last = pe.transpose(k.ps[:, 2 + b, j * P:(j + 1) * P], inverse[:, 4 * b + j, :], k.ident)
            last.then_inc(inverse_turned, 1)

    def gpsimd(pool):
        for o in range(NORD):
            for h in range(2):
                prod = prods[h]
                pool.wait_ge(product_put, 8 * o + 4 * h + 4)
                if h == 0:
                    pool.tensor_tensor(Y[:, h, :], prod[:, 0, :], prod[:, 1, :], ALU.subtract).then_inc(mixed, 1)
                pool.tensor_tensor(Y[:, 2 + h, :], prod[:, 2, :], prod[:, 3, :], ALU.add).then_inc(mixed, 1)

    def scalar(act):
        for o in range(NORD):
            act.wait_ge(z_turned, o + 1)
            for t in range(ST):
                act.activation(zs[:, t, :], k.ps[:, t, :], ACT.Copy).then_inc(z_put, 1)
        for c in range(HC):
            act.wait_ge(gated, HC + c + 1)
            act.activation(tmp[:, c, :], z[:, c, :], ACT.Square).then_inc(hy_square, 1)
        act.wait_ge(hy_mean, 1)
        act.activation(m, k.ps[:, 0, 0:4 * HC], ACT.Sqrt, bias=misc(k, 8, 1)).then_inc(hy_root, 1)

    def vector(dve):
        step = k.vector_order.on(dve)
        step(dve.memset(misc(k, 8, 1), EPS))
        for o in range(NORD):
            for h in range(2):
                dve.wait_ge(spectrum_done, 4 * o + 2 * h + 2)
                re, im = k.ps[:, 2 + h, :], k.ps[:, 4 + h, :]
                prod = prods[h]
                if o:
                    dve.wait_ge(mixed, 3 * o)
                for i, (a, b) in enumerate(((re, K[:, o, h, :]), (im, K[:, o, 2 + h, :]),
                                            (im, Kn[:, o, :] if h == 0 else K[:, o, 1, :]),
                                            (re, K[:, o, 2 + h, :]))):
                    dve.tensor_tensor(prod[:, i, :], a, b, ALU.mult).then_inc(product_put, 1)
            dve.wait_ge(product_put, 8 * o + 6)
            dve.tensor_tensor(Y[:, 1, :], prod[:, 0, :], prod[:, 1, :], ALU.subtract).then_inc(mixed_dve, 1)
            dve.wait_ge(gated, HC * o)
            for c in range(HC):
                dve.wait_ge(wave_done, HC * o + c + 1)
                step(dve.scalar_tensor_tensor(out=z[:, c, :], in0=z[:, c, :],
                                              scalar=fix(k, "skip")[:, 4 * o + c:4 * o + c + 1],
                                              in1=k.ps[:, 6 + c % 2, 0:S], op0=ALU.mult, op1=ALU.add))
                dve.tensor_tensor(z[:, c, :], z[:, c, :], U[:, 4 * o + c, :], ALU.mult).then_inc(gated, 1)
        dve.wait_ge(hy_root, 1)
        step(dve.reciprocal(m, m))
        dve.tensor_copy(inverse.rearrange("p c (g d) -> p (c g) d", g=2),
                        m.unsqueeze(2).to_broadcast([P, 4 * HC, P // 2])).then_inc(hy_inverse, 1)
        for c in range(HC):
            dve.wait_ge(inverse_turned, c // 2 + 1)
            dve.scalar_tensor_tensor(out=mixT[:, c, :], in0=z[:, c, :], scalar=fix(k, "hy_g")[:, c:c + 1],
                                     in1=k.ps[:, 2 + c // 2, (c % 2) * S:(c % 2 + 1) * S], op0=ALU.mult, op1=ALU.mult)

    return Stage(tensor, scalar, vector, gpsimd)


def skewed(heads, first, second, third):
    for h in range(heads + 2):
        if h < heads:
            first(h)
        if h >= 2 and third:
            third(h - 2)
        if 1 <= h <= heads and second:
            second(h - 1)


def attention(k, dist, lam_rows):
    sem = k.sem
    dist_loaded, score_done = sem("dist_loaded"), sem("score_done")
    score_read, score_put = sem("score_read"), sem("score_put")
    exp_done, lam_arg, lam_exp = sem("exp_done"), sem("lam_arg"), sem("lam_exp")
    a_put, a_turned, aT_put, o_done, o_put = sem("p_put"), sem("p_turned"), sem("pT_put"), sem("o_done"), sem("o_put")
    sq_put, ms_done, at_root = sem("sq_put"), sem("ms_done"), sem("at_root")
    mixT = k.hT
    dist_sb = area(k, 0, 512, t=ST)
    lam_sb = area(k, 512, 256)
    s = area(k, 1024, 2048, b=2, n=4)
    a = area(k, 3072, 1024, b=2, t=ST)
    aT = area(k, 4096, 1024, b=2, t=ST)
    oT = area(k, 5120, 1024, h=HEADS)
    sq = area(k, 6144, 1024, n=2)
    rt = area(k, 7168, 1024, n=8)
    m = misc(k, 10, 30)
    root = m[:, 8:16]
    at_inverse, inverse_turned = sem("at_inverse"), sem("inverse_turned")
    lam = m[:, 0:1]
    scale = DH ** -0.5
    slopes = [float(np.float32(2.0 ** (-8.0 * (i + 1) / HEADS))) for i in range(HEADS)]

    def tensor(pe):
        def scores(h):
            if h >= 2:
                pe.wait_ge(score_read, 2 * (h - 1))
            for c in range(2):
                for t in range(ST):
                    last = pe.matmul(k.ps[:, 2 * (h % 2) + c, t * S:(t + 1) * S],
                                     k.qk[c * DH:(c + 1) * DH, h, t * P:(t + 1) * P],
                                     k.qk[c * DH:(c + 1) * DH, HEADS + h, :], start=True, stop=True)
                last.then_inc(score_done, 1)

        def turn(h):
            pe.wait_ge(a_put, ST * (h + 1))
            if h >= 2:
                pe.wait_ge(aT_put, h - 1)
            for t in range(ST):
                for kc in range(ST):
                    last = pe.transpose(k.ps[:, 4 + h % 2, kc * S + t * P:kc * S + (t + 1) * P],
                                        a[:, h % 2, t, kc * P:(kc + 1) * P], k.ident)
            last.then_inc(a_turned, 1)

        def outputs(h):
            pe.wait_ge(aT_put, h + 1)
            if h >= 2:
                pe.wait_ge(o_put, h - 1)
            for kc in range(ST):
                last = pe.matmul(k.ps[:, 6 + h % 2, 0:S], k.v[:, kc, h * P:(h + 1) * P], aT[:, h % 2, kc, :],
                                 start=(kc == 0), stop=(kc == ST - 1))
            last.then_inc(o_done, 1)

        scores(0)
        skewed(HEADS, lambda h: scores(h + 1) if h + 1 < HEADS else None, turn, outputs)
        for n in range(2):
            pe.wait_ge(sq_put, n + 1)
            for i in range(4):
                last = pe.matmul(k.ps[:, 0, 4 * n + i:4 * n + i + 1], sq[:, n, i * P:(i + 1) * P], fix(k, "ones")[:, 0:1],
                                 start=True, stop=True)
        last.then_inc(ms_done, 1)
        pe.wait_ge(at_inverse, 1)
        for b in range(2):
            for j in range(4):
                last = pe.transpose(k.ps[:, 1 + b, j * P:(j + 1) * P], rt[:, 4 * b + j, :], k.ident)
            last.then_inc(inverse_turned, 1)

    def scalar(act):
        act.dma_start(dist_sb, dist).then_inc(dist_loaded, 16)
        act.dma_start(lam_sb, lam_rows).then_inc(dist_loaded, 16)
        act.wait_ge(lam_arg, 2)
        act.activation(m[:, 1:3], m[:, 1:3], ACT.Exp).then_inc(lam_exp, 1)
        def exponentials(h):
            act.wait_ge(score_put, h + 1)
            for n in range(4):
                act.activation(s[:, h % 2, n, :], s[:, h % 2, n, :], ACT.Exp, scale=scale,
                               bias=m[:, 8 + 4 * (h % 2) + n:9 + 4 * (h % 2) + n],
                               accum_out=m[:, 16 + 4 * (h % 2) + n:17 + 4 * (h % 2) + n]).then_inc(exp_done, 1)

        def output(h):
            act.wait_ge(o_done, h + 1)
            act.activation(oT[:, h, :], k.ps[:, 6 + h % 2, 0:S], ACT.Copy).then_inc(o_put, 1)

        skewed(HEADS, exponentials, None, output)
        for n in range(2):
            act.wait_ge(o_put, HEADS)
            act.activation(sq[:, n, :], oT[:, 2 * n:2 * n + 2, :], ACT.Square).then_inc(sq_put, 1)
        act.wait_ge(ms_done, 1)
        act.activation(root, k.ps[:, 0, 0:8], ACT.Sqrt, scale=1.0 / P, bias=misc(k, 8, 1)).then_inc(at_root, 1)

    def vector(dve):
        step = k.vector_order.on(dve)
        dve.wait_ge(dist_loaded, 32)
        for i in range(2):
            dve.tensor_tensor_reduce(lam_sb[:, 2 * i * DH:(2 * i + 1) * DH], lam_sb[:, 2 * i * DH:(2 * i + 1) * DH],
                                     lam_sb[:, (2 * i + 1) * DH:(2 * i + 2) * DH], 1.0, 0.0, ALU.mult, ALU.add,
                                     m[:, 1 + i:2 + i]).then_inc(lam_arg, 1)
        step(dve.tensor_scalar(m[:, 3:4], fix(k, "subln_g"), 1.0 - LAM_INIT, None, ALU.mult))
        dve.wait_ge(lam_exp, 1)
        step(dve.tensor_tensor(m[:, 0:1], m[:, 1:2], m[:, 2:3], ALU.subtract))
        step(dve.tensor_scalar(m[:, 0:1], m[:, 0:1], LAM_INIT, None, ALU.add))

        def score(h):
            b = h % 2
            if h >= 2:
                dve.wait_ge(a_put, ST * (h - 1))
            for c in range(2):
                dve.wait_ge(score_done, 2 * h + c + 1)
                dve.scalar_tensor_tensor(out=s[:, b, 2 * c:2 * c + 2, :], in0=dist_sb, scalar=-slopes[h] / scale,
                                         in1=k.ps[:, 2 * b + c, :].rearrange("p (t s) -> p t s", t=ST),
                                         op0=ALU.mult, op1=ALU.add).then_inc(score_read, 1)
            dve.wait_ge(score_read, 2 * h + 2)
            step(dve.tensor_reduce(m[:, 8 + 4 * b:12 + 4 * b], s[:, b], AX, ALU.max))
            dve.tensor_scalar(m[:, 8 + 4 * b:12 + 4 * b], m[:, 8 + 4 * b:12 + 4 * b], -scale, None,
                              ALU.mult).then_inc(score_put, 1)

        def combine(h):
            b = h % 2
            r = m[:, 16 + 4 * b:20 + 4 * b]
            dve.wait_ge(exp_done, 4 * h + 4)
            step(dve.reciprocal(r, r))
            step(dve.tensor_scalar(r[:, 2:4], r[:, 2:4], lam, None, ALU.mult))
            for t in range(ST):
                step(dve.tensor_scalar(s[:, b, 2 + t, :], s[:, b, 2 + t, :], r[:, 2 + t:3 + t], None, ALU.mult))
            for t in range(ST):
                dve.scalar_tensor_tensor(out=a[:, b, t, :], in0=s[:, b, t, :], scalar=r[:, t:t + 1],
                                         in1=s[:, b, 2 + t, :], op0=ALU.mult, op1=ALU.subtract).then_inc(a_put, 1)

        def turned(h):
            dve.wait_ge(a_turned, h + 1)
            dve.tensor_copy(aT[:, h % 2], k.ps[:, 4 + h % 2, :].rearrange("p (t s) -> p t s", t=ST)).then_inc(aT_put, 1)

        skewed(HEADS, score, combine, turned)
        dve.wait_ge(at_root, 1)
        step(dve.reciprocal(root, root))
        dve.tensor_copy(rt, root.unsqueeze(2).to_broadcast([P, 8, P])).then_inc(at_inverse, 1)
        for n in range(2):
            dve.wait_ge(inverse_turned, 2 + n + 1)
            dve.scalar_tensor_tensor(out=mixT[:, HC + 2 * n:HC + 2 * n + 2, :], in0=oT[:, 2 * n:2 * n + 2, :],
                                     scalar=m[:, 3:4], in1=k.ps[:, 1 + n, :].rearrange("p (h s) -> p h s", h=2), op0=ALU.mult, op1=ALU.mult)

    return Stage(tensor, scalar, vector)


def mixer_out(k, first, mixT, seed=None):
    out_done = k.sem("out_done")

    def tensor(pe):
        if seed is not None:
            residual(k, pe, seed)
        for n in range(first, first + 3):
            pe.wait_ge(k.ready(n), k.use.mark[n])
        for t in range(ST):
            for half in range(2):
                for kk in range(DK):
                    w = slot(k, first + kk // 3)[:, (kk % 3) * D + half * 512:(kk % 3) * D + (half + 1) * 512]
                    last = pe.matmul(k.ps[:, 2 * t + half, :], mixT[:, kk, t * P:(t + 1) * P], w,
                                     start=(kk == 0 and seed is None), stop=(kk == DK - 1), skip_group_check=True)
                last.then_inc(out_done, 1)
        pe.drain().then_inc(k.slot_freed, 3)

    return out_done, tensor


def routing(k, first_out):
    nc = k.nc
    sem = k.sem
    out_done, out_tensor = mixer_out(k, first_out, k.hT)
    ms_ready, rt_root, h_ready = sem("ms_ready"), sem("ms_root"), sem("rt_h_ready")
    hT_bank, hT_put, logits_done = sem("hT_bank"), sem("hT_put"), sem("logits_done")
    exp_arg, aff_exp, aff_ready, aff_turned = sem("exp_arg"), sem("aff_exp"), sem("aff_ready"), sem("aff_turned")
    slots_ready, slots_turned, pick_ready, weight_ready = sem("slots_ready"), sem("slots_turned"), sem("pick_ready"), sem("weight_ready")
    weight_turned, weight_put, xin_done, xin_put = sem("weight_turned"), sem("weight_put"), sem("xin_done"), sem("xin_put")
    router_loaded = sem("router_loaded")
    h = area(k, 2048, 2048, t=ST)
    pick = area(k, 4096, 1024, t=ST)
    k.weightT = area(k, 8960, 1024, q=NG)
    k.xin = k.arena[:, HT0:HT0 + 4096].rearrange("p (k c) -> p k c", k=DK)
    wr = area(k, 6144, 128, k=DK)
    logit = area(k, 6272, 32, t=ST)
    aff = area(k, 6304, 32, t=ST)
    affT = area(k, 6336, 256)
    left = area(k, 6592, 256)
    count = area(k, 6848, 256)
    top = area(k, 7104, 32)
    slot_of = area(k, 7136, 32, t=ST)
    pickw = area(k, 7168, 1024, t=ST)
    onesr = area(k, 8192, 256)
    m = misc(k, 10, 30)

    def tensor(pe):
        out_tensor(pe)
        pe.wait_ge(h_ready, 2)
        for b in range(4):
            for j in range(4):
                kk, t = 2 * b + j // 2, j % 2
                last = pe.transpose(k.ps[:, 4 + b, j * P:(j + 1) * P], h[:, t, kk * P:(kk + 1) * P], k.ident)
            last.then_inc(hT_bank, 1)
        pe.wait_ge(router_loaded, 16)
        for kk in range(DK):
            pe.wait_ge(hT_put, DK + kk + 1)
            for t in range(ST):
                last = pe.matmul(k.ps[:, t, 0:NE], k.hT[:, kk, t * P:(t + 1) * P], wr[:, kk, :],
                                 start=(kk == 0), stop=(kk == DK - 1))
        last.then_inc(logits_done, 1)
        pe.wait_ge(aff_ready, 1)
        for t in range(ST):
            last = pe.transpose(k.ps[0:NE, 2, t * P:(t + 1) * P], aff[:, t, :], k.ident)
        last.then_inc(aff_turned, 1)
        pe.wait_ge(slots_ready, 1)
        for t in range(ST):
            last = pe.transpose(k.ps[:, 3, t * NE:(t + 1) * NE], count[0:NE, t * P:(t + 1) * P], k.ident[0:NE, 0:NE])
        last.then_inc(slots_turned, 1)
        pe.wait_ge(pick_ready, 2)
        for kk in range(DK):
            if kk >= 4:
                pe.wait_ge(xin_put, kk - 3)
            for t in range(ST):
                last = pe.matmul(k.ps[:, 4 + kk % 4, :], h[:, t, kk * P:(kk + 1) * P], pick[:, t, :],
                                 start=(t == 0), stop=(t == ST - 1))
            last.then_inc(xin_done, 1)
        pe.wait_ge(weight_ready, 2)
        for q in range(NG):
            for t in range(ST):
                last = pe.transpose(k.ps[:, q // 2, (q % 2) * S + t * P:(q % 2) * S + (t + 1) * P],
                                    pickw[:, t, q * P:(q + 1) * P], k.ident)
            if q % 2:
                last.then_inc(weight_turned, 1)

    def scalar(act):
        act.dma_start(wr, k.w_router[0].rearrange("(k p) e -> p k e", p=P)).then_inc(router_loaded, 16)
        act.wait_ge(ms_ready, 2)
        act.activation(m[:, 2:4], m[:, 2:4], ACT.Sqrt).then_inc(rt_root, 1)
        act.wait_ge(exp_arg, 1)
        for t in range(ST):
            act.activation(aff[:, t, :], logit[:, t, :], ACT.Exp, bias=m[:, 6 + t:7 + t],
                           accum_out=m[:, 8 + t:9 + t]).then_inc(aff_exp, 1)
        for kk in range(DK):
            act.wait_ge(xin_done, kk + 1)
            act.activation(k.xin[:, kk, :], k.ps[:, 4 + kk % 4, :], ACT.Copy,
                           scale=fix(k, "ffn_g")[:, kk:kk + 1]).then_inc(xin_put, 1)

    def vector(dve):
        step = k.vector_order.on(dve)
        for t in range(ST):
            for half in range(2):
                dve.wait_ge(out_done, 2 * t + half + 1)
                part = k.x[:, t, half * 512:(half + 1) * 512]
                step(dve.tensor_tensor(part, part, k.ps[:, 2 * t + half, :], ALU.add))
            step(dve.tensor_tensor_reduce(h[:, t, :], k.x[:, t, :], k.x[:, t, :], 1.0, 0.0, ALU.mult, ALU.add,
                                          m[:, t:t + 1]))
        dve.tensor_scalar(m[:, 2:4], m[:, 0:2], 1.0 / D, EPS, ALU.mult, ALU.add).then_inc(ms_ready, 1)
        dve.memset(onesr[0:NE, :], 1.0)
        dve.wait_ge(rt_root, 2)
        step(dve.reciprocal(m[:, 4:6], m[:, 2:4]))
        for t in range(ST):
            dve.tensor_scalar(h[:, t, :], k.x[:, t, :], m[:, 4 + t:5 + t], None, ALU.mult).then_inc(h_ready, 1)
        for kk in range(DK):
            dve.wait_ge(hT_bank, 4 + kk // 2 + 1)
            dve.tensor_scalar(k.hT[:, kk, :], k.ps[:, 4 + kk // 2, (kk % 2) * S:(kk % 2 + 1) * S],
                              fix(k, "ffn_g")[:, kk:kk + 1], None, ALU.mult).then_inc(hT_put, 1)
        dve.wait_ge(logits_done, 1)
        step(dve.tensor_copy(logit, k.ps[:, 0:ST, 0:NE]))
        step(dve.tensor_reduce(m[:, 6:8], logit, AX, ALU.max))
        dve.tensor_scalar(m[:, 6:8], m[:, 6:8], -1.0, None, ALU.mult).then_inc(exp_arg, 1)
        dve.wait_ge(aff_exp, 2)
        step(dve.reciprocal(m[:, 8:10], m[:, 8:10]))
        for t in range(ST):
            last = dve.tensor_scalar(aff[:, t, :], aff[:, t, :], m[:, 8 + t:9 + t], None, ALU.mult)
            if t < ST - 1:
                step(last)
        last.then_inc(aff_ready, 1)
        dve.wait_ge(aff_turned, 1)
        step(dve.tensor_copy(left[0:NE, :], k.ps[0:NE, 2, 0:S]))
        for r in range(CAP // 8):
            step(dve.max(top[0:NE, 8 * r:8 * r + 8], left[0:NE, :]))
            step(dve.match_replace(out=left[0:NE, :], in_to_replace=top[0:NE, 8 * r:8 * r + 8],
                                   in_values=left[0:NE, :], imm_value=-1.0))
        step(dve.tensor_scalar(left[0:NE, :], left[0:NE, :], 0.0, None, ALU.is_lt))
        step(dve.tensor_tensor_scan(count[0:NE, :], onesr[0:NE, :], left[0:NE, :], 0.0, ALU.mult, ALU.add))
        step(dve.tensor_tensor(count[0:NE, :], count[0:NE, :], left[0:NE, :], ALU.mult))
        dve.tensor_scalar(count[0:NE, :], count[0:NE, :], 1.0, None, ALU.subtract).then_inc(slots_ready, 1)
        dve.wait_ge(slots_turned, 1)
        step(dve.tensor_copy(slot_of, k.ps[:, 3, 0:ST * NE].rearrange("p (t e) -> p t e", t=ST)))
        for t in range(ST):
            dve.tensor_tensor(pick[:, t, :].rearrange("p (e c) -> p e c", e=NE),
                              slot_of[:, t, :].unsqueeze(2).to_broadcast([P, NE, CAP]),
                              fix(k, "slot_no").unsqueeze(1).to_broadcast([P, NE, CAP]),
                              ALU.is_equal).then_inc(pick_ready, 1)
        dve.wait_ge(pick_ready, 2)
        for t in range(ST):
            dve.tensor_tensor(pickw[:, t, :].rearrange("p (e c) -> p e c", e=NE),
                              pick[:, t, :].rearrange("p (e c) -> p e c", e=NE),
                              aff[:, t, :].unsqueeze(2).to_broadcast([P, NE, CAP]), ALU.mult).then_inc(weight_ready, 1)
        for q in range(NG):
            dve.wait_ge(weight_turned, q // 2 + 1)
            dve.tensor_copy(k.weightT[:, q, :], k.ps[:, q // 2, (q % 2) * S:(q % 2 + 1) * S])

    return Stage(tensor, scalar, vector)


def experts(k, base, w_gate, w_up, w_down, final_norm_g, stages_before):
    nc = k.nc
    sem = k.sem
    x_ready, gate_up_done, silu_put, hidden_put = sem("ex_x_ready"), sem("gate_up_done"), sem("silu_put"), sem("hidden_put")
    turned, hidT_put, hidT_rest_put, down_done, y_put = sem("ex_turned"), sem("hidT_put"), sem("hidT_rest_put"), sem("down_done"), sem("y_put")
    xe = area(k, 6144, 256, k=DK)
    silu = area(k, 6400, FG)
    hidden = area(k, 6400 + FG, FG)
    hidT = area(k, 6400 + 2 * FG, (FT + 1) * P, m=FT + 1)
    k.final_g = area(k, 9984, D)
    k.Y = area(k, 2048, NG * D, q=NG)
    per = 3 * DK
    dmas = [1] * (2 * DK) + [1, 2] * NG
    mark = [k.use.landing(base + n, dmas[n]) for n in range(per)]
    again = [k.use.landing(base + per + n, dmas[n]) - mark[n] for n in range(per)]
    for e in range(2, NE):
        for n in range(per):
            k.use.landing(base + per * e + n, dmas[n])

    def load(sync):
        def expert(e):
            for n in range(per):
                s = slot(k, base + n)
                ready = k.ready(base + n)
                if isinstance(e, int) and n < WIDE:
                    if k.use.freed[base + n]:
                        sync.wait_ge(k.slot_freed, k.use.freed[base + n])
                    else:
                        for name in ("tensor", "scalar", "vector"):
                            sync.wait_ge(k.passed[name], stages_before)
                else:
                    sync.wait_ge(k.slot_freed, e * per + (base + n - WIDE + 1))
                if n < 2 * DK:
                    w, kk = (w_gate, w_up)[n % 2], n // 2
                    sync.dma_start(s[:, 0:FF], w[0, bass.ds(e, 1), kk * P:(kk + 1) * P, :].rearrange("e p f -> p (e f)")).then_inc(ready, 16)
                else:
                    g, part = (n - 2 * DK) // 2, n % 2
                    rows = FG * g + 3 * P * part
                    whole = 3 - part
                    sync.dma_start(s[:, 0:whole * D].rearrange("p (m d) -> p m d", m=whole),
                                   w_down[0, bass.ds(e, 1), rows:rows + whole * P, :].rearrange("e (m p) d -> p (e m) d", p=P)).then_inc(ready, 16)
                    if part:
                        sync.dma_start(s[0:FR, 2 * D:3 * D],
                                       w_down[0, bass.ds(e, 1), rows + 2 * P:rows + 2 * P + FR, :].rearrange("e p d -> p (e d)")).then_inc(ready, 16)

        expert(0)
        with sync.Fori(1, NE) as e:
            expert(e)

    def gpsimd(pool):
        with pool.Fori(0, NE) as e:
            pool.wait_ge(gate_up_done, e + 1)
            pool.tensor_copy(xe, k.xin[:, :, bass.ds(e * CAP, CAP)]).then_inc(x_ready, 1)

    def tensor(pe):
        pe.sem_inc(gate_up_done, 1)
        def expert(e, last_one=False):
            pe.wait_ge(x_ready, e + 1)
            for kk in range(DK):
                for w in range(2):
                    n = 2 * kk + w
                    pe.wait_ge(k.ready(base + n), e * again[n] + mark[n])
                    for half in range(2):
                        for g in range(NG):
                            last = pe.matmul(k.ps[32 * g:32 * g + CAP, 2 * w + half, 0:FH], xe[:, kk, :],
                                             slot(k, base + n)[:, g * FG + half * FH:g * FG + (half + 1) * FH],
                                             start=(kk == 0), stop=(kk == DK - 1))
                    if n < 2 * DK - 1:
                        last.then_inc(k.slot_freed, 1)
            last.then_inc(gate_up_done, 1)
            pe.wait_ge(hidden_put, e + 1)
            for m in range(FT + 1):
                w = P if m < FT else FR
                last = pe.transpose(k.ps[0:w, 4 + m // 4, (m % 4) * P:(m % 4 + 1) * P], hidden[:, m * P:m * P + w], k.ident)
                if m == 0:
                    last.then_inc(k.slot_freed, 1)
            last.then_inc(turned, 1)
            pe.wait_ge(hidT_put, e + 1)
            pe.wait_ge(hidT_rest_put, e + 1)
            pe.wait_ge(y_put, e + 1)
            if last_one:
                weighted_sums(k, pe, range(NG - 1))
            for g in range(NG):
                for m in range(FT + 1):
                    n = 2 * DK + 2 * g + m // 3
                    if m % 3 == 0:
                        pe.wait_ge(k.ready(base + n), e * again[n] + mark[n])
                    w = P if m < FT else FR
                    for j in range(NG):
                        last = pe.matmul(k.ps[32 * j:32 * j + CAP, 6, 0:256], hidT[0:w, m, 32 * g:32 * g + CAP],
                                         slot(k, base + n)[0:w, (m % 3) * D + j * 256:(m % 3) * D + (j + 1) * 256],
                                         start=(g == 0 and m == 0), stop=(g == NG - 1 and m == FT))
                    if m % 3 == 2 and not (g == NG - 1 and m == FT):
                        last.then_inc(k.slot_freed, 1)
            last.then_inc(down_done, 1)
            pe.drain().then_inc(k.slot_freed, 1)

        with pe.Fori(0, NE - 1) as e:
            expert(e)
        expert(NE - 1, last_one=True)

    def scalar(act):
        act.dma_start(k.final_g, final_norm_g.partition_broadcast(P)).then_inc(sem("g_loaded"), 16)
        with act.Fori(0, NE) as e:
            act.wait_ge(gate_up_done, e + 2)
            for half in range(2):
                act.activation(silu[:, half * FH:(half + 1) * FH], k.ps[:, half, 0:FH], ACT.Silu).then_inc(silu_put, 1)
            act.wait_ge(turned, e + 1)
            act.activation(hidT[:, 0:4, :], k.ps[:, 4, :], ACT.Copy).then_inc(hidT_put, 1)

    def vector(dve):
        dve.sem_inc(y_put, 1)
        with dve.Fori(0, NE // NG) as four:
            for i in range(NG):
                for half in range(2):
                    dve.wait_ge(silu_put, four * (2 * NG) + (2 * i + half + 1))
                    last = dve.tensor_tensor(hidden[:, half * FH:(half + 1) * FH], silu[:, half * FH:(half + 1) * FH],
                                             k.ps[:, 2 + half, 0:FH], ALU.mult)
                last.then_inc(hidden_put, 1)
                dve.wait_ge(turned, four * NG + (i + 1))
                dve.tensor_copy(hidT[:, 4, :], k.ps[:, 5, 0:P])
                dve.tensor_copy(hidT[0:FR, 5, :], k.ps[0:FR, 5, P:2 * P]).then_inc(hidT_rest_put, 1)
                dve.wait_ge(down_done, four * NG + (i + 1))
                for g in range(NG):
                    last = dve.tensor_copy(k.Y[CAP * i:CAP * (i + 1), bass.ds(four, 1), g * 256:(g + 1) * 256]
                                           .rearrange("p q d -> p (q d)"), k.ps[32 * g:32 * g + CAP, 6, 0:256])
                last.then_inc(y_put, 1)

    return load, Stage(tensor, scalar, vector, gpsimd)


def weighted_sums(k, pe, parts, done=None):
    for t in range(ST):
        for half in range(2):
            for q in parts:
                last = pe.matmul(k.ps[:, 2 * t + half, :], k.weightT[:, q, t * P:(t + 1) * P],
                                 k.Y[:, q, half * 512:(half + 1) * 512], start=(q == 0), stop=(q == NG - 1),
                                 skip_group_check=True)
            if done:
                last.then_inc(done, 1)


class Turn:

    def __init__(self, k):
        self.k, self.x_put, self.bank = k, k.sem("x_put"), k.sem("x_turned")

    def tensor(self, pe):
        k = self.k
        pe.wait_ge(self.x_put, 2 * ST)
        for b in range(4):
            for j in range(4):
                kk, t = 2 * b + j // 2, j % 2
                last = pe.transpose(k.ps[:, 4 + b, j * P:(j + 1) * P], k.x[:, t, kk * P:(kk + 1) * P], k.ident)
            last.then_inc(self.bank, 1)

    def copy(self, engine, write, banks):
        k = self.k
        for b in banks:
            engine.wait_ge(self.bank, b + 1)
            write(k.hT[:, 2 * b:2 * b + 2, :], k.ps[:, 4 + b, :].rearrange("p (k s) -> p k s", k=2))

    def scalar(self, act):
        self.copy(act, lambda out, src: act.activation(out, src, ACT.Copy), (1, 3))

    def vector(self, dve):
        self.copy(dve, lambda out, src: dve.tensor_copy(out, src), (0, 2))


def experts_combine(k):
    sem = k.sem
    g_loaded, sum_done = sem("g_loaded"), sem("sum_done")
    ms_ready, root, y_put = sem("ms_ready"), sem("ms_root"), sem("y_put")
    g = k.final_g
    sq = area(k, 7168, 1024)
    m = misc(k, 10, 30)
    turn = Turn(k)

    def tensor(pe):
        pe.wait_ge(y_put, NE + 1)
        weighted_sums(k, pe, [NG - 1], sum_done)
        turn.tensor(pe)

    def scalar(act):
        act.wait_ge(ms_ready, 3)
        act.activation(m[:, 2:4], m[:, 2:4], ACT.Sqrt).then_inc(root, 1)
        turn.scalar(act)

    def vector(dve):
        step = k.vector_order.on(dve)
        for t in range(ST):
            for half in range(2):
                dve.wait_ge(sum_done, 2 * t + half + 1)
                part = k.x[:, t, half * 512:(half + 1) * 512]
                step(dve.tensor_tensor(part, part, k.ps[:, 2 * t + half, :], ALU.add))
            step(dve.tensor_tensor_reduce(sq, k.x[:, t, :], k.x[:, t, :], 1.0, 0.0, ALU.mult, ALU.add, m[:, t:t + 1]))
        dve.tensor_scalar(m[:, 2:4], m[:, 0:2], 1.0 / D, EPS, ALU.mult, ALU.add).then_inc(ms_ready, 1)
        dve.wait_ge(root, 3)
        step(dve.reciprocal(m[:, 4:6], m[:, 2:4]))
        dve.wait_ge(g_loaded, 16)
        for t in range(ST):
            dve.scalar_tensor_tensor(out=k.x[:, t, :], in0=k.x[:, t, :], scalar=m[:, 4 + t:5 + t], in1=g,
                                     op0=ALU.mult, op1=ALU.mult).then_inc(turn.x_put, 2)
        turn.vector(dve)

    return Stage(tensor, scalar, vector)


class NormAndTurn:

    def __init__(self, k, sums_done, sums_before, factor):
        sem = k.sem
        self.k, self.sums_done, self.sums_before, self.factor = k, sums_done, sums_before, factor
        self.u = k.norms
        k.norms += 1
        self.var_ready, self.root, self.ab_ready = sem("ln_var_ready"), sem("ln_root"), sem("ln_ab_ready")
        self.normed = (sem("ln_normed_0"), sem("ln_normed_1"))
        self.turned = sem("ln_turned")
        self.m = misc(k, 0, 36)

    def of(self, t, a, w=1):
        return self.m[:, 18 * t + a:18 * t + a + w]

    def tensor(self, pe):
        k = self.k
        for t in range(ST):
            for half in range(2):
                pe.wait_ge(self.normed[t], 2 * self.u + half + 1)
                for j in range(4):
                    kk = 4 * half + j
                    last = pe.transpose(k.ps[:, 4 + 2 * t + half, j * P:(j + 1) * P], k.x[:, t, kk * P:(kk + 1) * P], k.ident)
                last.then_inc(self.turned, 1)

    def copy(self, engine, write, banks):
        k = self.k
        for t, half in banks:
            engine.wait_ge(self.turned, 2 * ST * self.u + 2 * t + half + 1)
            for j in range(4):
                kk = 4 * half + j
                g, b = (fix(k, n)[:, DK * self.u + kk:DK * self.u + kk + 1] for n in ("ln_g", "ln_b"))
                write(k.hT[:, kk, t * P:(t + 1) * P], k.ps[:, 4 + 2 * t + half, j * P:(j + 1) * P], g, b)

    def scalar(self, act):
        k = self.k
        for t in range(ST):
            act.wait_ge(self.var_ready, ST * self.u + t + 1)
            act.activation(self.of(t, 14), self.of(t, 14), ACT.Sqrt).then_inc(self.root, 1)
            if t == 0:
                act.wait_ge(self.ab_ready, self.u + 1)
                for half in range(2):
                    act.activation(k.x[:, 0, half * 512:(half + 1) * 512], k.ps[:, half, :], ACT.Identity,
                                   scale=self.of(0, 15), bias=self.of(0, 16)).then_inc(self.normed[0], 1)
        self.copy(act, lambda out, src, g, b: act.activation(out, src, ACT.Identity, scale=g, bias=b),
                  [(0, 0), (0, 1), (1, 0)])

    def vector(self, dve):
        k = self.k
        step = k.vector_order.on(dve)

        def statistics(t):
            for half in range(2):
                dve.wait_ge(self.sums_done, self.sums_before + 2 * t + half + 1)
                step(dve.bn_stats(self.of(t, 6 * half, 6), k.ps[:, 2 * t + half, :]))
            step(dve.bn_aggr(self.of(t, 12, 2), self.of(t, 0, 12)))
            dve.tensor_scalar(self.of(t, 14), self.of(t, 13), self.factor ** 2, LN_EPS, ALU.mult,
                              ALU.add).then_inc(self.var_ready, 1)

        def scale(t):
            dve.wait_ge(self.root, ST * self.u + t + 1)
            step(dve.reciprocal(self.of(t, 14), self.of(t, 14)))
            step(dve.tensor_scalar(self.of(t, 15), self.of(t, 14), self.factor, None, ALU.mult))
            return dve.tensor_scalar(self.of(t, 16), self.of(t, 12), self.of(t, 15), -1.0, ALU.mult, ALU.mult)

        statistics(0)
        scale(0).then_inc(self.ab_ready, 1)
        statistics(1)
        step(scale(1))
        for half in range(2):
            dve.tensor_scalar(k.x[:, 1, half * 512:(half + 1) * 512], k.ps[:, 2 + half, :], self.of(1, 15), self.of(1, 16),
                              ALU.mult, ALU.add).then_inc(self.normed[1], 1)
        self.copy(dve, lambda out, src, g, b: dve.tensor_scalar(out, src, g, b, ALU.mult, ALU.add), [(1, 1)])


def residual(k, pe, seed):
    for t in range(ST):
        for kk in range(DK):
            pe.matmul(k.ps[:, 2 * t + kk // 4, (kk % 4) * P:(kk % 4 + 1) * P], k.hT[:, kk, t * P:(t + 1) * P], seed,
                      start=(kk % 4 == 0), stop=False, skip_group_check=True)


FC = FF // P


def ffn_weights(k, base, w):
    loads = []
    for c in range(FC):
        k.use.landing(base + c)
        loads.append((base + c, [(slot(k, base + c), w[c])]))
    return loads


def ffn(k, u, base):
    sem = k.sem
    (h_high, h_split, w13_high, w2_high, w13_split, w2_split, pair_done, silu_put, hidden_put,
     hidden_high, hidden_split, sums_done) = (
        sem(f"ffn_{s}") for s in ("h_high", "h_split", "w13_high", "w2_high", "w13_split", "w2_split", "pair_done", "silu_put", "hidden_put", "hidden_high", "hidden_split",
                                  "sums_done"))
    norm = NormAndTurn(k, sums_done, 2 * ST * u, 0.5)
    silu = area(k, 0, 2 * S, n=2)
    hidden = area(k, 2 * S, 2 * S, n=2)
    assert R0 + 3072 <= ARENA - PARTS
    before = FC * u
    h_before, w_before = k.h_splits, k.w_splits
    k.h_splits, k.w_splits = h_before + DK, w_before + 2 * FC
    TURNS = FC // SLOTS

    def landed(c, e):
        return e * 16 + k.use.mark[base + c]

    def raw(c, w):
        return slot(k, base + c)[:, w * D:(w + 1) * D].rearrange("p (k f) -> p k f", k=DK)

    def tensor(pe):
        residual(k, pe, fix(k, "seed2"))

        def pair(c, e=0):
            b = c % 2
            for w in range(2):
                pe.wait_ge(w13_split, e * (2 * SLOTS) + (w_before + 2 * c + w + 1))
                for kk in range(DK):
                    if c == 0 and w == 0:
                        pe.wait_ge(h_split, h_before + kk + 1)
                    for n, (i, j) in enumerate(((0, 0), (0, 1), (1, 0))):
                        last = pe.matmul(k.ps[:, 4 + c % 4, w * S:(w + 1) * S], k.w13[:, b, w, i, kk, :],
                                         k.hsplit[:, j, kk, :], start=(kk == 0 and n == 0), stop=(kk == DK - 1 and n == 2))
            last.then_inc(pair_done, 1)

        def down(c, e=0):
            b = c % 2
            pe.wait_ge(w2_split, e * SLOTS + (before + c + 1))
            pe.wait_ge(hidden_split, e * SLOTS + (before + c + 1))
            for t in range(ST):
                for i, j in ((0, 0), (0, 1), (1, 0)):
                    for half in range(2):
                        last = pe.matmul(k.ps[:, 2 * t + half, :], k.hidsplit[:, b, i, t * P:(t + 1) * P],
                                         k.w2[:, b, j, half * 512:(half + 1) * 512], start=False, stop=False,
                                         skip_group_check=True)
                if c == FC - 1 and t == 0:
                    last.then_inc(sums_done, 2)
            last.then_inc(k.slot_freed, 1)

        pair(0)
        with pe.Fori(0, TURNS) as e:
            for c in range(SLOTS):
                pair(c + 1, e)
                down(c, e)
        for c in range(TURNS * SLOTS, FC):
            if c + 1 < FC:
                pair(c + 1)
            down(c)
        pe.drain().then_inc(sums_done, 2)
        norm.tensor(pe)

    def scalar(act):
        def pair_high(c, w, e=0):
            if w == 0:
                act.wait_ge(k.ready(base + c), landed(c, e))
            act.activation(k.w13[:, c % 2, w, 0], raw(c, w), ACT.Copy).then_inc(w13_high, 1)

        def down_high(c, e=0):
            if c:
                act.wait_ge(k.slot_freed, e * SLOTS + (base + c - 1))
            act.activation(k.w2[:, c % 2, 0], slot(k, base + c)[:, 2 * D:3 * D], ACT.Copy).then_inc(w2_high, 1)

        def chunk(c, e=0):
            act.wait_ge(pair_done, e * SLOTS + (before + c + 1))
            act.activation(silu[:, c % 2, :], k.ps[:, 4 + c % 4, 0:S], ACT.Silu).then_inc(silu_put, 1)
            if c + 2 < FC:
                pair_high(c + 2, 0, e)
            act.wait_ge(hidden_put, e * SLOTS + (before + c + 1))
            act.activation(k.hidsplit[:, c % 2, 0], hidden[:, c % 2, :], ACT.Copy).then_inc(hidden_high, 1)
            if c + 2 < FC:
                pair_high(c + 2, 1, e)
            if c + 1 < FC:
                down_high(c + 1, e)

        for kk in range(DK):
            act.activation(k.hsplit[:, 0, kk, :], k.hT[:, kk, :], ACT.Copy).then_inc(h_high, 1)
            if kk == 0:
                pair_high(0, 0)
                pair_high(0, 1)
        down_high(0)
        pair_high(1, 0)
        pair_high(1, 1)
        with act.Fori(0, TURNS) as e:
            for c in range(SLOTS):
                chunk(c, e)
        for c in range(TURNS * SLOTS, FC):
            chunk(c)
        norm.scalar(act)

    def vector(dve):
        def pair_low(c, w, e=0):
            dve.wait_ge(w13_high, e * (2 * SLOTS) + (w_before + 2 * c + w + 1))
            dve.tensor_tensor(k.w13[:, c % 2, w, 1], raw(c, w), k.w13[:, c % 2, w, 0].bitcast(F32),
                              ALU.subtract).then_inc(w13_split, 1)

        def down_low(c, e=0):
            dve.wait_ge(w2_high, e * SLOTS + (before + c + 1))
            dve.tensor_tensor(k.w2[:, c % 2, 1], slot(k, base + c)[:, 2 * D:3 * D], k.w2[:, c % 2, 0].bitcast(F32),
                              ALU.subtract).then_inc(w2_split, 1)

        def chunk(c, e=0):
            dve.wait_ge(silu_put, e * SLOTS + (before + c + 1))
            dve.tensor_tensor(hidden[:, c % 2, :], silu[:, c % 2, :], k.ps[:, 4 + c % 4, S:2 * S],
                              ALU.mult).then_inc(hidden_put, 1)
            if c + 2 < FC:
                pair_low(c + 2, 0, e)
            dve.wait_ge(hidden_high, e * SLOTS + (before + c + 1))
            dve.tensor_tensor(k.hidsplit[:, c % 2, 1], hidden[:, c % 2, :], k.hidsplit[:, c % 2, 0].bitcast(F32),
                              ALU.subtract).then_inc(hidden_split, 1)
            if c + 2 < FC:
                pair_low(c + 2, 1, e)
            if c + 1 < FC:
                down_low(c + 1, e)

        for kk in range(DK):
            dve.wait_ge(h_high, h_before + kk + 1)
            dve.tensor_tensor(k.hsplit[:, 1, kk, :], k.hT[:, kk, :], k.hsplit[:, 0, kk, :].bitcast(F32),
                              ALU.subtract).then_inc(h_split, 1)
            if kk == 0:
                pair_low(0, 0)
                pair_low(0, 1)
        down_low(0)
        pair_low(1, 0)
        pair_low(1, 1)
        with dve.Fori(0, TURNS) as e:
            for c in range(SLOTS):
                chunk(c, e)
        for c in range(TURNS * SLOTS, FC):
            chunk(c)
        norm.vector(dve)

    return Stage(tensor, scalar, vector)


def conv_s5(k, base, s5_params):
    sem = k.sem
    n_glu, n_out = base + 8, base + 9
    names = ("gate_put", "param_loaded", "exp1", "exp_arg", "mag_put", "bc_ready", "bc_turned", "bc_put", "input_done", "v_parts", "v_put", "w_put", "s_put", "s_put_dve", "y_done",
             "gelu_arg", "z_put", "glu_done", "sig_put", "yb_put")
    q = {s: sem(f"s5_{s}") for s in names}
    B = {"column_done": 22, "copied": 8, "sin_arg": 2, "sin_done": 2}
    q.update({s: sem(s) for s in B})
    mixT = area(k, 0, 2048, c=DK)
    u = area(k, 2048, 1024, q=4)
    z = area(k, 3072, 1024, q=4)
    par = area(k, 4096, 1072)
    re_im = par[:, 0:48].rearrange("p (n i) -> p n i", n=3)
    b_in = par[:, 48:560].rearrange("p (n i c) -> p n i c", n=2, i=16)
    c_in = par[:, 560:1072].rearrange("p (n q s) -> p n q s", n=2, q=4)
    bT = area(k, 5168, 1024, n=2, q=4)
    cT = area(k, 6192, 1024, n=2, q=4)
    small = area(k, 7216, 16 * 16, n=16)
    wide = area(k, 7472, 1024)
    cosT, sinT = work(k, 0, 4096, i=16), work(k, 4096, 4096, i=16)
    m1, m2 = work(k, 8192, 1024), work(k, 9216, 1024)
    prods = [work(k, 8192, 2048, n=4, i=2), work(k, 10240, 2048, n=4, i=2), area(k, 8704, 2048, n=4, i=2)]
    conv_w = fix(k, "conv_w2")

    def phases(j):
        return cosT[:, 2 * j:2 * j + 2, :], sinT[:, 2 * j:2 * j + 2, :]

    ORDER = [c for j in range(4) for c in (j, 8 + j, 4 + j)] + [12, 13, 14, 15]

    def tensor(pe):
        for n in range(base, base + 8):
            pe.wait_ge(k.ready(n), k.use.mark[n])
        for i, c in enumerate(ORDER):
            if i >= 6:
                pe.wait_ge(q["copied"], B["copied"] + i - 5)
            for kk in range(DK):
                last = pe.matmul(k.ps[:, i % 6, 0:S], slot(k, base + kk)[:, c * P:(c + 1) * P], k.hT[:, kk, :],
                                 start=(kk == 0), stop=(kk == DK - 1))
            last.then_inc(q["column_done"], 1)
        pe.drain().then_inc(k.slot_freed, 8)
        for n in range(4):
            pe.wait_ge(q["bc_ready"], n + 1)
            if n:
                pe.wait_ge(q["bc_put"], n)
            for j in range(4):
                last = pe.transpose(k.ps[:, 6, j * P:(j + 1) * P], wide[:, 0:512][:, j * P:(j + 1) * P] if n % 2 == 0
                                    else wide[:, 512:1024][:, j * P:(j + 1) * P], k.ident)
            last.then_inc(q["bc_turned"], 1)
        pe.wait_ge(q["bc_put"], 4)
        pe.wait_ge(q["copied"], B["copied"] + 16)

        def states(j):
            for i in range(2):
                tile = 2 * j + i
                r = 32 * (tile % 4)
                for n in range(2):
                    last = pe.matmul(k.ps[:, 2 * (j % 2) + i, n * S:(n + 1) * S], bT[r:r + 32, n, tile // 4, :],
                                     u[r:r + 32, tile // 4, :], start=True, stop=True)
            last.then_inc(q["input_done"], 1)

        def outputs(j):
            pe.wait_ge(q["s_put"], 2 * (j + 1))
            pe.wait_ge(q["s_put_dve"], 2 * (j + 1))
            for i in range(2):
                tile = 2 * j + i
                r = 32 * (tile % 4)
                for at, (n, part) in enumerate(((0, 1), (0, 3), (1, 0), (1, 2))):
                    last = pe.matmul(k.ps[r:r + 32, 4 + tile // 4, 0:S], cT[:, n, tile // 4, r:r + 32],
                                     prods[j % 3][:, part, i, :], start=(at == 0), stop=(at == 3))
            last.then_inc(q["y_done"], 1)

        states(0)
        states(1)
        for j in range(8):
            if j < 6:
                pe.wait_ge(q["v_parts"], 4 * (j + 1))
                states(j + 2)
            outputs(j)
        pe.wait_ge(k.ready(n_glu), k.use.mark[n_glu])
        pe.wait_ge(q["z_put"], 4)
        for c in range(4):
            for kk in range(4):
                last = pe.matmul(k.ps[:, c, 0:S], slot(k, n_glu)[:, kk * CC + c * P:kk * CC + (c + 1) * P], z[:, kk, :],
                                 start=(kk == 0), stop=(kk == 3))
            last.then_inc(q["glu_done"], 1)
        pe.drain().then_inc(k.slot_freed, 1)
        pe.wait_ge(q["yb_put"], 4)
        out_tensor(pe)
        norm.tensor(pe)

    out_done, out_tensor = mixer_out(k, n_out, mixT, fix(k, "seed1"))
    norm = NormAndTurn(k, out_done, 2 * ST, 1.0)

    def scalar(act):
        act.dma_start(par, s5_params).then_inc(q["param_loaded"], 16)
        act.wait_ge(q["param_loaded"], 16)
        act.activation(re_im[:, 2, :], re_im[:, 2, :], ACT.Exp).then_inc(q["exp1"], 1)
        act.wait_ge(q["exp_arg"], 1)
        act.activation(small[:, 2, :], small[:, 2, :], ACT.Exp).then_inc(q["mag_put"], 1)
        act.wait_ge(q["sin_arg"], B["sin_arg"] + 1)
        act.activation(small[:, 4, :], small[:, 4, :], ACT.Sin).then_inc(q["sin_done"], 1)
        act.activation(small[:, 5, :], small[:, 5, :], ACT.Sin).then_inc(q["sin_done"], 1)
        for i, c in enumerate(ORDER):
            act.wait_ge(q["column_done"], B["column_done"] + i + 1)
            if c >= 12:
                act.activation(u[:, c - 12, :], k.ps[:, i % 6, 0:S], ACT.Copy).then_inc(q["copied"], 1)
            else:
                if i >= 3:
                    act.wait_ge(q["gate_put"], i // 3)
                act.activation(z[:, i % 3, :], k.ps[:, i % 6, 0:S], ACT.Copy).then_inc(q["copied"], 1)
        for n in range(4):
            act.wait_ge(q["bc_turned"], n + 1)
            act.activation((bT if n < 2 else cT)[:, n % 2], k.ps[:, 6, :].rearrange("p (q c) -> p q c", q=4),
                           ACT.Copy).then_inc(q["bc_put"], 1)
        for c in range(4):
            act.wait_ge(q["gelu_arg"], c + 1)
            act.activation(z[:, c, :], z[:, c, :], ACT.Gelu_apprx_tanh).then_inc(q["z_put"], 1)
        for c in range(4):
            act.wait_ge(q["glu_done"], c + 1)
            act.activation(u[:, c, :], k.ps[:, c, 0:S], ACT.Sigmoid, bias=fix(k, "b_glu")[:, c:c + 1]).then_inc(q["sig_put"], 1)
        norm.scalar(act)

    def vector(dve):
        step = k.vector_order.on(dve)

        def sm(i):
            return small[:, i, :]

        lr, li, dt = re_im[:, 0, :], re_im[:, 1, :], re_im[:, 2, :]
        dve.wait_ge(q["param_loaded"], 16)
        step(dve.tensor_scalar(lr, lr, -1e-4, None, ALU.min))
        dve.wait_ge(q["exp1"], 1)
        dve.tensor_tensor(sm(2), lr, dt, ALU.mult).then_inc(q["exp_arg"], 1)
        step(dve.tensor_tensor(sm(3), li, dt, ALU.mult))
        step(range_reduce(step, dve, sm(4), sm(3), sm(5)))
        step(dve.scalar_tensor_tensor(out=sm(5), in0=sm(4), scalar=-1.0, in1=sm(4), op0=ALU.mult, op1=ALU.max))
        dve.tensor_scalar(sm(5), sm(5), -1.0, math.pi / 2, ALU.mult, ALU.add).then_inc(q["sin_arg"], 1)
        step(dve.tensor_tensor(sm(6), lr, lr, ALU.mult))
        step(dve.tensor_tensor(sm(7), li, li, ALU.mult))
        step(dve.tensor_tensor(sm(6), sm(6), sm(7), ALU.add))
        step(dve.reciprocal(sm(6), sm(6)))
        dve.wait_ge(q["mag_put"], 1)
        dve.wait_ge(q["sin_done"], B["sin_done"] + 2)
        step(dve.tensor_tensor(sm(7), sm(2), sm(5), ALU.mult))
        step(dve.tensor_scalar(sm(7), sm(7), 1.0, None, ALU.subtract))
        step(dve.tensor_tensor(sm(8), sm(2), sm(4), ALU.mult))
        step(dve.tensor_tensor(sm(9), sm(7), lr, ALU.mult))
        step(dve.tensor_tensor(sm(10), sm(8), li, ALU.mult))
        step(dve.tensor_tensor(sm(9), sm(9), sm(10), ALU.add))
        step(dve.tensor_tensor(sm(9), sm(9), sm(6), ALU.mult))
        step(dve.tensor_tensor(sm(10), sm(8), lr, ALU.mult))
        step(dve.tensor_tensor(sm(11), sm(7), li, ALU.mult))
        step(dve.tensor_tensor(sm(10), sm(10), sm(11), ALU.subtract))
        step(dve.tensor_tensor(sm(10), sm(10), sm(6), ALU.mult))

        fre, fim = (sm(i).unsqueeze(2).to_broadcast([P, 16, S5C]) for i in (9, 10))
        t1 = wide[:, 0:256].rearrange("p (i c) -> p i c", i=16)
        t2 = wide[:, 256:512].rearrange("p (i c) -> p i c", i=16)
        t3 = z[:, 3, :].rearrange("p (i c) -> p i c", i=16)
        t4 = mixT[:, 7, :].rearrange("p (i c) -> p i c", i=16)
        step(dve.tensor_tensor(t1, b_in[:, 0], fre, ALU.mult))
        step(dve.tensor_tensor(t2, b_in[:, 1], fim, ALU.mult))
        step(dve.tensor_tensor(t3, t1, t2, ALU.subtract))
        step(dve.tensor_tensor(t1, b_in[:, 1], fre, ALU.mult))
        step(dve.tensor_tensor(t2, b_in[:, 0], fim, ALU.mult))
        step(dve.tensor_tensor(t4, t1, t2, ALU.add))
        mb, mc = fix(k, "mask_b"), fix(k, "mask_c")
        for n, src in enumerate((t3, t4)):
            out = wide[:, 512 * n:512 * n + 512].rearrange("p (i g c) -> p i g c", i=16, g=2)
            for g in range(2):
                last = dve.tensor_scalar(out[:, :, g, :], src, mb[:, g:g + 1], None, ALU.mult)
                if g == 0:
                    step(last)
            last.then_inc(q["bc_ready"], 1)

        def c_part(n):
            dve.wait_ge(q["bc_turned"], n + 1)
            out = wide[:, 512 * n:512 * n + 512].rearrange("p (q g s) -> p q g s", q=4, g=2)
            for g in range(2):
                last = dve.tensor_scalar(out[:, :, g, :], c_in[:, n], mc[:, g:g + 1], -1.0 if n else 1.0, ALU.mult, ALU.mult)
                if g == 0:
                    step(last)
            last.then_inc(q["bc_ready"], 1)

        def gate(j):
            dve.wait_ge(q["copied"], B["copied"] + 3 * j + 3)
            h, gc, gb, y = z[:, 0, :], z[:, 1, :], z[:, 2, :], mixT[:, j, :]
            step(dve.tensor_tensor(h, h, gc, ALU.mult))
            step(dve.tensor_scalar(y, h, conv_w[:, 8 + j:9 + j], None, ALU.mult))
            step(dve.scalar_tensor_tensor(out=y[:, 1:S], in0=h[:, 0:S - 1], scalar=conv_w[:, 4 + j:5 + j], in1=y[:, 1:S],
                                          op0=ALU.mult, op1=ALU.add))
            step(dve.scalar_tensor_tensor(out=y[:, 2:S], in0=h[:, 0:S - 2], scalar=conv_w[:, j:j + 1], in1=y[:, 2:S],
                                          op0=ALU.mult, op1=ALU.add))
            dve.tensor_tensor(y, y, gb, ALU.mult).then_inc(q["gate_put"], 1)

        step(dve.memset(cosT[:, :, 0:1], 1.0))
        step(dve.memset(sinT[:, :, 0:1], 0.0))
        step(dve.tensor_copy(sm(12), sm(5)))
        step(dve.tensor_copy(sm(13), sm(4)))
        n = 1
        while n < S:
            pr, pi = (sm(i).unsqueeze(2).to_broadcast([P, 16, n]) for i in (12, 13))
            for h in range(0, 16, 16 if n <= 64 else 8):
                hh = slice(h, h + (16 if n <= 64 else 8))
                size = (16 if n <= 64 else 8) * n
                a1 = m1[:, 0:size].rearrange("p (i t) -> p i t", t=n)
                a2 = m2[:, 0:size].rearrange("p (i t) -> p i t", t=n)
                step(dve.tensor_tensor(a1, cosT[:, hh, 0:n], pr[:, hh], ALU.mult))
                step(dve.tensor_tensor(a2, sinT[:, hh, 0:n], pi[:, hh], ALU.mult))
                step(dve.tensor_tensor(cosT[:, hh, n:2 * n], a1, a2, ALU.subtract))
                step(dve.tensor_tensor(a1, cosT[:, hh, 0:n], pi[:, hh], ALU.mult))
                step(dve.tensor_tensor(a2, sinT[:, hh, 0:n], pr[:, hh], ALU.mult))
                step(dve.tensor_tensor(sinT[:, hh, n:2 * n], a1, a2, ALU.add))
            if n in (16, 64):
                gate((16, 64).index(n))
            n *= 2
            if n < S:
                step(dve.tensor_tensor(sm(14), sm(12), sm(12), ALU.mult))
                step(dve.tensor_tensor(sm(15), sm(13), sm(13), ALU.mult))
                step(dve.scalar_tensor_tensor(out=sm(13), in0=sm(12), scalar=2.0, in1=sm(13), op0=ALU.mult, op1=ALU.mult))
                step(dve.tensor_tensor(sm(12), sm(14), sm(15), ALU.subtract))

        gate(2)
        gate(3)
        c_part(0)
        c_part(1)

        def turn_back(j):
            c, sn = phases(j)
            dve.wait_ge(q["input_done"], j + 1)
            if j >= 3:
                dve.wait_ge(q["y_done"], j - 2)
            bre, bim = (k.ps[:, 2 * (j % 2):2 * (j % 2) + 2, n * S:(n + 1) * S] for n in range(2))
            for n, (x, y) in enumerate(((bre, c), (bim, sn), (bim, c), (bre, sn))):
                dve.tensor_tensor(prods[j % 3][:, n], x, y, ALU.mult).then_inc(q["v_parts"], 1)

        def scan(j):
            c, sn = phases(j)
            part = prods[j % 3]
            for n in range(2):
                dve.wait_ge(q["v_put"], 2 * j + n + 1)
                for i in range(2):
                    tile = 2 * j + i
                    dve.tensor_tensor_scan(part[:, 2 * n, i, :], small[:, 2, tile:tile + 1].to_broadcast([P, S]),
                                           part[:, 2 * n, i, :], 0.0, ALU.mult, ALU.add).then_inc(q["w_put"], 1)
            dve.wait_ge(q["w_put"], 4 * j + 4)
            dve.tensor_tensor(part[:, 1], part[:, 0], c, ALU.mult).then_inc(q["s_put_dve"], 1)
            dve.scalar_tensor_tensor(out=part[:, 3], in0=part[:, 2], scalar=-1.0, in1=sn, op0=ALU.mult,
                                     op1=ALU.mult).then_inc(q["s_put_dve"], 1)

        turn_back(0)
        for j in range(8):
            if j < 7:
                turn_back(j + 1)
            scan(j)
        for c in range(4):
            dve.wait_ge(q["y_done"], 2 * (c + 1))
            dve.scalar_tensor_tensor(out=z[:, c, :], in0=u[:, c, :], scalar=fix(k, "s5_d")[:, c:c + 1],
                                     in1=k.ps[:, 4 + c, 0:S], op0=ALU.mult, op1=ALU.add).then_inc(q["gelu_arg"], 1)
        for c in range(4):
            dve.wait_ge(q["sig_put"], c + 1)
            dve.tensor_tensor(mixT[:, 4 + c, :], z[:, c, :], u[:, c, :], ALU.mult).then_inc(q["yb_put"], 1)
        norm.vector(dve)

    def gpsimd(pool):
        def add(j):
            part = prods[j % 3]
            pool.wait_ge(q["v_parts"], 4 * j + 4)
            pool.tensor_tensor(part[:, 0], part[:, 0], part[:, 1], ALU.add).then_inc(q["v_put"], 1)
            pool.tensor_tensor(part[:, 2], part[:, 2], part[:, 3], ALU.subtract).then_inc(q["v_put"], 1)

        add(0)
        for j in range(8):
            if j < 7:
                add(j + 1)
            c, sn = phases(j)
            part = prods[j % 3]
            for n, phase in enumerate((sn, c)):
                pool.wait_ge(q["s_put_dve"], 2 * j + n + 1)
                pool.tensor_tensor(part[:, 2 * n], part[:, 2 * n], phase, ALU.mult).then_inc(q["s_put"], 1)

    return Stage(tensor, scalar, vector, gpsimd)


def ple(k, u, base, out=None):
    sem = k.sem
    proj_done, gate_done, sig_put, part_put, turned, x_put, stored = (
        sem(f"ple_{s}") for s in ("proj_done", "gate_done", "sig_put", "part_put", "turned", "x_put", "stored"))
    before = 2 * ST * u
    h_high, h_split, w_high, w_split = (sem(f"ffn_{s}") for s in ("h_high", "h_split", "w13_high", "w13_split"))
    h_before, w_before = k.h_splits, k.w_splits
    k.h_splits, k.w_splits = h_before + DK, w_before + DK
    low = k.w_low.rearrange("p c k f -> p c (k f)")
    w_parts = lambda kk: (k.gate_high[kk // 4][:, kk % 4], low[:, 3 * Ring.slot_of(base + kk // 3) + kk % 3])
    raw = lambda kk: slot(k, base + kk // 3)[:, (kk % 3) * D:(kk % 3 + 1) * D]
    sig = area(k, 1024, 2048, n=4)
    n_proj = base + 3
    p_sb = slot(k, n_proj)[:, 2 * D:2 * D + 2 * S].rearrange("p (k s) -> p k s", k=2)

    def tensor(pe):
        pe.wait_ge(k.ready(n_proj), k.use.mark[n_proj])
        for t in range(ST):
            for half in range(2):
                for kk in range(PLE // P):
                    last = pe.matmul(k.ps[:, 4 + 2 * t + half, :], p_sb[:, kk, t * P:(t + 1) * P],
                                     slot(k, n_proj)[:, kk * D + half * 512:kk * D + (half + 1) * 512],
                                     start=(kk == 0), stop=(kk == PLE // P - 1))
                last.then_inc(proj_done, 1)
        for kk in range(DK):
            pe.wait_ge(h_split, h_before + kk + 1)
            pe.wait_ge(w_split, w_before + kk + 1)
            for t in range(ST):
                for half in range(2):
                    for n, (i, j) in enumerate(((0, 0), (0, 1), (1, 0))):
                        last = pe.matmul(k.ps[:, 2 * t + half, :], k.hsplit[:, i, kk, t * P:(t + 1) * P],
                                         w_parts(kk)[j][:, half * 512:(half + 1) * 512],
                                         start=(kk == 0 and n == 0), stop=(kk == DK - 1 and n == 2))
                    if kk == DK - 1:
                        last.then_inc(gate_done, 1)
        for i in range(4):
            t, half = i // 2, i % 2
            pe.wait_ge(sig_put, before + i + 1)
            if out is None:
                pe.wait_ge(part_put, before + i + 1)
            for j in range(4):
                kk = 4 * half + j
                src = sig[:, i, j * P:(j + 1) * P] if out is None else k.hT[:, kk, t * P:(t + 1) * P]
                last = pe.transpose(k.ps[:, i, j * P:(j + 1) * P], src, k.ident)
            last.then_inc(turned, 1)
        pe.drain().then_inc(k.slot_freed, 4)

    def scalar(act):
        for kk in range(DK):
            act.activation(k.hsplit[:, 0, kk, :], k.hT[:, kk, :], ACT.Copy).then_inc(h_high, 1)
            if kk % 3 == 0:
                act.wait_ge(k.ready(base + kk // 3), k.use.mark[base + kk // 3])
            act.activation(w_parts(kk)[0], raw(kk), ACT.Copy).then_inc(w_high, 1)
        for i in range(4):
            act.wait_ge(gate_done, before + i + 1)
            act.activation(sig[:, i, :], k.ps[:, i, :], ACT.Sigmoid).then_inc(sig_put, 1)
        if out is not None:
            for i in range(4):
                t, cols = i // 2, slice((i % 2) * 512, (i % 2 + 1) * 512)
                act.wait_ge(x_put, before + i + 1)
                act.dma_start(out[0, t * P:(t + 1) * P, cols], k.x[:, t, cols]).then_inc(stored, 16)
            act.wait_ge(stored, 16 * 4)

    def vector(dve):
        for kk in range(DK):
            dve.wait_ge(h_high, h_before + kk + 1)
            dve.tensor_tensor(k.hsplit[:, 1, kk, :], k.hT[:, kk, :], k.hsplit[:, 0, kk, :].bitcast(F32),
                              ALU.subtract).then_inc(h_split, 1)
            dve.wait_ge(w_high, w_before + kk + 1)
            dve.tensor_tensor(w_parts(kk)[1], raw(kk), w_parts(kk)[0].bitcast(F32), ALU.subtract).then_inc(w_split, 1)
        for i in range(4):
            dve.wait_ge(sig_put, before + i + 1)
            dve.wait_ge(proj_done, before + i + 1)
            dve.tensor_tensor(sig[:, i, :], sig[:, i, :], k.ps[:, 4 + i, :], ALU.mult).then_inc(part_put, 1)
        for i in range(4):
            t, half = i // 2, i % 2
            dve.wait_ge(turned, before + i + 1)
            if out is None:
                x = k.hT[:, 4 * half:4 * half + 4, t * P:(t + 1) * P]
                dve.tensor_tensor(x, x, k.ps[:, i, :].rearrange("p (k s) -> p k s", k=4), ALU.add).then_inc(x_put, 1)
            else:
                dve.wait_ge(part_put, before + i + 1)
                dve.tensor_tensor(k.x[:, t, half * 512:(half + 1) * 512], sig[:, i, :], k.ps[:, i, :],
                                  ALU.add).then_inc(x_put, 1)

    return Stage(tensor, scalar, vector)


def sparse_attention(k, base, causal, positions):
    sem = k.sem
    n_out = base + C_SLOTS
    names = ("loaded", "rope_done", "turned",
             "turned_act", "turned_dve", "index_done", "relu_put", "relu_used")
    q = {s: sem(f"dsa_{s}") for s in names}
    B = {"column_done": 38, "copied": 24, "sin_arg": 3, "sin_done": 4, "score_done": 2 * HEADS, "score_read": 2 * HEADS, "score_put": HEADS, "exp_done": 4 * HEADS, "p_put": ST * HEADS,
         "p_turned": HEADS, "pT_put": HEADS, "o_done": HEADS, "o_put": HEADS}
    q.update({s: sem(s) for s in B})
    HH = QH + KVH
    WIDE, W = HH * HD, IH * ID
    ROW = WIDE + W + ID
    NPR = ST * ROW
    pr = area(k, 0, NPR, t=ST)
    qT = area(k, NPR, QH * S, h=QH)
    kT = area(k, NPR + 2048, KVH * S, h=KVH)
    qiT = area(k, NPR + 2560, 4 * S, h=4)
    kiT = area(k, NPR + 3584, S)
    v = area(k, NPR + 3840, ST * KVH * HD, t=ST)
    wi = area(k, NPR + 4352, ST * IH, t=ST)
    ki2 = area(k, NPR + 4368, ST * 2 * ID, t=ST)
    mixT = area(k, NPR + 4624, DK * S, k=DK)
    assert R0 + NPR + 4624 + DK * S <= ARENA and NPR + 4624 == C_HT_LOW
    out_done, out_tensor = mixer_out(k, n_out, mixT, fix(k, "seed1"))
    norm = NormAndTurn(k, out_done, 4 * ST, 1.0)
    score = area(k, 0, 512, t=ST)
    left = area(k, 512, 512, t=ST)
    relu = area(k, 1024, 1024, n=4)
    keep = area(k, 2048, 512, t=ST)
    s = k.arena[:, X0:X0 + 4 * ST * S].rearrange("p (b t s) -> p b t s", b=4, t=ST)
    pT = area(k, 1024, 1024, b=2, c=ST)

    causal_sb = work(k, 0, 512, t=ST)
    pos_i = work(k, 512, ST).bitcast(I32)
    pos = work(k, 514, ST)
    ang, arg, rev = work(k, 520, 48, t=ST), work(k, 568, 96, n=2, t=ST), work(k, 664, 48, t=ST)
    trig = work(k, 712, 96, n=2, t=ST)
    tmp = [work(k, 1024 + 320 * i, 320) for i in range(4)]
    m = misc(k, 0, 40)
    scale = HD ** -0.5
    NOT = -1e30
    TAKEN = -2e30
    h_high, h_split, w_high, w_split = (sem(f"ffn_{s}") for s in ("h_high", "h_split", "w13_high", "w13_split"))
    h_before, w_before = k.h_splits, k.w_splits
    k.h_splits, k.w_splits = h_before + DK, w_before + 2 * C_SLOTS
    WIDTH = [C_TILE] * (C_SLOTS - 1) + [S]
    FIRST = [C_TILE * n for n in range(C_SLOTS - 1)] + [C_IN - S]
    low = k.w_low.rearrange("p c k f -> p (c k f)")

    def by_chunk(v, n):
        return v[:, 0:DK * WIDTH[n]].rearrange("p (k f) -> p k f", k=DK)

    def w_part(n, part):
        at = Ring.slot_of(base + n) * SLOT
        return by_chunk(low[:, at:at + SLOT] if part else k.c_high[:, n % 2], n)

    h_parts = (k.c_hT_high, k.c_hT_low)
    BLOCKS = ([(qT[:, h, :], h * HD) for h in range(QH)] + [(kT[:, h, :], (QH + h) * HD) for h in range(KVH)]
              + [(qiT[:, h, :], WIDE + h * P) for h in range(4)] + [(kiT, None)])

    def tensor(pe):
        for n in range(C_SLOTS):
            if n >= 4:
                pe.wait_ge(q["copied"], B["copied"] + 2 * (n - 3))
            for kk in range(DK):
                if n == 0:
                    pe.wait_ge(h_split, h_before + kk + 1)
                if kk % 4 == 0:
                    pe.wait_ge(w_split, w_before + 2 * n + kk // 4 + 1)
                for t in range(ST):
                    for at, (i, j) in enumerate(((0, 0), (0, 1), (1, 0))):
                        last = pe.matmul(k.ps[:, (2 * n + t) % 8, 0:WIDTH[n]], h_parts[i][:, kk, t * P:(t + 1) * P],
                                         w_part(n, j)[:, kk, :], start=(kk == 0 and at == 0), stop=(kk == DK - 1 and at == 2))
                    if kk == DK - 1:
                        last.then_inc(q["column_done"], 1)
        pe.drain().then_inc(k.slot_freed, C_SLOTS)
        pe.wait_ge(q["rope_done"], 1)
        pe.wait_ge(q["copied"], B["copied"] + ST * C_SLOTS)
        for i, (_, at) in enumerate(BLOCKS):
            for t in range(ST):
                src = ki2[:, t, :] if at is None else pr[:, t, at:at + P]
                last = pe.transpose(k.ps[:, i // 2, (i % 2) * S + t * P:(i % 2) * S + (t + 1) * P], src, k.ident)
            if i % 2 or i == len(BLOCKS) - 1:
                last.then_inc(q["turned"], 1)
        pe.wait_ge(q["turned_act"], 4)
        pe.wait_ge(q["turned_dve"], 4)
        for i in range(ST * IH):
            t, h = i // IH, i % IH
            if i >= 8:
                pe.wait_ge(q["relu_put"], i - 7)
            r = ID * (h % 2)
            pe.matmul(k.ps[:, i % 8, 0:P * (t + 1)], qiT[r:r + ID, h // 2, t * P:(t + 1) * P], kiT[r:r + ID, 0:P * (t + 1)],
                      start=True, stop=True).then_inc(q["index_done"], 1)
        pe.wait_ge(q["relu_put"], ST * IH)
        def scores(h):
            if h >= 2:
                pe.wait_ge(q["score_read"], B["score_read"] + h - 1)
            for t in range(ST):
                last = pe.matmul(k.ps[:, h % 2, t * S:(t + 1) * S], qT[:, h, t * P:(t + 1) * P],
                                 kT[:, h // (QH // KVH), :], start=True, stop=True)
            last.then_inc(q["score_done"], 1)

        def turn(h):
            pe.wait_ge(q["p_put"], B["p_put"] + ST * (h + 1))
            if h >= 2:
                pe.wait_ge(q["pT_put"], B["pT_put"] + h - 1)
            for t in range(ST):
                for kc in range(ST):
                    last = pe.transpose(k.ps[:, 2 + h % 2, kc * S + t * P:kc * S + (t + 1) * P],
                                        s[:, h % 4, t, kc * P:(kc + 1) * P], k.ident)
            last.then_inc(q["p_turned"], 1)

        def outputs(h):
            pe.wait_ge(q["pT_put"], B["pT_put"] + h + 1)
            if h >= 2:
                pe.wait_ge(q["o_put"], B["o_put"] + h - 1)
            kv = h // (QH // KVH)
            for kc in range(ST):
                last = pe.matmul(k.ps[:, 4 + h % 2, 0:S], v[:, kc, kv * HD:(kv + 1) * HD], pT[:, h % 2, kc, :],
                                 start=(kc == 0), stop=(kc == ST - 1))
            last.then_inc(q["o_done"], 1)

        scores(0)
        skewed(QH, lambda h: scores(h + 1) if h + 1 < QH else None, turn, outputs)
        pe.wait_ge(q["o_put"], B["o_put"] + QH)
        out_tensor(pe)
        norm.tensor(pe)

    def scalar(act):
        act.dma_start(causal_sb, causal).then_inc(q["loaded"], 16)
        act.dma_start(pos_i, positions).then_inc(q["loaded"], 16)
        def high(n):
            act.wait_ge(k.ready(base + n), k.use.mark[base + n])
            for half in range(2):
                rows = slice(4 * half, 4 * half + 4)
                act.activation(w_part(n, 0)[:, rows], by_chunk(slot(k, base + n), n)[:, rows], ACT.Copy).then_inc(w_high, 1)

        for kk in range(DK):
            act.activation(k.c_hT_high[:, kk, :], k.hT[:, kk, :], ACT.Copy).then_inc(h_high, 1)
            if kk == 0:
                high(0)
        high(1)
        for n in range(2):
            act.wait_ge(q["sin_arg"], B["sin_arg"] + n + 1)
            act.activation(trig[:, n], arg[:, n], ACT.Sin).then_inc(q["sin_done"], 1)
        PLACES = ((0, 1280, pr, 0, 1.0), (1280, 1536, v, 0, 1.0), (1536, 1536 + W + ID, pr, WIDE, 1.0),
                  (1536 + W + ID, C_IN, wi, 0, IH ** -0.5 * ID ** -0.5))
        for i in range(ST * C_SLOTS):
            n, t = i // 2, i % 2
            act.wait_ge(q["column_done"], B["column_done"] + i + 1)
            for c0, c1, to, at, factor in PLACES:
                a0, a1 = max(c0, C_TILE * n), min(c1, C_TILE * (n + 1))
                if a0 < a1:
                    last = act.activation(to[:, t, at + a0 - c0:at + a1 - c0], k.ps[:, i % 8, a0 - FIRST[n]:a1 - FIRST[n]],
                                          ACT.Copy, scale=factor)
            last.then_inc(q["copied"], 1)
            if t == 1 and n + 2 < C_SLOTS:
                high(n + 2)
        for b in (1, 3, 5, 7):
            act.wait_ge(q["turned"], b + 1)
            for j in range(2):
                if 2 * b + j < len(BLOCKS):
                    last = act.activation(BLOCKS[2 * b + j][0], k.ps[:, b, j * S:(j + 1) * S], ACT.Copy)
            last.then_inc(q["turned_act"], 1)
        for i in range(ST * IH):
            t = i // IH
            act.wait_ge(q["index_done"], i + 1)
            if i >= 4:
                act.wait_ge(q["relu_used"], i - 3)
            act.activation(relu[:, i % 4, 0:P * (t + 1)], k.ps[:, i % 8, 0:P * (t + 1)], ACT.Relu).then_inc(q["relu_put"], 1)
        def exponentials(h):
            act.wait_ge(q["score_put"], B["score_put"] + h + 1)
            for t in range(ST):
                act.activation(s[:, h % 4, t, :], s[:, h % 4, t, :], ACT.Exp, bias=m[:, 2 * (h % 2) + t:2 * (h % 2) + t + 1],
                               accum_out=m[:, 4 + 2 * (h % 2) + t:5 + 2 * (h % 2) + t]).then_inc(q["exp_done"], 1)

        def output(h):
            act.wait_ge(q["o_done"], B["o_done"] + h + 1)
            act.activation(mixT[:, h, :], k.ps[:, 4 + h % 2, 0:S], ACT.Copy).then_inc(q["o_put"], 1)

        skewed(QH, exponentials, None, output)
        norm.scalar(act)

    def vector(dve):
        step = k.vector_order.on(dve)
        def lows(n):
            for half in range(2):
                rows = slice(4 * half, 4 * half + 4)
                dve.wait_ge(w_high, w_before + 2 * n + half + 1)
                dve.tensor_tensor(w_part(n, 1)[:, rows], by_chunk(slot(k, base + n), n)[:, rows],
                                  w_part(n, 0)[:, rows].bitcast(F32), ALU.subtract).then_inc(w_split, 1)

        for kk in range(DK):
            dve.wait_ge(h_high, h_before + kk + 1)
            dve.tensor_tensor(k.c_hT_low[:, kk, :], k.hT[:, kk, :], k.c_hT_high[:, kk, :].bitcast(F32),
                              ALU.subtract).then_inc(h_split, 1)
            if kk == 0:
                lows(0)
        lows(1)
        dve.wait_ge(q["loaded"], 32)
        step(dve.tensor_copy(pos, pos_i))
        for t in range(ST):
            step(dve.tensor_scalar(ang[:, t, :], fix(k, "inv_freq"), pos[:, t:t + 1], None, ALU.mult))
        step(range_reduce(step, dve, arg[:, 0], ang, rev))
        step(dve.scalar_tensor_tensor(out=arg[:, 1], in0=arg[:, 0], scalar=-1.0, in1=arg[:, 0], op0=ALU.mult, op1=ALU.max))
        dve.tensor_scalar(arg[:, 1], arg[:, 1], -1.0, math.pi / 2, ALU.mult, ALU.add).then_inc(q["sin_arg"], 2)
        dve.wait_ge(q["sin_done"], B["sin_done"] + 2)
        for n in range(2, C_SLOTS):
            lows(n)
        dve.wait_ge(q["copied"], B["copied"] + ST * C_SLOTS)
        for c0, heads, width, a0, half in ((0, HH, HD, 0, 16), (WIDE, IH + 1, ID, 16, 8)):
            part = pr[:, :, c0:c0 + heads * width].rearrange("p t (h d) -> p t h d", d=width)
            t1, t2 = part[:, :, :, 0:half], part[:, :, :, half:2 * half]
            sin, cos = (trig[:, n, :, a0:a0 + half].unsqueeze(2).to_broadcast([P, ST, heads, half]) for n in range(2))
            p = [x[:, 0:ST * heads * half].rearrange("p (t h d) -> p t h d", t=ST, d=half) for x in tmp]
            step(dve.tensor_tensor(p[0], t1, cos, ALU.mult))
            step(dve.tensor_tensor(p[1], t2, sin, ALU.mult))
            step(dve.tensor_tensor(p[2], t2, cos, ALU.mult))
            step(dve.tensor_tensor(p[3], t1, sin, ALU.mult))
            step(dve.tensor_tensor(t1, p[0], p[1], ALU.subtract))
            step(dve.tensor_tensor(t2, p[2], p[3], ALU.add))
        step(dve.tensor_copy(ki2[:, :, 0:ID], pr[:, :, WIDE + W:ROW]))
        dve.tensor_copy(ki2[:, :, ID:2 * ID], pr[:, :, WIDE + W:ROW]).then_inc(q["rope_done"], 1)
        for b in (0, 2, 4, 6):
            dve.wait_ge(q["turned"], b + 1)
            for j in range(2):
                last = dve.tensor_copy(BLOCKS[2 * b + j][0], k.ps[:, b, j * S:(j + 1) * S])
            last.then_inc(q["turned_dve"], 1)
        for i in range(ST * IH):
            t, h = i // IH, i % IH
            w = slice(0, P * (t + 1))
            dve.wait_ge(q["relu_put"], i + 1)
            if h:
                dve.wait_ge(q["relu_used"], i)
            dve.scalar_tensor_tensor(out=score[:, t, w], in0=relu[:, i % 4, w], scalar=wi[:, t, h:h + 1],
                                     in1=causal_sb[:, t, w] if h == 0 else score[:, t, w], op0=ALU.mult,
                                     op1=ALU.add).then_inc(q["relu_used"], 1)
        dve.wait_ge(q["relu_used"], ST * IH)
        for t in range(ST):
            w = slice(0, P * (t + 1))
            for r in range(TOPK // 8):
                src = left[:, t, w] if r else score[:, t, w]
                step(dve.max(m[:, 8:16], src))
                step(dve.match_replace(out=left[:, t, w], in_to_replace=m[:, 8:16], in_values=src, imm_value=TAKEN))
            step(dve.tensor_scalar(left[:, t, w], left[:, t, w], TAKEN, -NOT, ALU.is_equal, ALU.mult))
            step(dve.scalar_tensor_tensor(out=keep[:, t, w], in0=left[:, t, w], scalar=NOT, in1=causal_sb[:, t, w],
                                          op0=ALU.add, op1=ALU.add))
        step(dve.tensor_copy(keep[:, 0, P:S], causal_sb[:, 0, P:S]))

        def weights(h):
            b = h % 2
            neg = m[:, 2 * b:2 * b + 2]
            dve.wait_ge(q["score_done"], B["score_done"] + h + 1)
            dve.scalar_tensor_tensor(out=s[:, h % 4], in0=k.ps[:, b, :].rearrange("p (t s) -> p t s", t=ST), scalar=scale,
                                     in1=keep, op0=ALU.mult, op1=ALU.add).then_inc(q["score_read"], 1)
            dve.wait_ge(q["score_read"], B["score_read"] + h + 1)
            step(dve.tensor_reduce(neg, s[:, h % 4], AX, ALU.max))
            dve.tensor_scalar(neg, neg, -1.0, None, ALU.mult).then_inc(q["score_put"], 1)

        def normalise(h):
            b = h % 2
            total = m[:, 4 + 2 * b:6 + 2 * b]
            dve.wait_ge(q["exp_done"], B["exp_done"] + 2 * h + 2)
            step(dve.reciprocal(total, total))
            for t in range(ST):
                dve.tensor_scalar(s[:, h % 4, t, :], s[:, h % 4, t, :], total[:, t:t + 1], None, ALU.mult).then_inc(q["p_put"], 1)

        def turned(h):
            b = h % 2
            dve.wait_ge(q["p_turned"], B["p_turned"] + h + 1)
            dve.tensor_copy(pT[:, b], k.ps[:, 2 + b, :].rearrange("p (c s) -> p c s", c=ST)).then_inc(q["pT_put"], 1)

        skewed(QH, weights, normalise, turned)
        norm.vector(dve)

    return Stage(tensor, scalar, vector)


def second(k, t, base, out):
    loads, stages = [], []

    def add(new, stage):
        nonlocal loads
        loads += new
        stages.append(stage)

    def add_ffn(i, j, n):
        add(ffn_weights(k, n, t["ffn_w"][2 * i + j]), ffn(k, 2 * i + j, n))
        return n + FC

    def add_ple(i, n, out=None):
        new = weights_in_slots(k, n, t["ple_w_gate_2"][i], 3, D)
        k.use.landing(n + 3, 2)
        new += [(n + 3, [(slot(k, n + 3, 2 * D), t["ple_proj"][i]), (slot(k, n + 3)[:, 2 * D:2 * D + 2 * S], t["pT"][i])])]
        add(new, ple(k, i, n, out))
        return n + 4

    n = add_ffn(0, 0, base)
    new = weights_in_slots(k, n, t["ab_w_in_2"][0], 1, 3 * CC + S5G * S5C)
    new += weights_in_slots(k, n + 8, t["s5_w_glu_2"][0], 6, CC)
    new += weights_in_slots(k, n + 9, t["ab_w_out_2"][0], 3, D)
    add(new, conv_s5(k, n, t["s5_params"]))
    n = add_ffn(0, 1, n + 12)
    n = add_ple(0, n)
    n = add_ffn(1, 0, n)
    new = []
    for i in range(C_SLOTS):
        k.use.landing(n + i)
        new.append((n + i, [(slot(k, n + i), t["c_w_tiles"][i]) if i < C_SLOTS - 1
                            else (slot(k, n + i, DK * S), t["c_w_rest"])]))
    new += weights_in_slots(k, n + C_SLOTS, t["c_w_out_2"][0], 3, D)
    add(new, sparse_attention(k, n, t["causal"], t["positions"]))
    n = add_ffn(1, 1, n + C_SLOTS + 3)
    add_ple(1, n, out)
    return loads, stages


def laid_out_second(a):
    def by_state(v):
        v = np.asarray(v)
        v = v.reshape(S5G // 2, 2 * S5N, -1)
        return v.transpose(1, 0, 2).reshape(P, -1)

    log_dt = np.repeat(np.asarray(a["s5_log_dt_2"][0])[:, None], S5N, 1)
    c_parts = [np.asarray(a[n][0]).reshape(4, P, S5N).transpose(1, 0, 2).reshape(P, -1) for n in ("s5_c_re_2", "s5_c_im_2")]
    params = [by_state(a["s5_lam_re_2"][0]), by_state(a["s5_lam_im_2"][0]), by_state(log_dt),
              by_state(a["s5_b_re_2"][0]), by_state(a["s5_b_im_2"][0])] + c_parts
    w1, w3 = (np.asarray(a[n]).reshape(4, DK, P, FC, P).transpose(0, 3, 2, 1, 4).reshape(4, FC, P, D)
              for n in ("ffn_w1_2", "ffn_w3_2"))
    w2 = np.asarray(a["ffn_w2_2"]).reshape(4, FC, P, D)
    t, s = np.arange(S)[:, None], np.arange(S)[None, :]
    causal = np.where(s <= t, 0.0, -1e30).astype(np.float32)
    c_w = np.asarray(a["c_w_in_2"][0]).reshape(DK, P, C_IN)
    tiles = C_SLOTS - 1
    return {
        "c_w_tiles": np.ascontiguousarray(c_w[:, :, 0:tiles * C_TILE].reshape(DK, P, tiles, C_TILE).transpose(2, 1, 0, 3)
                                          .reshape(tiles, P, SLOT)),
        "c_w_rest": np.ascontiguousarray(c_w[:, :, C_IN - S:].transpose(1, 0, 2).reshape(P, DK * S)),
        "ffn_w": np.concatenate([w1, w3, w2], 3),
        "s5_params": np.ascontiguousarray(np.concatenate(params, 1)),
        "pT": np.ascontiguousarray(np.asarray(a["p_2"])[:, 0].transpose(0, 2, 1).reshape(2, PLE // P, P, S).transpose(0, 2, 1, 3)
                                   .reshape(2, P, 2 * S)),
        "ple_proj": np.ascontiguousarray(np.asarray(a["ple_w_proj_2"]).reshape(2, PLE // P, P, D).transpose(0, 2, 1, 3)
                                         .reshape(2, P, 2 * D)),
        "positions": np.ascontiguousarray(np.asarray(a["positions_2"]).reshape(ST, P).T),
        "causal": np.ascontiguousarray(causal.reshape(ST, P, S).transpose(1, 0, 2)),
    }


def weights_in_slots(k, first, w, rows_per_slot, cols, r0=0):
    chunks = w.shape[0] // P
    out = []
    for i in range(-(-chunks // rows_per_slot)):
        c0, c1 = i * rows_per_slot, min((i + 1) * rows_per_slot, chunks)
        n = first + i
        k.use.landing(n)
        dst = slot(k, n, (c1 - c0) * cols).rearrange("p (c f) -> p c f", c=c1 - c0)
        out.append((n, [(dst, w[c0 * P:c1 * P, :].rearrange("(c p) f -> p c f", p=P))]))
    return out


def program(nc, t, out):
    with ExitStack() as stack:
        k = setup(nc, stack)
        k.w_router = t["w_router"]
        n_out = DK
        n_experts = n_out + 3
        loads = []
        for n in range(DK):
            k.use.landing(n)
            loads.append((n, [(slot(k, n), t["w_in_tiles"][n])]))
        first_loads, first = filters(k, t["x"], t["fixed"], t["dft"], t["filt_tables"], t["filt_w1"], t["filt_w2"],
                                     t["filt_w3"], t["zT"])
        loads += weights_in_slots(k, n_out, t["w_out"][0], 3, D)
        stages = [first, projections(k), hyena(k), attention(k, t["dist"], t["lam_rows"]), routing(k, n_out)]
        expert_loads, expert_stage = experts(k, n_experts, t["w_gate"], t["w_up"], t["w_down"],
                                             t["final_norm_g"], stages_before=4)
        stages += [expert_stage, experts_combine(k)]
        more_loads, more_stages = second(k, t, n_experts + 3 * DK * NE, out["out"])
        stages += more_stages

        with nc.Block() as block:
            @block.sync
            def _(sync):
                first_loads(sync)
                sync.wait_ge(k.sem("tables_loaded"), 16 * 6)
                load_slots(k, sync, loads)
                expert_loads(sync)
                load_slots(k, sync, more_loads)

            @block.tensor
            def _(pe):
                for i, stage in enumerate(stages):
                    stage.tensor(pe)
                    meet(k, "tensor", pe, i)

            @block.scalar
            def _(act):
                for i, stage in enumerate(stages):
                    stage.scalar(act)
                    meet(k, "scalar", act, i)

            @block.vector
            def _(dve):
                for i, stage in enumerate(stages):
                    stage.vector(dve)
                    meet(k, "vector", dve, i)

            @block.gpsimd
            def _(pool):
                for i, stage in enumerate(stages):
                    stage.gpsimd(pool)
                    meet(k, "gpsimd", pool, i)


def constants():
    f32 = np.float32
    s = np.arange(S, dtype=np.float64)[:, None]
    f = np.arange(S, dtype=np.float64)[None, :]
    ang = 2 * np.pi * ((s * f) % NF) / NF
    nyq = np.where(np.arange(S) % 2 == 0, 1.0, -1.0)
    fwd = np.concatenate([np.cos(ang), -np.sin(ang)], 1)
    fwd[:, S] = nyq
    inv = np.concatenate([2 * np.cos(ang.T), -2 * np.sin(ang.T)], 0) / NF
    inv[0] = 1.0 / NF
    inv[S] = nyq / NF

    def tiles(a):
        return a.reshape(-1, P, a.shape[1]).transpose(1, 0, 2).reshape(P, -1).astype(f32)

    t = np.linspace(0.0, 1.0, S, dtype=f32)[:, None]
    w = (f32(2.0 * math.pi) * np.arange(S, dtype=f32)[:, None] / f32(S)).astype(f32)
    bands = np.linspace(1e-4, (EMB - 1) // 2 - 1, (EMB - 1) // 2, dtype=f32)[None, :]
    z = np.concatenate([t, np.cos(bands * w), -np.sin(bands * w)], axis=-1).astype(f32)
    deltas = np.abs(np.linspace(math.log(1e-2) / 1.5, math.log(1e-2) / 0.3, HY, dtype=f32))
    decay = np.exp(-t * deltas).astype(f32)
    dist = np.abs(np.arange(S)[:, None] - np.arange(S)[None, :]).astype(f32)
    eye = np.eye(P, dtype=f32)
    ones0 = np.ones((P, P), f32)
    ones0[0] = 0.0
    inv_attn = (500000.0 ** (-np.arange(0, 32, 2, dtype=f32) / f32(32))).astype(f32)
    inv_idx = (500000.0 ** (-np.arange(0, 16, 2, dtype=f32) / f32(16))).astype(f32)
    return {
        "dft": np.concatenate([tiles(fwd), tiles(inv)], 1),
        "filt_tables": tiles(decay),
        "zT": np.ascontiguousarray(z.T), "dist": tiles(dist).reshape(P, ST, S),
        "ident": eye, "ones": np.ones((P, P), f32), "ones0": ones0,
        "group_mean": np.kron(np.eye(2, dtype=f32), np.full((64, 64), 1 / 64, f32)),
        "mask_b": np.kron(np.eye(2, dtype=f32), np.ones((S5N, 1), f32)),
        "mask_c": np.tile(np.kron(np.eye(2, dtype=f32), np.ones((S5C, 1), f32)), (4, 1)),
        "seed1": eye * f32(ALPHA), "seed2": eye * f32(2 * ALPHA),
        "slot_no": np.tile(np.arange(CAP, dtype=f32), (P, 1)),
        "inv_freq": np.tile(np.concatenate([inv_attn, inv_idx]), (P, 1)),
    }


def laid_out(a):
    c = constants()

    def by_channel(v):
        v = np.asarray(v)
        return np.ascontiguousarray(v.reshape(-1, P).T)

    filt = np.zeros((P, 3), np.float32)
    for i, n in enumerate(("filt_b1", "filt_b2", "filt_freq")):
        filt[:HID, i] = a[n][0]
    parts = dict(c)
    parts.update(attn_g=by_channel(a["attn_norm_g"]), conv_w=by_channel(a["conv_w"]), conv_b=by_channel(a["conv_b"]),
                 skip=by_channel(a["hyena_skip"]), hy_g=by_channel(a["hyena_norm_g"]), subln_g=by_channel(a["subln_g"]),
                 ffn_g=by_channel(a["ffn_norm_g"]), filt=filt, conv_w2=by_channel(a["conv_w_2"]),
                 s5_d=by_channel(a["s5_d_2"]), b_glu=by_channel(a["s5_b_glu_2"]),
                 ln_g=by_channel(a["ln_g_2"]), ln_b=by_channel(a["ln_b_2"]))
    out = {n: np.ascontiguousarray(a[n]) for n in WHOLE}
    out["fixed"] = np.concatenate([parts[n] for n, (at, w) in FIX.items() if n != "misc"], 1)
    out["w_in_tiles"] = np.ascontiguousarray(np.asarray(a["w_in"][0]).reshape(DK, P, DK, 3, P).transpose(2, 1, 3, 0, 4)
                                             .reshape(DK, P, 3 * D))
    for n in ("dft", "filt_tables", "zT", "dist"):
        out[n] = c[n]
    lam = np.concatenate([a[n][0] for n in ("lambda_q1", "lambda_k1", "lambda_q2", "lambda_k2")])
    out["lam_rows"] = np.ascontiguousarray(np.broadcast_to(lam, (P, lam.size)))
    out.update(laid_out_second(a))
    return out


WHOLE = ["x", "filt_w1", "filt_w2", "filt_w3", "w_out", "w_router", "w_gate", "w_up", "w_down", "final_norm_g",
         "ple_w_gate_2", "ab_w_in_2",
         "ab_w_out_2", "s5_w_glu_2", "c_w_out_2"]


def kernel(**inputs):
    import concourse.bacc as bacc
    from concourse.bass_utils import run_bass_kernel_spmd

    arrays = laid_out({n: np.asarray(v) for n, v in inputs.items()})
    nc = bacc.Bacc("TRN2", target_bir_lowering=False, num_devices=1)
    tensors = {n: nc.dram_tensor(f"in_{n}", v.shape, mybir.dt.from_np(v.dtype), kind="ExternalInput").ap()
               for n, v in arrays.items()}
    out = nc.dram_tensor("result", (1, S, D), F32, kind="ExternalOutput").ap()
    program(nc, tensors, {"out": out})
    done = run_bass_kernel_spmd(nc, [{f"in_{n}": v for n, v in arrays.items()}], core_ids=[0])
    return done.results[0]["result"]
```
